# Optimizing a Trainium2 kernel written in Bass

```python
import jax, jax.numpy as jnp
from jax import lax
import numpy as np

D_MODEL = 1024
BATCH = 1
SEQ = 1024
DEPTH = 1

CHUNK = 64
HG_HEADS = 4
HG_DK = 128
HG_DV = 128
HG_QK_W = HG_HEADS * HG_DK
HG_V_W = HG_HEADS * HG_DV
ATT_HEADS = 8
ATT_KV_HEADS = 2
ATT_GROUP = ATT_HEADS // ATT_KV_HEADS
ATT_DH = 64
ATT_Q_W = ATT_HEADS * ATT_DH
ATT_KV_W = ATT_KV_HEADS * ATT_DH
WINDOW = 128
WINDOW_CHUNKS = WINDOW // CHUNK
MIX_W = HG_V_W + ATT_Q_W
IN_WIDTHS = (HG_QK_W, HG_QK_W, HG_V_W, HG_V_W, ATT_Q_W, ATT_KV_W, ATT_KV_W)
IN_DIM = sum(IN_WIDTHS)
IN_SPLITS = tuple(sum(IN_WIDTHS[:i + 1]) for i in range(len(IN_WIDTHS) - 1))
N_BUCKETS = 32
MAX_DISTANCE = 128
N_GROUPS = 4
EXPERTS_PER_GROUP = 8
N_EXPERTS = N_GROUPS * EXPERTS_PER_GROUP
TOP_K = 2
D_EXPERT = 512
EXPERT_BLOCK = 256
ALPHA = (2.0 * DEPTH) ** 0.25
BETA = (8.0 * DEPTH) ** -0.25
EPS = 1e-5

kernel_name = "hybrid_hgrn2_swa_sink_hmoe_block"

def _layer_norm(x, gain=None, bias=None):
    xf = x.astype(jnp.float32)
    mu = jnp.mean(xf, axis=-1, keepdims=True)
    var = jnp.mean(jnp.square(xf - mu), axis=-1, keepdims=True)
    y = (xf - mu) * lax.rsqrt(var + EPS)
    if gain is not None:
        y = y * gain.astype(jnp.float32) + bias.astype(jnp.float32)
    return y.astype(x.dtype)

def _t5_buckets():
    qpos = np.arange(CHUNK)[:, None]
    kpos = np.arange(WINDOW_CHUNKS * CHUNK)[None, :] - (WINDOW_CHUNKS - 1) * CHUNK
    n = qpos - kpos
    half = N_BUCKETS // 2
    ret = (n < 0).astype(np.int32) * half
    n = np.abs(n)
    max_exact = half // 2
    large = max_exact + (np.log(np.maximum(n, 1) / max_exact) / np.log(MAX_DISTANCE / max_exact)
                         * (half - max_exact)).astype(np.int32)
    large = np.minimum(large, half - 1)
    return (ret + np.where(n < max_exact, n, large)).astype(np.int32)

def _hgrn2(hq, hf, hi, hgate, lb, norm_g):
    B, S, _ = hq.shape
    n_c = S // CHUNK
    f = lb + (1.0 - lb) * jax.nn.sigmoid(hf.astype(jnp.float32))
    logf = jnp.log(f)
    k = 1.0 - f
    q = jax.nn.silu(hq.astype(jnp.float32))
    v = hi.astype(jnp.float32)

    def to_chunks(t, d):
        return t.reshape(B, n_c, CHUNK, HG_HEADS, d).transpose(1, 0, 3, 2, 4)

    xs = (to_chunks(q, HG_DK), to_chunks(k, HG_DK), to_chunks(v, HG_DV), to_chunks(logf, HG_DK))
    tril = jnp.tril(jnp.ones((CHUNK, CHUNK), dtype=bool))

    def step(state, inp):
        qc, kc, vc, lc = inp
        bcum = jnp.cumsum(lc, axis=2)
        diff = bcum[:, :, :, None, :] - bcum[:, :, None, :, :]
        decay = jnp.exp(jnp.where(tril[:, :, None], diff, -jnp.inf))
        scores = jnp.einsum('bhtd,bhsd,bhtsd->bhts', qc, kc, decay)
        o = (jnp.einsum('bhts,bhsv->bhtv', scores, vc)
             + jnp.einsum('bhtd,bhdv->bhtv', qc * jnp.exp(bcum), state))
        blast = bcum[:, :, -1:, :]
        state = (jnp.exp(blast[:, :, 0, :])[..., None] * state
                 + jnp.einsum('bhsd,bhsv->bhdv', kc * jnp.exp(blast - bcum), vc))
        return state, o

    s0 = jnp.zeros((B, HG_HEADS, HG_DK, HG_DV), jnp.float32)
    _, o = lax.scan(step, s0, xs)
    o = o.transpose(1, 0, 3, 2, 4).reshape(B, S, HG_HEADS, HG_DV)
    o = o * lax.rsqrt(jnp.mean(jnp.square(o), axis=-1, keepdims=True) + EPS) * norm_g.astype(jnp.float32)
    o = o.reshape(B, S, HG_V_W) * jax.nn.silu(hgate.astype(jnp.float32))
    return o.astype(hq.dtype)

def _swa_sink_attention(q, k, v, sinks, rel_bias):
    B, S = q.shape[0], q.shape[1]
    n_c = S // CHUNK
    band = WINDOW_CHUNKS * CHUNK
    qb = q.reshape(B, n_c, CHUNK, ATT_KV_HEADS, ATT_GROUP, ATT_DH)
    pad = ((0, 0), (WINDOW_CHUNKS - 1, 0), (0, 0), (0, 0), (0, 0))
    kc = jnp.pad(k.reshape(B, n_c, CHUNK, ATT_KV_HEADS, ATT_DH), pad)
    vc = jnp.pad(v.reshape(B, n_c, CHUNK, ATT_KV_HEADS, ATT_DH), pad)
    kb = jnp.concatenate([kc[:, j:j + n_c] for j in range(WINDOW_CHUNKS)], axis=2)
    vb = jnp.concatenate([vc[:, j:j + n_c] for j in range(WINDOW_CHUNKS)], axis=2)
    s = jnp.einsum('bcqhgd,bckhd->bhgcqk', qb, kb).astype(jnp.float32) * (ATT_DH ** -0.5)
    bias = rel_bias.astype(jnp.float32)[jnp.asarray(_t5_buckets())]
    bias = bias.transpose(2, 0, 1).reshape(ATT_KV_HEADS, ATT_GROUP, CHUNK, band)
    s = s + bias[None, :, :, None]
    valid = (jnp.arange(n_c)[:, None] + jnp.arange(band)[None, :] // CHUNK) >= (WINDOW_CHUNKS - 1)
    s = jnp.where(valid[:, None, :], s, -jnp.inf)
    sink = sinks.astype(jnp.float32).reshape(ATT_KV_HEADS, ATT_GROUP)[None, :, :, None, None, None]
    m = jnp.maximum(jnp.max(s, axis=-1, keepdims=True), sink)
    p = jnp.exp(s - m)
    p = p / (jnp.sum(p, axis=-1, keepdims=True) + jnp.exp(sink - m))
    o = jnp.einsum('bhgcqk,bckhd->bcqhgd', p.astype(v.dtype), vb)
    return o.reshape(B, S, ATT_Q_W)

def _mixer(h, w_in, b_in, w_out, lb, hg_norm, sinks, rel_bias):
    B, S, _ = h.shape
    z = h @ w_in + b_in
    hq, hf, hi, hg, aq, ak, av = jnp.split(z, IN_SPLITS, axis=-1)
    o_rec = _hgrn2(hq, hf, hi, hg, lb, hg_norm)
    o_att = _swa_sink_attention(aq.reshape(B, S, ATT_HEADS, ATT_DH),
                                ak.reshape(B, S, ATT_KV_HEADS, ATT_DH),
                                av.reshape(B, S, ATT_KV_HEADS, ATT_DH), sinks, rel_bias)
    return jnp.concatenate([o_rec, o_att], axis=-1) @ w_out

def _hier_moe(h, w_group, b_group, w_sub, b_sub, w1, w3, w2):
    B, S, D = h.shape
    T = B * S
    xt = h.reshape(T, D)
    g_logits = (xt @ w_group + b_group).astype(jnp.float32)
    p_group = jax.nn.softmax(g_logits, axis=-1)
    _, g_sel = lax.top_k(g_logits, 1)
    p_sel = jnp.take_along_axis(p_group, g_sel, axis=1)
    e_logits = (xt @ w_sub + b_sub).astype(jnp.float32).reshape(T, N_GROUPS, EXPERTS_PER_GROUP)
    e_logits = jnp.take_along_axis(e_logits, g_sel[:, :, None], axis=1)[:, 0]
    top_v, top_i = lax.top_k(e_logits, TOP_K)
    weights = p_sel * jax.nn.softmax(top_v, axis=-1)
    eid = (g_sel * EXPERTS_PER_GROUP + top_i).astype(jnp.int32)
    A = T * TOP_K
    e_flat = eid.reshape(A)
    t_flat = jnp.repeat(jnp.arange(T, dtype=jnp.int32), TOP_K)
    w_flat = weights.reshape(A)
    se, st, sw = lax.sort((e_flat, t_flat, w_flat), num_keys=1, is_stable=True)
    counts = jnp.zeros((N_EXPERTS,), jnp.int32).at[e_flat].add(1)
    pcounts = (counts + EXPERT_BLOCK - 1) // EXPERT_BLOCK * EXPERT_BLOCK
    pend = jnp.cumsum(pcounts)
    pstart = pend - pcounts
    start = jnp.cumsum(counts) - counts
    dest = pstart[se] + jnp.arange(A, dtype=jnp.int32) - start[se]
    P = A + N_EXPERTS * EXPERT_BLOCK
    n_blocks = P // EXPERT_BLOCK
    slot_tok = jnp.full((P,), T, jnp.int32).at[dest].set(st)
    slot_w = jnp.zeros((P,), jnp.float32).at[dest].set(sw)
    blk_e = jnp.minimum(jnp.searchsorted(pend, jnp.arange(n_blocks, dtype=jnp.int32) * EXPERT_BLOCK,
                                         side='right'), N_EXPERTS - 1).astype(jnp.int32)
    x_pad = jnp.concatenate([xt, jnp.zeros((1, D), xt.dtype)], axis=0)
    xb = x_pad[slot_tok].reshape(n_blocks, EXPERT_BLOCK, D)

    def expert_block(args):
        xblk, e = args
        hid = jax.nn.silu(xblk @ w1[e]) * (xblk @ w3[e])
        return hid @ w2[e]

    yb = lax.map(expert_block, (xb, blk_e)).reshape(P, D)
    out = jnp.zeros((T + 1, D), h.dtype).at[slot_tok].add(yb * slot_w[:, None].astype(h.dtype))[:T]
    return out.reshape(B, S, D)

def setup_inputs(seed: int = 0) -> dict:
    key = jax.random.key(seed)
    ks = jax.random.split(key, 24)
    L, D = DEPTH, D_MODEL

    def nrm(k, shape, scale):
        return jax.random.normal(k, shape, jnp.float32) * scale

    col_scale = jnp.concatenate([
        jnp.ones((2 * HG_QK_W,), jnp.float32), jnp.full((HG_V_W,), BETA, jnp.float32),
        jnp.ones((HG_V_W + ATT_Q_W + ATT_KV_W,), jnp.float32), jnp.full((ATT_KV_W,), BETA, jnp.float32)])
    return {
        "x": nrm(ks[0], (BATCH, SEQ, D), 1.0),
        "c": nrm(ks[1], (BATCH, D), 1.0),
        "w_in": nrm(ks[2], (L, D, IN_DIM), D ** -0.5) * col_scale,
        "b_in": nrm(ks[3], (L, IN_DIM), 0.02),
        "w_out": nrm(ks[4], (L, MIX_W, D), MIX_W ** -0.5) * BETA,
        "hg_lower": nrm(ks[5], (L + 1, HG_QK_W), 1.0),
        "hg_norm": 1.0 + nrm(ks[6], (L, HG_DV), 0.02),
        "attn_sinks": nrm(ks[7], (L, ATT_HEADS), 0.5),
        "rel_bias": nrm(ks[8], (N_BUCKETS, ATT_HEADS), 0.5),
        "ada_w": nrm(ks[9], (L, D, 6 * D), 0.5 * D ** -0.5),
        "ada_b": nrm(ks[10], (L, 6 * D), 0.02),
        "ln1_g": 1.0 + nrm(ks[11], (L, D), 0.02),
        "ln1_b": nrm(ks[12], (L, D), 0.02),
        "ln2_g": 1.0 + nrm(ks[13], (L, D), 0.02),
        "ln2_b": nrm(ks[14], (L, D), 0.02),
        "w_group": nrm(ks[15], (L, D, N_GROUPS), D ** -0.5),
        "b_group": nrm(ks[16], (L, N_GROUPS), 0.01),
        "w_sub": nrm(ks[17], (L, D, N_EXPERTS), D ** -0.5),
        "b_sub": nrm(ks[18], (L, N_EXPERTS), 0.01),
        "w1": nrm(ks[19], (L, N_EXPERTS, D, D_EXPERT), D ** -0.5),
        "w3": nrm(ks[20], (L, N_EXPERTS, D, D_EXPERT), D ** -0.5) * BETA,
        "w2": nrm(ks[21], (L, N_EXPERTS, D_EXPERT, D), D_EXPERT ** -0.5) * BETA,
    }

def reference(x, c, w_in, b_in, w_out, hg_lower, hg_norm, attn_sinks, rel_bias, ada_w, ada_b,
              ln1_g, ln1_b, ln2_g, ln2_b, w_group, b_group, w_sub, b_sub, w1, w3, w2):
    lower_bounds = jnp.cumsum(jax.nn.softmax(hg_lower.astype(jnp.float32), axis=0), axis=0)
    cond = jax.nn.silu(c)
    for l in range(DEPTH):
        mod = cond @ ada_w[l] + ada_b[l]
        sh1, sc1, gt1, sh2, sc2, gt2 = [m[:, None, :] for m in jnp.split(mod, 6, axis=-1)]
        h = _layer_norm(x) * (1.0 + sc1) + sh1
        mix = _mixer(h, w_in[l], b_in[l], w_out[l], lower_bounds[l], hg_norm[l], attn_sinks[l], rel_bias)
        x = _layer_norm(ALPHA * x + gt1 * mix, ln1_g[l], ln1_b[l])
        h = _layer_norm(x) * (1.0 + sc2) + sh2
        ffn = _hier_moe(h, w_group[l], b_group[l], w_sub[l], b_sub[l], w1[l], w3[l], w2[l])
        x = _layer_norm(ALPHA * x + gt2 * ffn, ln2_g[l], ln2_b[l])
    return x


_drawn_inputs = setup_inputs


def setup_inputs(seed=0):
    import zlib

    import numpy as np

    out = dict(_drawn_inputs(seed))
    spreads = {}
    factors = {'b_in': 8.0,
     'hg_lower': 8.0,
     'hg_norm': 38.069,
     'attn_sinks': 64.0,
     'rel_bias': 8.0,
     'ada_b': 7.154,
     'ln1_g': 7.925,
     'ln1_b': 8.016,
     'ln2_g': 7.618,
     'ln2_b': 7.876,
     'b_group': 64.0,
     'b_sub': 64.0,
     'w_group': 5.041,
     'w_sub': 5.306,
     'w1': 4.964,
     'w3': 4.593,
     'w2': 4.613}
    for name, (base, spread) in spreads.items():
        noise = np.random.default_rng([zlib.crc32(name.encode()), seed]).standard_normal(out[name].shape)
        drawn = base * np.exp(spread * noise) if base else spread * noise
        out[name] = __import__('jax').numpy.asarray(drawn.astype(out[name].dtype))
    for name, factor in factors.items():
        out[name] = (out[name] * factor).astype(out[name].dtype)
    return out
```

```python
from contextlib import ExitStack

import numpy as np

import concourse.bass as bass
from concourse import mybir

P = 128
D = 1024
T = 1024
KD = D // P
NT = T // P
CHUNK = 64
HEADS = 4
HALF = 512
UNITS = HEADS * 2
LEVELS = [32, 16, 8, 4, 2, 1]
AH = 8
KVH = 2
GRP = 4
DH = 64
BAND = 192
DIFFS = 320
NE = 32
NG = 4
EPG = 8
DE = 512
MAX_BLOCKS = 48
COLS = MAX_BLOCKS + 2
ALPHA = 2.0 ** 0.25
EPS = 1e-5
NEG = -1.0e30
SLOT = 4096
OUTS = [((1, 1024, 1024), "float32")]


def block_kernel(nc, x, c, w_in, b_in_row, b_in_cols, w_out, hg_lower_cols, hg_norm, attn_sinks, rel_bias,
                 ada_w, ada_b, ln1_g, ln1_b, ln2_g, ln2_b, w_group, b_group, w_sub, b_sub, w1, w3, w2,
                 c_f32, c_masks, c_onehot, c_tokens, out):
    f32, i32, u32, u8 = mybir.dt.float32, mybir.dt.int32, mybir.dt.uint32, mybir.dt.uint8
    ALU, ACT, AX = mybir.AluOpType, mybir.ActivationFunctionType, mybir.AxisListType
    ctx = ExitStack()
    with ctx:
        def sb(name, shape, dt=f32):
            return ctx.enter_context(nc.sbuf_tensor(name, shape, dt))

        def sem(name):
            return ctx.enter_context(nc.semaphore(name))

        ring = sb("ring", [P, 6 * SLOT])
        hx = sb("hx", [P, NT * D])
        area = sb("area", [P, 17792])
        cf = sb("cf", [P, 128 * 2 + 48 + 8])
        masks = sb("masks", [P, 7 * P], u8)
        tokens = sb("tokens", [P, NT], i32)
        ones = sb("ones", [P, P])
        mean = sb("mean", [P, P])
        keep = sb("keep", [P, HALF], mybir.dt.bfloat16)
        modc = sb("modc", [P, 6, KD])
        adac = sb("adac", [P, 6, KD])
        cond = sb("cond", [P, KD])
        small = sb("small", [P, 1024])

        def slot(s):
            return ring[:, s * SLOT:(s + 1) * SLOT]

        mixT = ring[:, 4 * SLOT:6 * SLOT].rearrange("p (m t) -> p m t", m=8)
        hT = hx[:, :].rearrange("p (k t) -> p k t", k=KD)
        x2 = hx[:, :].rearrange("p (t d) -> p t d", t=NT)
        ident, tri = cf[:, 0:128], cf[:, 128:256]
        iota48, thresholds = cf[:, 256:304], cf[:, 304:312]

        cut = [0]

        def part(n):
            cut[0] += n
            assert cut[0] <= 17792, cut[0]
            return area[:, cut[0] - n:cut[0]]

        vtok = part(NT * 640).rearrange("p (t v) -> p t v", t=NT)
        kT = part(T)
        bias = part(AH * BAND).rearrange("p (h k) -> p h k", h=AH)
        sa_all = [part(64 + GRP * BAND) for _ in range(2)]
        ptp = part(GRP * CHUNK)
        pto = part(GRP * P)
        hg0 = cut[0]
        sg, fbuf, bcum, kbuf, score, qdec, kdec = (part(HALF) for _ in range(7))
        qbuf = [part(HALF) for _ in range(2)]
        ebuf = [part(HALF) for _ in range(2)]
        xbuf = [part(HALF) for _ in range(2)]
        state = part(8 * P).rearrange("p (c v) -> p c v", c=8)
        kdT, sq, rms = sa_all[0][:, 0:HALF], sa_all[1][:, 0:HALF], pto
        cut[0] = hg0
        xin = [part(D) for _ in range(2)]
        xn = [part(D) for _ in range(2)]
        acc = [part(HALF) for _ in range(2)]
        adarow = part(2048)
        trep = area[:, 0:AH * DIFFS].rearrange("p (h m) -> p h m", h=AH)
        wide_masks = area[:, 3072:3072 + 7 * P].bitcast(i32)
        relb = kT
        hirow = part(HALF)
        onehot = sa_all[1][:, 0:DIFFS]
        rowbuf = pto
        cut[0] = 0
        gt1 = part(D)
        g1, b1 = part(D), part(D)
        xr = [part(D) for _ in range(2)]
        rbuf = [part(D) for _ in range(2)]
        h2T = [part(D) for _ in range(2)]
        wr = part(KD * 36).rearrange("p (k n) -> p k n", k=KD)
        br = part(36)
        lg = part(NT * 36).rearrange("p (t n) -> p t n", t=NT)
        oh = [part(NT * NE).rearrange("p (t e) -> p t e", t=NT) for _ in range(2)]
        ohsum = part(NT * NE).rearrange("p (t e) -> p t e", t=NT)
        before = part(9 * NE).rearrange("p (t e) -> p t e", t=9)
        pos = part(NT * NE).rearrange("p (t e) -> p t e", t=NT)
        prod = part(NT * NE)
        counted = part(NE * 8).rearrange("p (e m) -> p e m", e=NE)
        blkcmp = part(48 * NE).rearrange("p (b e) -> p b e", b=48)
        cut[0] = 0
        xg = [part(D) for _ in range(2)]
        xT = [part(D) for _ in range(2)]
        sl = [part(DE) for _ in range(2)]
        hid = [part(DE) for _ in range(2)]
        hidT = [part(DE) for _ in range(2)]
        yo = [part(D) for _ in range(2)]
        gt2, g2, b2 = part(D), part(D), part(D)
        ya = [ring[:, i * D:(i + 1) * D] for i in range(2)]
        yb = [ring[:, (2 + i) * D:(3 + i) * D] for i in range(2)]
        fo = [ring[:, (4 + i) * D:(5 + i) * D] for i in range(2)]

        at = [0]

        def bit(*shape):
            n = int(np.prod(shape))
            at[0] += n
            assert at[0] <= 1024
            v = small[:, at[0] - n:at[0]]
            if len(shape) == 2:
                v = v.rearrange("p (a b) -> p a b", a=shape[0])
            return v

        stats = bit(2, 12)
        mv = bit(2, 2)
        rstd = bit(2, 1)
        lowc = bit(2, HEADS)
        lowd = bit(HEADS)
        lb, oml = bit(HEADS), bit(HEADS)
        bcols = bit(22)
        nbcols = bit(22)
        norm, eps = bit(1), bit(1)
        rel_src = bit(AH)
        carry = bit(P)
        sink = bit(AH)
        mx = bit(2, GRP)
        sums, esink, rden = bit(2, GRP), bit(2, GRP), bit(2, GRP)
        eblast = bit(8)
        ecols = bit(2, KD)
        gmax, emax = bit(NT, 8), bit(NT, 8)
        gpad, e8 = bit(NT, 8), bit(NT, 8)
        gsel = bit(NT)
        oh4 = bit(NT, NG)
        gexp = bit(NT, NG)
        psel, ex, den, wa, wb = bit(NT), bit(NT), bit(NT), bit(NT), bit(NT)
        eid = bit(2, NT)
        eidx = bit(2, NT)
        cnt, nblk, bend, bstart = bit(NE), bit(NE), bit(NE), bit(NE)
        slotf = bit(2, NT)
        addrf = bit(2, NT)
        ebf = bit(48)
        gidx = sb("gidx", [P, NT, 8], u32)
        eix = sb("eix", [P, NT, 8], u32)
        sloti = sb("sloti", [P, 2, NT], i32)
        blki = sb("blki", [P, 2, NT], i32)
        rowi = sb("rowi", [P, 2, NT], i32)
        addri = sb("addri", [P, 2, NT], i32)
        ebi = sb("ebi", [P, 48], i32)
        npi = sb("npi", [P, 2], i32)
        slot_tok = sb("slot_tok", [P, COLS], i32)
        pick = [sb(f"pick{i}", [P, 1], i32) for i in range(2)]

        ps = ctx.enter_context(nc.psum_tensor("ps", [P, 8 * 512], f32))

        def bank(b, n=1):
            return ps[:, b * 512:(b + n) * 512]

        diffs_d = nc.dram_tensor("diffs_d", [P, AH, DIFFS], f32).ap()
        gates_d = nc.dram_tensor("gates_d", [2, D], f32).ap()
        n2_d = nc.dram_tensor("n2_d", [T, D], f32).ap()
        table_d = nc.dram_tensor("table_d", [P * COLS, 1], i32).ap()
        y_d = nc.dram_tensor("y_d", [(MAX_BLOCKS + 4) * P, D], f32).ap()

        piece_in = [sem(f"piece_in{s}") for s in range(5)]
        consts_in, cols_in, rows_in, x_in = sem("consts_in"), sem("cols_in"), sem("rows_in"), [sem("x_in0"), sem("x_in1")]
        set_up, filled = sem("set_up"), sem("filled")
        cond_e, cond_ready = sem("cond_e"), sem("cond_ready")
        xn_ready, xt_done, xt_evac = sem("xn_ready"), sem("xt_done"), sem("xt_evac")
        ada_summed, mod_done, mod_read, row_out = sem("ada_summed"), sem("mod_done"), sem("mod_read"), sem("row_out")
        lowexp = sem("lowexp")
        rel_rows, trep_done, trep_read, diffs_out, bias_in, bias_ready = (
            sem("rel_rows"), sem("trep_done"), sem("trep_read"), sem("diffs_out"), sem("bias_in"), sem("bias_ready"))
        v_done, v_evac = sem("v_done"), sem("v_evac")
        z_done, z_act, z_dve, z_sig, q_dec = (sem(n) for n in ("z_done", "z_act", "z_dve", "z_sig", "q_dec"))
        var_ready, rstd_ready, rms_ready = sem("var_ready"), sem("rstd_ready"), sem("rms_ready")
        o_scaled = sem("o_scaled")
        h_ready, xv_evac = sem("h_ready"), sem("xv_evac")
        blocks_out, spare_out = sem("blocks_out"), sem("spare_out")
        row_ready, sa_clear = sem("row_ready"), sem("sa_clear")
        s_done, s_shift, p_exp, p_ready, pt_done, pt_evac, o_done, o_evac, sa_read = (sem(n) for n in (
            "s_done", "s_shift", "p_exp", "p_ready", "pt_done", "pt_evac", "o_done", "o_evac", "sa_read"))
        f_ready, lf_ready, scanned, e_in, e_out, x_ready, gram_done, gram_read = (sem(n) for n in (
            "f_ready", "lf_ready", "scanned", "e_in", "e_out", "x_ready", "gram_done", "gram_read"))
        dec_out, kd_in, kd_out, kd_ready, kdt_done, kdt_evac, u_done, st_ready, ho_done, sq_ready, ms_done, head_out = (
            sem(n) for n in ("dec_out", "kd_in", "kd_out", "kd_ready", "kdt_done", "kdt_evac", "u_done", "st_ready",
                             "ho_done", "sq_ready", "ms_done", "head_out"))
        mix_done, mix_read, xr_in, r_in, n2_ready, n2_out, t2_done, t2_evac, rt_done, rt_read = (
            sem("mix_done"), sem("mix_read"), [sem("xr_in0"), sem("xr_in1")], sem("r_in"), sem("n2_ready"),
            [sem("n2_out0"), sem("n2_out1")], sem("t2_done"), sem("t2_evac"), sem("rt_done"), sem("rt_read"))
        rexp_in, rexp_out, onehots, ranked, addr_ready, table_out, scattered, table_in, plan_ready = (sem(n) for n in (
            "rexp_in", "rexp_out", "onehots", "ranked", "addr_ready", "table_out", "scattered", "table_in", "plan_ready"))
        w1_in, w3_in, w2_in = ([sem(f"{n}_in{b}") for b in range(2)] for n in ("w1", "w3", "w2"))
        pick_ready = sem("pick_ready")
        xg_in = [sem(f"xg_in{b}") for b in range(2)]
        xg_t, xT_evac, g_done, u2_done, silu_out, hid_ready, ht_done, ht_evac, y_done, y_act, y_dve = (sem(n) for n in (
            "xg_t", "xT_evac", "g_done", "u2_done", "silu_out", "hid_ready", "ht_done", "ht_evac", "y_done",
            "y_act", "y_dve"))
        y_out = [sem(f"y_out{b}") for b in range(2)]
        ya_in, yb_in = [sem("ya_in0"), sem("ya_in1")], [sem("yb_in0"), sem("yb_in1")]
        ys_read, fin_ready, fin_out = sem("ys_read"), sem("fin_ready"), [sem("fin_out0"), sem("fin_out1")]
        fin_rows = sem("fin_rows")
        v_chain, a_chain, p_chain = sem("v_chain"), sem("a_chain"), sem("p_chain")

        held = {0: ["ada0", "kv", "hf", "wo1"], 1: ["ada1", "aq", "hq"], 2: ["ada2", "hi", "hg"],
                3: ["ada3", "ada4", "ada6", "ada8", "ada10", "wo0"], 4: ["ada5", "ada7", "ada9", "ada11"]}
        place = {n: (s, i + 1) for s, names in held.items() for i, n in enumerate(names)}
        W_COL = {"hq": 0, "hf": 512, "hi": 1024, "hg": 1536, "aq": 2048, "kv": 2560}
        Z0 = 10
        Z_ALL = Z0 + 3 * UNITS

        def arrived(eng, name):
            s, n = place[name]
            eng.wait_ge(piece_in[s], 16 * n)

        def view(name, n=512):
            return slot(place[name][0])[:, 0:KD * n].rearrange("p (k f) -> p k f", k=KD)

        w_in_v = w_in[0].rearrange("(p k) n -> p k n", p=P)
        ada_v = ada_w[0].rearrange("(p k) n -> p k n", p=P)

        block = ctx.enter_context(nc.Block())

        @block.sync
        def _(sp):
            def load(name, src, dst):
                s, n = place[name]
                sp.dma_start(dst, src).then_inc(piece_in[s], 16)

            def load_ada(n):
                load(f"ada{n}", ada_v[:, :, n * 512:(n + 1) * 512], view(f"ada{n}"))

            def load_z(name, n=512):
                load(name, w_in_v[:, :, W_COL[name]:W_COL[name] + n], view(name, n))

            for n in range(4):
                load_ada(n)
            sp.wait_ge(ada_summed, 1)
            load_z("kv", 256)
            sp.wait_ge(ada_summed, 2)
            load_z("aq")
            sp.wait_ge(ada_summed, 3)
            load_z("hi")
            sp.wait_ge(ada_summed, 4)
            load_ada(4)
            load_ada(5)
            for n in range(6, 12):
                sp.wait_ge(ada_summed, n - 1)
                load_ada(n)
            sp.wait_ge(z_done, Z0)
            load_z("hq")
            sp.wait_ge(v_done, NT)
            load_z("hf")
            load_z("hg")
            sp.wait_ge(ada_summed, 11)
            load("wo0", w_out[0, 0:512, :].rearrange("(m p) n -> p m n", p=P), slot(3).rearrange("p (m n) -> p m n", m=4))
            sp.wait_ge(z_done, Z_ALL - 2)
            wo1 = slot(0).rearrange("p (m n) -> p m n", m=4)
            for g in range(KVH):
                rows = w_out[0, 512 + g * 256:768 + g * 256, :].rearrange("(j p) n -> p j n", p=DH)
                sp.dma_start(wo1[g * DH:(g + 1) * DH, :, :], rows).then_inc(piece_in[0], 16)

            sp.wait_ge(plan_ready, 1)
            pairs = sp.value_load(npi[0:1, 0:1], min_val=1, max_val=MAX_BLOCKS // 2)
            with sp.Fori(0, pairs) as i:
                for b in range(2):
                    j = i * 2 + b
                    e = sp.value_load(ebi[0:1, bass.ds(j, 1)], min_val=0, max_val=NE - 1)
                    sp.wait_ge(g_done, j + 1)
                    sp.dma_start(slot(3 * b), w1[0][bass.ds(e, 1)].rearrange("o (p k) f -> (o p) (k f)", p=P)).then_inc(w1_in[b], 16)
                    sp.wait_ge(u2_done, j + 1)
                    sp.dma_start(slot(3 * b + 1), w3[0][bass.ds(e, 1)].rearrange("o (p k) f -> (o p) (k f)", p=P)).then_inc(w3_in[b], 16)
                    sp.wait_ge(y_done, j * 2 + 1)
                    sp.dma_start(slot(3 * b + 2), w2[0][bass.ds(e, 1)].rearrange("o (p k) f -> (o p) (k f)", p=P)).then_inc(w2_in[b], 16)

        @block.gpsimd
        def _(pool):
            nc.gpsimd.memset(ones[:], 1.0).then_inc(set_up, 1)
            nc.gpsimd.memset(keep[:], 1.0).then_inc(filled, 1)
            nc.gpsimd.memset(slot_tok[:], 0).then_inc(set_up, 1)
            nc.gpsimd.memset(eps, EPS)
            nc.gpsimd.memset(mean[:], 1.0 / P).then_inc(set_up, 1)
            pool.wait_ge(filled, 1)
            nc.gpsimd.memset(keep[:].rearrange("p (c s) -> p c s", s=CHUNK)[:, :, 0:1], 0.0).then_inc(set_up, 1)
            pool.wait_ge(set_up, 4)
            pool.dma_start(table_d.rearrange("(p j) o -> p (j o)", p=P), slot_tok[:]).then_inc(table_out, 16)
            pool.wait_ge(trep_read, AH)
            pool.dma_start(diffs_d, trep).then_inc(diffs_out, 16)
            pool.wait_ge(diffs_out, 16)
            skewed = bass.AP(tensor=diffs_d.tensor, offset=P - 1, ap=[[AH * DIFFS - 1, P], [DIFFS, AH], [1, BAND]])
            pool.dma_start(bias, skewed).then_inc(bias_in, 16)
            for r in range(4):
                pool.wait_ge(row_ready, r + 1)
                pool.dma_start(gates_d[r // 2:r // 2 + 1, (r % 2) * 512:(r % 2 + 1) * 512], rowbuf[0:1, :]).then_inc(row_out, 16)
            pool.wait_ge(addr_ready, 1)
            pool.wait_ge(table_out, 16)
            for ch in range(2):
                for t in range(NT):
                    nc.gpsimd.indirect_dma_start(
                        out=table_d, out_offset=bass.IndirectOffsetOnAxis(ap=addri[:, ch, t:t + 1], axis=0),
                        in_=tokens[:, t:t + 1], in_offset=None).then_inc(scattered, 16)
            pool.wait_ge(scattered, 16 * 2 * NT)
            pool.dma_start(slot_tok[:], table_d.rearrange("(p j) o -> p (j o)", p=P)).then_inc(table_in, 16)
            pool.wait_ge(table_in, 16)
            for b in range(2):
                pool.wait_ge(n2_out[b], 16 * NT // 2)

            def gather(b):
                nc.gpsimd.indirect_dma_start(
                    out=xg[b], out_offset=None, in_=n2_d,
                    in_offset=bass.IndirectOffsetOnAxis(ap=pick[b][:, 0:1], axis=0)).then_inc(xg_in[b], 16)

            pool.wait_ge(plan_ready, 1)
            pairs = pool.value_load(npi[0:1, 0:1], min_val=1, max_val=MAX_BLOCKS // 2)
            picks = pool.alloc_register("picks")
            pool.reg_mov(picks, 3)
            for b in range(2):
                nc.gpsimd.tensor_copy(pick[b][:], slot_tok[:, b:b + 1]).then_inc(pick_ready, 1)
                pool.wait_ge(pick_ready, b + 1)
                gather(b)
            pool.wait_ge(fin_rows, 16 * 3)
            with pool.Fori(pairs, MAX_BLOCKS // 2 + 1) as i:
                for b in range(2):
                    pool.dma_start(y_d[bass.ds((i * 2 + b) * P, P), :], gt2).then_inc(spare_out, 16)
            with pool.Fori(0, pairs) as i:
                for b in range(2):
                    j = i * 2 + b
                    pool.wait_ge(xg_t, j + 1)
                    pool.wait_ge(xg_in[b], i * 16 + 16)
                    nc.gpsimd.tensor_copy(pick[b][:], slot_tok[:, bass.ds(j + 2, 1)]).then_inc(pick_ready, 1)
                    pool.wait_ge(pick_ready, picks)
                    pool.reg_add(picks, picks, 1)
                    gather(b)

            pool.wait_ge(blocks_out, 1)
            for t in range(NT):
                if t >= 2:
                    pool.wait_ge(ys_read, t - 1)
                for ch, (buf, got) in enumerate(((ya, ya_in), (yb, yb_in))):
                    nc.gpsimd.indirect_dma_start(
                        out=buf[t % 2], out_offset=None, in_=y_d,
                        in_offset=bass.IndirectOffsetOnAxis(ap=sloti[:, ch, t:t + 1], axis=0)).then_inc(got[t % 2], 16)

        @block.scalar
        def _(act):
            n_link = [0]

            def link(ins):
                n_link[0] += 1
                ins.then_inc(a_chain, 1)
                act.wait_ge(a_chain, n_link[0])

            n_norm = [0]

            def root(s):
                n_norm[0] += 1
                act.wait_ge(var_ready, n_norm[0])
                link(nc.scalar.activation(rstd[:, s, :], mv[:, s, 1:2], ACT.Ln, bias=eps))
                nc.scalar.activation(rstd[:, s, :], rstd[:, s, :], ACT.Exp, scale=-0.5).then_inc(rstd_ready, 1)

            def evac_x(t):
                act.wait_ge(xt_done, t + 1)
                nc.scalar.activation(hT[:, 0:4, t * P:(t + 1) * P],
                                     bank(4 + 2 * (t % 2)).rearrange("p (k t) -> p k t", k=4), ACT.Copy).then_inc(xt_evac, 1)

            def sigmoid(z, col, dst, sem_out):
                act.wait_ge(z_done, z + 1)
                nc.scalar.activation(dst, bank(z % 2), ACT.Exp, bias=nbcols[:, col:col + 1], scale=-1.0).then_inc(z_act, 1)
                act.wait_ge(z_act, z + 1)
                link(nc.scalar.activation(dst, dst, ACT.Ln, bias=ones[:, 0:1]))
                nc.scalar.activation(dst, dst, ACT.Exp, scale=-1.0).then_inc(sem_out, 1)

            act.dma_start(cond[:], c.rearrange("o (p k) -> (o p) k", p=P)).then_inc(cols_in, 16)
            for t in range(2):
                act.dma_start(xin[t], x[0, t * P:(t + 1) * P, :]).then_inc(x_in[t], 16)
            act.dma_start(cf[:], c_f32).then_inc(consts_in, 16)
            act.dma_start(wide_masks, c_masks).then_inc(consts_in, 16)
            act.dma_start(onehot[0:32, :], c_onehot).then_inc(consts_in, 16)
            act.dma_start(tokens[:], c_tokens).then_inc(consts_in, 16)
            for kind in (0, 1, 3, 4):
                act.dma_start(adac[:, kind, :], ada_b[0, kind * D:(kind + 1) * D].rearrange("(p k) -> p k", p=P)).then_inc(cols_in, 16)
            act.dma_start(bcols, b_in_cols).then_inc(cols_in, 16)
            act.dma_start(lowc, hg_lower_cols.rearrange("p (r h) -> p r h", r=2)).then_inc(cols_in, 16)
            act.dma_start(norm, hg_norm[0].rearrange("(p o) -> p o", o=1)).then_inc(cols_in, 16)
            act.dma_start(sink, attn_sinks.broadcast_to([P, AH])).then_inc(rows_in, 16)
            act.dma_start(hirow, b_in_row[:, 0:HALF].broadcast_to([P, HALF])).then_inc(rows_in, 16)
            act.dma_start(carry, b_in_row[:, HALF:640].broadcast_to([P, P])).then_inc(rows_in, 16)
            act.dma_start(rel_src[0:32], rel_bias).then_inc(rows_in, 16)
            for i, kind in enumerate((2, 5)):
                act.dma_start(adarow[0:1, i * D:(i + 1) * D], ada_b[0:1, kind * D:(kind + 1) * D]).then_inc(rows_in, 16)
            act.wait_ge(cols_in, 16 * 8)
            act.wait_ge(set_up, 4)
            root(0)
            root(1)
            link(nc.scalar.activation(ecols[:, 0, :], cond[:], ACT.Exp, scale=-1.0))
            link(nc.scalar.activation(ecols[:, 0, :], ecols[:, 0, :], ACT.Ln, bias=ones[:, 0:1]))
            nc.scalar.activation(ecols[:, 0, :], ecols[:, 0, :], ACT.Exp, scale=-1.0).then_inc(cond_e, 1)
            act.wait_ge(lowexp, 1)
            nc.scalar.activation(lowc, lowc, ACT.Exp).then_inc(lowexp, 1)
            for t in range(2, NT + 2):
                if t >= 4:
                    root(t % 2)
                evac_x(t - 2)
                if t < NT:
                    act.wait_ge(xn_ready, t - 1)
                    act.dma_start(xin[t % 2], x[0, t * P:(t + 1) * P, :]).then_inc(x_in[t % 2], 16)
            act.wait_ge(mod_read, 1)
            act.wait_ge(xt_evac, NT)
            for k in range(4):
                last = nc.scalar.activation(hT[:, k, :], hT[:, k, :], ACT.Identity, bias=modc[:, 0, k:k + 1], scale=modc[:, 1, k:k + 1])
            last.then_inc(h_ready, 1)
            for z in range(Z0):
                act.wait_ge(z_done, z + 1)
                half = z % 2
                dst = kT[:, half * HALF:(half + 1) * HALF] if z < 2 else mixT[:, 4 + (z - 2) // 2, half * HALF:(half + 1) * HALF]
                col = 20 if z < 2 else 16 + (z - 2) // 2
                nc.scalar.activation(dst, bank(z % 2), ACT.Identity, bias=bcols[:, col:col + 1]).then_inc(z_act, 1)

            def attn_exp(n):
                act.wait_ge(s_shift, n + 1)
                lo = CHUNK if n < 2 else 0
                v = sa_all[n % 2][:, 64:].rearrange("p (h k) -> p h k", h=GRP)[:, :, lo:]
                nc.scalar.activation(v, v, ACT.Exp)
                nc.scalar.activation(esink[:, n % 2, :], esink[:, n % 2, :], ACT.Exp).then_inc(p_exp, 1)

            def attn_evac(n):
                i, g = n // 2, n % 2
                act.wait_ge(pt_done, n + 1)
                last = nc.scalar.activation(pto, bank(4), ACT.Copy)
                if i:
                    last = nc.scalar.activation(ptp[CHUNK:P, :], bank(5)[CHUNK:P, 0:GRP * CHUNK], ACT.Copy)
                last.then_inc(pt_evac, 1)

            def attn_out(n):
                i, g = n // 2, n % 2
                act.wait_ge(o_done, n + 1)
                nc.scalar.activation(mixT[g * DH:(g + 1) * DH, 4:8, i * P:(i + 1) * P],
                                     bank(4)[g * DH:(g + 1) * DH, :].rearrange("p (j t) -> p j t", j=GRP),
                                     ACT.Copy).then_inc(o_evac, 1)

            def exp_level(u, lv):
                act.wait_ge(e_in, 6 * u + lv + 1)
                nc.scalar.activation(ebuf[lv % 2], ebuf[lv % 2], ACT.Exp).then_inc(e_out, 1)

            def gate_z(n):
                period, which = n // 3, n % 3
                h, half = period // 2, period % 2
                dst = (sg, qbuf[period % 2], mixT[:, h, half * HALF:(half + 1) * HALF])[which]
                if which == 0 and period:
                    act.wait_ge(f_ready, period)
                if which == 1 and period >= 2:
                    act.wait_ge(gram_read, 7 * (period - 1))
                sigmoid(Z0 + n, (4, 0, 12)[which] + h, dst, z_sig)

            act.wait_ge(row_out, 16 * 4)
            for n in range(16):
                attn_exp(n)
                if n >= 2:
                    attn_evac(n - 2)
                    attn_out(n - 2)
            for n in (14, 15):
                attn_evac(n)
                attn_out(n)

            def rms_root(u):
                act.wait_ge(ms_done, u + 1)
                link(nc.scalar.activation(rms, bank(7), ACT.Ln, bias=eps))
                nc.scalar.activation(rms, rms, ACT.Exp, scale=-0.5).then_inc(rms_ready, 1)

            for period in range(UNITS + 1):
                u = period - 1
                for part3 in range(3):
                    n = 3 * period + part3
                    if 1 <= n <= 3 * UNITS:
                        gate_z(n - 1)
                    if u < 0:
                        continue
                    if part3 == 0:
                        act.wait_ge(f_ready, u + 1)
                        nc.scalar.activation(ebuf[1], fbuf, ACT.Ln).then_inc(lf_ready, 1)
                        act.wait_ge(scanned, u + 1)
                        if u:
                            act.wait_ge(ho_done, u)
                            act.wait_ge(st_ready, u)
                        nc.scalar.activation(qdec, bcum, ACT.Exp)
                        nc.scalar.activation(eblast, bcum.rearrange("p (c s) -> p c s", s=CHUNK)[:, :, CHUNK - 1:CHUNK].rearrange("p c o -> p (c o)"),
                                             ACT.Exp).then_inc(dec_out, 1)
                        exp_level(u, 0)
                        act.wait_ge(kd_in, u + 1)
                        nc.scalar.activation(kdec, kdec, ACT.Exp).then_inc(kd_out, 1)
                        exp_level(u, 1)
                        if u:
                            rms_root(u - 1)
                        for lv in (2, 3):
                            exp_level(u, lv)
                        act.wait_ge(kdt_done, u + 1)
                        nc.scalar.activation(kdT, bank(2), ACT.Copy).then_inc(kdt_evac, 1)
                    elif part3 == 1:
                        for lv in (4, 5):
                            exp_level(u, lv)
                    else:
                        act.wait_ge(ho_done, u + 1)
                        nc.scalar.activation(sq, bank(6), ACT.Square).then_inc(sq_ready, 1)
            rms_root(UNITS - 1)

            act.wait_ge(head_out, UNITS)
            act.wait_ge(row_out, 16 * 4)
            for dst, src in ((gt1, gates_d[0:1, :]), (g1, ln1_g), (b1, ln1_b)):
                act.dma_start(dst, src.broadcast_to([P, D])).then_inc(r_in, 16)
            for t in range(2):
                act.dma_start(xr[t], x[0, t * P:(t + 1) * P, :]).then_inc(xr_in[t], 16)
            act.dma_start(wr[:, :, 0:NG], w_group[0].rearrange("(p k) n -> p k n", p=P)).then_inc(r_in, 16)
            act.dma_start(wr[:, :, NG:36], w_sub[0].rearrange("(p k) n -> p k n", p=P)).then_inc(r_in, 16)
            act.dma_start(br[:, 0:NG], b_group.broadcast_to([P, NG])).then_inc(r_in, 16)
            act.dma_start(br[:, NG:36], b_sub.broadcast_to([P, NE])).then_inc(r_in, 16)
            for t in range(NT):
                root(0)
                root(1)
                act.wait_ge(n2_ready, t + 1)
                act.dma_start(n2_d[t * P:(t + 1) * P, :], rbuf[t % 2]).then_inc(n2_out[t % 2], 16)
                if t + 2 < NT:
                    act.dma_start(xr[t % 2], x[0, (t + 2) * P:(t + 3) * P, :]).then_inc(xr_in[t % 2], 16)
                act.wait_ge(t2_done, t + 1)
                if t >= 2:
                    act.wait_ge(rt_done, t - 1)
                for k in range(KD):
                    last = nc.scalar.activation(h2T[t % 2][:, k * P:(k + 1) * P], bank(4, 2)[:, k * P:(k + 1) * P],
                                                ACT.Identity, bias=modc[:, 3, k:k + 1], scale=modc[:, 4, k:k + 1])
                last.then_inc(t2_evac, 1)
            act.wait_ge(rexp_in, 1)
            nc.scalar.activation(gexp, gexp, ACT.Exp).then_inc(rexp_out, 1)
            act.wait_ge(rexp_in, 2)
            nc.scalar.activation(ex, ex, ACT.Exp).then_inc(rexp_out, 1)

            act.wait_ge(plan_ready, 1)
            for dst, src in ((gt2, gates_d[1:2, :]), (g2, ln2_g), (b2, ln2_b)):
                act.dma_start(dst, src.broadcast_to([P, D])).then_inc(fin_rows, 16)
            pairs = act.value_load(npi[0:1, 0:1], min_val=1, max_val=MAX_BLOCKS // 2)

            def evac_block(b, count):
                act.wait_ge(xg_t, count)
                for k in range(KD):
                    last = nc.scalar.activation(xT[b][:, k * P:(k + 1) * P], bank(0, 2)[:, k * P:(k + 1) * P],
                                                ACT.Identity, bias=modc[:, 3, k:k + 1], scale=modc[:, 4, k:k + 1])
                last.then_inc(xT_evac, 1)

            act.wait_ge(fin_rows, 16 * 3)
            for b in range(2):
                act.dma_start(y_d[(MAX_BLOCKS + 2 + b) * P:(MAX_BLOCKS + 3 + b) * P, :], gt2).then_inc(y_out[b], 16)
            for free in (silu_out, y_act):
                act.sem_inc(free, 1)
            evac_block(0, 1)
            with act.Fori(0, pairs) as i:
                for b in range(2):
                    j = i * 2 + b
                    act.wait_ge(g_done, j + 3)
                    act.wait_ge(hid_ready, j + 1)
                    nc.scalar.activation(sl[b], bank(2), ACT.Silu).then_inc(silu_out, 1)
                    evac_block(1 - b, j + 2)
                    act.wait_ge(y_done, j * 2 + 4)
                    act.wait_ge(y_out[b], i * 16 + 16)
                    nc.scalar.activation(yo[b][:, 0:HALF], bank(6), ACT.Copy).then_inc(y_act, 1)
                    act.wait_ge(y_act, j + 2)
                    act.wait_ge(y_dve, j + 2)
                    act.dma_start(y_d[bass.ds(j * P, P), :], yo[b]).then_inc(y_out[b], 16)
            for t in range(NT):
                root(0)
                act.wait_ge(fin_ready, t + 1)
                act.dma_start(out[0, t * P:(t + 1) * P, :], fo[t % 2]).then_inc(fin_out[t % 2], 16)
            for b in range(2):
                act.wait_ge(fin_out[b], 16 * NT // 2)

        @block.vector
        def _(dve):
            n_link = [0]

            def link(ins):
                n_link[0] += 1
                ins.then_inc(v_chain, 1)
                dve.wait_ge(v_chain, n_link[0])

            V = nc.vector
            n_norm = [0]

            def normalise(src, dst, s, done=None):
                V.bn_stats(stats[:, s, 0:6], src[:, 0:512])
                link(V.bn_stats(stats[:, s, 6:12], src[:, 512:1024]))
                V.bn_aggr(mv[:, s, :], stats[:, s, :]).then_inc(var_ready, 1)
                n_norm[0] += 1
                dve.wait_ge(var_ready, n_norm[0])
                dve.wait_ge(rstd_ready, n_norm[0])
                ins = V.tensor_scalar(dst, src, mv[:, s, 0:1], rstd[:, s, :], ALU.subtract, ALU.mult)
                if done is None:
                    link(ins)
                else:
                    ins.then_inc(done, 1)

            def layer_norm1(t):
                dve.wait_ge(x_in[t % 2], 16 * (t // 2 + 1))
                if t >= 2:
                    dve.wait_ge(xt_done, t - 1)
                normalise(xin[t % 2], xn[t % 2], t % 2, xn_ready)

            def ada_sum(n):
                arrived(dve, f"ada{n}")
                if n >= 2:
                    dve.wait_ge(mod_done, n - 1)
                a, w = acc[n % 2], view(f"ada{n}")
                link(V.tensor_scalar(a, w[:, 0, :], cond[:, 0:1], None, ALU.mult))
                for k in range(1, KD):
                    ins = V.scalar_tensor_tensor(a, w[:, k, :], cond[:, k:k + 1], a, ALU.mult, ALU.add)
                    if k < KD - 1:
                        link(ins)
                ins.then_inc(ada_summed, 1)

            def take_row(r):
                dve.wait_ge(mod_done, (5, 6, 11, 12)[r])
                if r:
                    dve.wait_ge(row_out, 16 * r)
                V.tensor_copy(rowbuf, bank(3)).then_inc(row_ready, 1)

            def evac_x(t):
                dve.wait_ge(xt_done, t + 1)
                V.tensor_copy(hT[:, 4:8, t * P:(t + 1) * P], bank(5 + 2 * (t % 2)).rearrange("p (k t) -> p k t", k=4)).then_inc(xv_evac, 1)

            layer_norm1(0)
            layer_norm1(1)
            dve.wait_ge(cols_in, 16 * 8)
            dve.wait_ge(cond_e, 1)
            link(V.tensor_tensor(cond[:], cond[:], ecols[:, 0, :], ALU.mult))
            link(V.tensor_tensor(lowd, lowc[:, 0, :], lowc[:, 1, :], ALU.max))
            V.tensor_tensor(lowc, lowc, lowd[:, None, :].broadcast_to([P, 2, HEADS]), ALU.subtract).then_inc(lowexp, 1)
            dve.wait_ge(lowexp, 2)
            link(V.tensor_tensor(lowd, lowc[:, 0, :], lowc[:, 1, :], ALU.add))
            link(V.reciprocal(lowd, lowd))
            link(V.tensor_tensor(lb, lowc[:, 0, :], lowd, ALU.mult))
            link(V.tensor_scalar(oml, lb, -1.0, 1.0, ALU.mult, ALU.add))
            link(V.tensor_scalar(nbcols, bcols, -1.0, None, ALU.mult))
            evac_x(0)
            layer_norm1(2)
            evac_x(1)
            layer_norm1(3)
            for n in range(4):
                ada_sum(n)
                evac_x(n + 2)
                if n + 4 < NT:
                    layer_norm1(n + 4)
            dve.wait_ge(mod_done, 4)
            V.scalar_tensor_tensor(modc[:, 0, :], bank(2)[:, 0:KD], 0.0, adac[:, 0, :], ALU.add, ALU.add)
            V.scalar_tensor_tensor(modc[:, 1, :], bank(2)[:, KD:2 * KD], 1.0, adac[:, 1, :], ALU.add, ALU.add).then_inc(mod_read, 1)
            dve.wait_ge(mod_read, 1)
            evac_x(NT - 2)
            evac_x(NT - 1)
            dve.wait_ge(xv_evac, NT)
            for k in range(4, KD):
                ins = V.tensor_scalar(hT[:, k, :], hT[:, k, :], modc[:, 1, k:k + 1], modc[:, 0, k:k + 1], ALU.mult, ALU.add)
            ins.then_inc(h_ready, 1)
            dve.wait_ge(rows_in, 16 * 6)
            dve.wait_ge(consts_in, 16 * 4)
            V.tensor_copy(masks[:], wide_masks)
            V.tensor_copy(relb[0:32, :].rearrange("b (h m) -> b h m", h=AH),
                          rel_src[0:32, :, None].broadcast_to([32, AH, P])).then_inc(rel_rows, 1)
            for h in range(AH):
                dve.wait_ge(trep_done, h + 1)
                V.tensor_copy(trep[:, h, :], bank(h % 2)[:, 0:DIFFS]).then_inc(trep_read, 1)
            dve.wait_ge(bias_in, 16)
            V.memset(bias[0:CHUNK, :, P:BAND], NEG)
            V.memset(bias[CHUNK:P, :, 0:CHUNK], NEG).then_inc(bias_ready, 1)
            row = 0
            for n in range(4, 12):
                ada_sum(n)
                if n in (4, 5, 10, 11):
                    take_row(row)
                    row += 1
            V.memset(sa_all[0][:, 0:64], 0.0)
            V.memset(sa_all[1][:, 0:64], 0.0).then_inc(sa_clear, 1)
            V.scalar_tensor_tensor(modc[:, 3, :], bank(2)[:, 3 * KD:4 * KD], 0.0, adac[:, 3, :], ALU.add, ALU.add)
            V.scalar_tensor_tensor(modc[:, 4, :], bank(2)[:, 4 * KD:5 * KD], 1.0, adac[:, 4, :], ALU.add, ALU.add).then_inc(mod_read, 1)
            dve.wait_ge(sa_clear, 1)
            dve.wait_ge(bias_ready, 1)

            def attn_shift(n):
                i, g = n // 2, n % 2
                lo = CHUNK if i == 0 else 0
                v = sa_all[n % 2][:, 64:].rearrange("p (h k) -> p h k", h=GRP)[:, :, lo:]
                src = bank(2, 2).rearrange("p (h k) -> p h k", h=GRP)[:, :, lo:BAND]
                dve.wait_ge(s_done, n + 1)
                if n >= 2:
                    dve.wait_ge(pt_done, n - 1)
                V.scalar_tensor_tensor(v, src, DH ** -0.5, bias[:, g * GRP:(g + 1) * GRP, lo:], ALU.mult, ALU.add).then_inc(sa_read, 1)
                dve.wait_ge(sa_read, n + 1)
                link(V.tensor_reduce(mx[:, n % 2, :], v, AX.X, ALU.max))
                link(V.tensor_tensor(mx[:, n % 2, :], mx[:, n % 2, :], sink[:, g * GRP:(g + 1) * GRP], ALU.max))
                V.tensor_tensor(v, v, mx[:, n % 2, :, None].broadcast_to([P, GRP, BAND - lo]), ALU.subtract)
                V.tensor_tensor(esink[:, n % 2, :], sink[:, g * GRP:(g + 1) * GRP], mx[:, n % 2, :], ALU.subtract).then_inc(s_shift, 1)

            def attn_divide(n):
                i = n // 2
                lo = CHUNK if i == 0 else 0
                v = sa_all[n % 2][:, 64:].rearrange("p (h k) -> p h k", h=GRP)[:, :, lo:]
                dve.wait_ge(p_exp, n + 1)
                link(V.tensor_reduce(sums[:, n % 2, :], v, AX.X, ALU.add))
                link(V.tensor_tensor(sums[:, n % 2, :], sums[:, n % 2, :], esink[:, n % 2, :], ALU.add))
                link(V.reciprocal(rden[:, n % 2, :], sums[:, n % 2, :]))
                V.tensor_tensor(v, v, rden[:, n % 2, :, None].broadcast_to([P, GRP, BAND - lo]), ALU.mult).then_inc(p_ready, 1)

            def halves(buf, w):
                v = buf.rearrange("p (n two w) -> p n two w", two=2, w=w)
                return v[:, :, 0, :], v[:, :, 1, :]

            def level_exponent(u, lv):
                w = LEVELS[lv]
                lo, hi = halves(bcum, w)
                elo, ehi = halves(ebuf[lv % 2], w)
                ref = lo[:, :, w - 1:w].broadcast_to([P, HALF // (2 * w), w])
                if lv == 1:
                    dve.wait_ge(scanned, u + 1)
                V.tensor_tensor(elo, ref, lo, ALU.subtract)
                V.tensor_tensor(ehi, hi, ref, ALU.subtract).then_inc(e_in, 1)

            def level_factors(u, lv):
                w = LEVELS[lv]
                klo, _ = halves(kbuf, w)
                _, qhi = halves(qbuf[u % 2], w)
                elo, ehi = halves(ebuf[lv % 2], w)
                xlo, xhi = halves(xbuf[lv % 2], w)
                dve.wait_ge(e_out, 6 * u + lv + 1)
                if lv >= 2:
                    dve.wait_ge(gram_done, 7 * u + lv)
                V.tensor_tensor(xlo, klo, elo, ALU.mult)
                V.tensor_tensor(xhi, qhi, ehi, ALU.mult).then_inc(x_ready, 1)

            def take_gram(u, s):
                dve.wait_ge(gram_done, 7 * u + s + 1)
                g = bank(4 + s % 2).rearrange("p (i t) -> p i t", i=4)
                sc = score.rearrange("p (i t) -> p i t", i=4)
                if s == 0:
                    if u:
                        dve.wait_ge(ho_done, u)
                    V.tensor_tensor(sc, g, ident[:, None, :].broadcast_to([P, 4, P]), ALU.mult).then_inc(gram_read, 1)
                else:
                    dve.wait_ge(gram_read, 7 * u + s)
                    V.copy_predicated(sc, masks[:, None, s * P:(s + 1) * P].broadcast_to([P, 4, P]), g).then_inc(gram_read, 1)

            def gate_z(n):
                z, ph, phalf = Z0 + n, n // 6, (n // 3) % 2
                dst = qbuf[phalf] if n % 3 == 1 else mixT[:, ph, phalf * HALF:(phalf + 1) * HALF]
                col = (0 if n % 3 == 1 else 12) + ph
                dve.wait_ge(z_sig, n + 1)
                V.scalar_tensor_tensor(dst, bank(z % 2), bcols[:, col:col + 1], dst, ALU.add, ALU.mult).then_inc(z_dve, 1)

            for i in range(NT):
                attn_shift(2 * i)
                if i:
                    attn_divide(2 * i - 1)
                attn_shift(2 * i + 1)
                attn_divide(2 * i)
                dve.wait_ge(v_done, i + 1)
                V.tensor_tensor(vtok[:, i, 0:512], bank(i % 2), hirow, ALU.add)
                V.tensor_tensor(vtok[:, i, 512:640], bank(6 + i % 2)[:, 0:128], carry, ALU.add).then_inc(v_evac, 1)
            attn_divide(15)

            def head_norm(u):
                dve.wait_ge(rms_ready, u + 1)
                dve.wait_ge(z_dve, 2 * u + 2)
                g = mixT[:, u // 2, (u % 2) * HALF:(u % 2 + 1) * HALF]
                V.tensor_tensor(rms, rms, bank(6), ALU.mult).then_inc(o_scaled, 1)
                dve.wait_ge(o_scaled, u + 1)
                V.scalar_tensor_tensor(g, g, norm[:, 0:1], rms, ALU.mult, ALU.mult).then_inc(head_out, 1)

            def carry_states(u):
                dve.wait_ge(u_done, u + 1)
                if u:
                    dve.wait_ge(ho_done, u)
                upd = bank(2, 2).rearrange("p (o c v) -> p c o v", o=2, c=4)
                if u % 2 == 0:
                    link(V.memset(state[:, 0, :], 0.0))
                else:
                    link(V.tensor_copy(state[:, 0, :], carry))
                for cc in range(7):
                    link(V.scalar_tensor_tensor(state[:, cc + 1, :], state[:, cc, :], eblast[:, cc:cc + 1], upd[:, cc // 2, cc % 2, :], ALU.mult, ALU.add))
                V.scalar_tensor_tensor(carry, state[:, 7, :], eblast[:, 7:8], upd[:, 3, 1, :], ALU.mult, ALU.add).then_inc(st_ready, 1)
                dve.wait_ge(st_ready, u + 1)

            for period in range(UNITS + 1):
                u = period - 1
                h = u // 2
                for part3 in range(3):
                    n = 3 * period + part3
                    if 1 <= n <= 3 * UNITS and (n - 1) % 3:
                        gate_z(n - 1)
                    if u < 0:
                        continue
                    if part3 == 0:
                        dve.wait_ge(z_sig, 3 * u + 1)
                        link(V.tensor_scalar(fbuf, sg, oml[:, h:h + 1], lb[:, h:h + 1], ALU.mult, ALU.add))
                        V.tensor_scalar(kbuf, fbuf, -1.0, 1.0, ALU.mult, ALU.add).then_inc(f_ready, 1)
                        dve.wait_ge(lf_ready, u + 1)
                        V.tensor_tensor_scan(bcum, keep[:], ebuf[1], 0.0, ALU.mult, ALU.add).then_inc(scanned, 1)
                        dve.wait_ge(scanned, u + 1)
                        level_exponent(u, 0)
                        b3 = bcum.rearrange("p (c s) -> p c s", s=CHUNK)
                        V.tensor_tensor(kdec.rearrange("p (c s) -> p c s", s=CHUNK),
                                        b3[:, :, CHUNK - 1:CHUNK].broadcast_to([P, 8, CHUNK]), b3, ALU.subtract).then_inc(kd_in, 1)
                        dve.wait_ge(f_ready, u + 1)
                        level_exponent(u, 1)
                        dve.wait_ge(dec_out, u + 1)
                        dve.wait_ge(z_dve, 2 * u + 1)
                        V.tensor_tensor(qdec, qdec, qbuf[u % 2], ALU.mult).then_inc(q_dec, 1)
                        level_factors(u, 0)
                        dve.wait_ge(kd_out, u + 1)
                        V.tensor_tensor(kdec, kdec, kbuf, ALU.mult).then_inc(kd_ready, 1)
                        take_gram(u, 0)
                        dve.wait_ge(x_ready, 6 * u + 1)
                        level_exponent(u, 2)
                        level_factors(u, 1)
                        if u:
                            head_norm(u - 1)
                        take_gram(u, 1)
                        dve.wait_ge(x_ready, 6 * u + 2)
                        level_exponent(u, 3)
                        level_factors(u, 2)
                        take_gram(u, 2)
                    elif part3 == 1:
                        dve.wait_ge(x_ready, 6 * u + 3)
                        level_exponent(u, 4)
                        level_factors(u, 3)
                        take_gram(u, 3)
                        dve.wait_ge(x_ready, 6 * u + 4)
                        level_exponent(u, 5)
                        carry_states(u)
                        level_factors(u, 4)
                        take_gram(u, 4)
                        level_factors(u, 5)
                        take_gram(u, 5)
                    else:
                        take_gram(u, 6)
            head_norm(UNITS - 1)

            V.memset(before[:, 0, :], 0.0)
            V.memset(gpad, -3.0e38)
            dve.wait_ge(r_in, 16 * 7)
            for t in range(NT):
                dve.wait_ge(mix_done, t + 1)
                dve.wait_ge(xr_in[t % 2], 16 * (t // 2 + 1))
                if t >= 2:
                    dve.wait_ge(n2_out[t % 2], 16 * (t // 2))
                    dve.wait_ge(t2_done, t - 1)
                r = rbuf[t % 2]
                V.tensor_tensor(r, bank(2 * (t % 2), 2), gt1, ALU.mult).then_inc(mix_read, 1)
                dve.wait_ge(mix_read, t + 1)
                link(V.scalar_tensor_tensor(r, xr[t % 2], ALPHA, r, ALU.mult, ALU.add))
                normalise(r, x2[:, t, :], 0)
                link(V.tensor_tensor(x2[:, t, :], x2[:, t, :], g1, ALU.mult))
                link(V.tensor_tensor(x2[:, t, :], x2[:, t, :], b1, ALU.add))
                normalise(x2[:, t, :], r, 1, n2_ready)
                if t:
                    dve.wait_ge(rt_done, t)
                    V.tensor_tensor(lg[:, t - 1, :], bank(6 + (t - 1) % 2)[:, 0:36], br, ALU.add).then_inc(rt_read, 1)
            dve.wait_ge(rt_done, NT)
            V.tensor_tensor(lg[:, NT - 1, :], bank(7)[:, 0:36], br, ALU.add).then_inc(rt_read, 1)
            dve.wait_ge(rt_read, NT)
            link(V.tensor_copy(gpad[:, :, 0:NG], lg[:, :, 0:NG]))
            for t in range(NT):
                link(V.max(gmax[:, t, :], gpad[:, t, :]))
                link(V.max_index(gidx[:, t, :], gmax[:, t, :], gpad[:, t, :]))
            V.tensor_tensor(gexp, lg[:, :, 0:NG], gmax[:, :, 0:1].broadcast_to([P, NT, NG]), ALU.subtract).then_inc(rexp_in, 1)
            link(V.tensor_copy(gsel, gidx[:, :, 0]))
            link(V.tensor_tensor(oh4, iota48[:, None, 0:NG].broadcast_to([P, NT, NG]), gsel[:, :, None].broadcast_to([P, NT, NG]), ALU.is_equal))
            link(V.tensor_tensor(prod.rearrange("p (t e g) -> p t e g", t=NT, g=NG),
                                 lg[:, :, NG:36].rearrange("p t (g e) -> p t e g", g=NG),
                                 oh4[:, :, None, :].broadcast_to([P, NT, EPG, NG]), ALU.mult))
            link(V.tensor_reduce(e8, prod.rearrange("p (t e g) -> p t e g", t=NT, g=NG), AX.X, ALU.add))
            for t in range(NT):
                link(V.max(emax[:, t, :], e8[:, t, :]))
                link(V.max_index(eix[:, t, :], emax[:, t, :], e8[:, t, :]))
            V.tensor_tensor(ex, emax[:, :, 1], emax[:, :, 0], ALU.subtract).then_inc(rexp_in, 1)
            for ch in range(2):
                link(V.tensor_copy(eidx[:, ch, :], eix[:, :, ch]))
                link(V.scalar_tensor_tensor(eid[:, ch, :], gsel, float(EPG), eidx[:, ch, :], ALU.mult, ALU.add))
                link(V.tensor_tensor(oh[ch], iota48[:, None, 0:NE].broadcast_to([P, NT, NE]),
                                     eid[:, ch, :, None].broadcast_to([P, NT, NE]), ALU.is_equal))
            link(V.tensor_tensor(ohsum, oh[0], oh[1], ALU.add))
            for t in range(NT):
                ins = V.tensor_tensor(before[:, t + 1, :], before[:, t, :], ohsum[:, t, :], ALU.add)
                if t < NT - 1:
                    link(ins)
            ins.then_inc(onehots, 1)
            dve.wait_ge(rexp_out, 2)
            link(V.tensor_reduce(psel, gexp, AX.X, ALU.add))
            link(V.tensor_scalar(den, ex, 1.0, None, ALU.add))
            link(V.tensor_tensor(den, den, psel, ALU.mult))
            link(V.reciprocal(wa, den))
            link(V.tensor_tensor(wb, wa, ex, ALU.mult))
            dve.wait_ge(ranked, 1)
            link(V.tensor_copy(cnt, bank(1)[:, 0:NE]))
            link(V.tensor_tensor(counted, cnt[:, :, None].broadcast_to([P, NE, 8]),
                                 thresholds[:, None, :].broadcast_to([P, NE, 8]), ALU.is_gt))
            link(V.tensor_reduce(nblk, counted, AX.X, ALU.add))
            link(V.tensor_tensor_scan(bend, ones[:, 0:NE], nblk, 0.0, ALU.mult, ALU.add))
            link(V.tensor_tensor(bstart, bend, nblk, ALU.subtract))
            link(V.tensor_scalar(bstart, bstart, float(P), None, ALU.mult))
            link(V.tensor_tensor(pos, bank(0)[:, 0:NT * NE].rearrange("p (t e) -> p t e", t=NT),
                                 bstart[:, None, :].broadcast_to([P, NT, NE]), ALU.add))
            for ch in range(2):
                pv = prod.rearrange("p (t e) -> p t e", t=NT)
                link(V.tensor_tensor(pv, oh[ch], pos, ALU.mult))
                link(V.tensor_reduce(slotf[:, ch, :], pv, AX.X, ALU.add))
            link(V.tensor_copy(sloti[:], slotf))
            link(V.tensor_scalar(blki[:], sloti[:], 7, None, ALU.arith_shift_right))
            link(V.tensor_scalar(rowi[:], sloti[:], P - 1, None, ALU.bitwise_and))
            link(V.tensor_copy(slotf, blki[:]))
            link(V.tensor_copy(addrf, rowi[:]))
            link(V.scalar_tensor_tensor(addrf, addrf, float(COLS), slotf, ALU.mult, ALU.add))
            V.tensor_copy(addri[:], addrf).then_inc(addr_ready, 1)
            link(V.tensor_tensor(blkcmp[0:1], iota48[0:1, :, None].broadcast_to([1, 48, NE]),
                                 bend[0:1, None, :].broadcast_to([1, 48, NE]), ALU.is_ge))
            link(V.tensor_reduce(ebf[0:1], blkcmp[0:1], AX.X, ALU.add))
            link(V.tensor_scalar(ebf[0:1], ebf[0:1], float(NE - 1), None, ALU.min))
            link(V.tensor_copy(ebi[0:1], ebf[0:1]))
            link(V.tensor_scalar(cnt[0:1, 0:1], bend[0:1, NE - 1:NE], 1.0, None, ALU.add))
            link(V.tensor_copy(npi[0:1, 1:2], cnt[0:1, 0:1]))
            link(V.tensor_scalar(npi[0:1, 0:1], npi[0:1, 1:2], 1, None, ALU.arith_shift_right))
            link(V.tensor_copy(cnt[0:1, 1:2], npi[0:1, 0:1]))
            link(V.tensor_scalar(cnt[0:1, 1:2], cnt[0:1, 1:2], -1.0, float(MAX_BLOCKS // 2 + 1), ALU.mult, ALU.add))
            V.tensor_copy(npi[0:1, 1:2], cnt[0:1, 1:2]).then_inc(plan_ready, 1)

            dve.wait_ge(plan_ready, 1)
            pairs = dve.value_load(npi[0:1, 0:1], min_val=1, max_val=MAX_BLOCKS // 2)
            spare = dve.value_load(npi[0:1, 1:2], min_val=1, max_val=MAX_BLOCKS // 2)
            for free in (hid_ready, y_dve):
                dve.sem_inc(free, 1)
            with dve.Fori(0, pairs) as i:
                for b in range(2):
                    j = i * 2 + b
                    dve.wait_ge(u2_done, j + 3)
                    dve.wait_ge(silu_out, j + 2)
                    V.tensor_tensor(hid[b], sl[b], bank(3), ALU.mult).then_inc(hid_ready, 1)
                    dve.wait_ge(ht_done, j + 1)
                    V.tensor_copy(hidT[b], bank(4)).then_inc(ht_evac, 1)
                    dve.wait_ge(y_done, j * 2 + 5)
                    dve.wait_ge(y_out[b], i * 16 + 16)
                    V.tensor_copy(yo[b][:, HALF:D], bank(7)).then_inc(y_dve, 1)

            for b in range(2):
                dve.wait_ge(y_out[b], pairs * 16 + 16)
            dve.wait_ge(y_done, pairs * 4 + 3)
            for b in range(2):
                dve.wait_ge(xg_in[b], pairs * 16 + 16)
            dve.wait_ge(spare_out, spare * 32)
            V.memset(stats[:, 0, 0:1], 0.0).then_inc(blocks_out, 1)

            dve.wait_ge(fin_rows, 16 * 3)
            for t in range(NT):
                a, b_, f = ya[t % 2], yb[t % 2], fo[t % 2]
                dve.wait_ge(ya_in[t % 2], 16 * (t // 2 + 1))
                dve.wait_ge(yb_in[t % 2], 16 * (t // 2 + 1))
                if t >= 2:
                    dve.wait_ge(fin_out[t % 2], 16 * (t // 2))
                link(V.tensor_scalar(a, a, wa[:, t:t + 1], None, ALU.mult))
                link(V.scalar_tensor_tensor(f, b_, wb[:, t:t + 1], a, ALU.mult, ALU.add))
                V.tensor_tensor(f, f, gt2, ALU.mult).then_inc(ys_read, 1)
                dve.wait_ge(ys_read, t + 1)
                link(V.scalar_tensor_tensor(f, x2[:, t, :], ALPHA, f, ALU.mult, ALU.add))
                normalise(f, f, 0)
                link(V.tensor_tensor(f, f, g2, ALU.mult))
                V.tensor_tensor(f, f, b2, ALU.add).then_inc(fin_ready, 1)

        @block.tensor
        def _(pe):
            M = nc.tensor.matmul

            def transposes(src, dst, n, step):
                v = src.rearrange("p (d k) -> p k d", k=step)
                for k in range(n):
                    last = nc.tensor.transpose(dst[:, k * P:(k + 1) * P], v[:, k, :], ident)
                return last

            def transpose_x(t):
                pe.wait_ge(xn_ready, t + 1)
                if t >= 2:
                    pe.wait_ge(xt_evac, t - 1)
                    pe.wait_ge(xv_evac, t - 1)
                transposes(xn[t % 2], bank(4 + 2 * (t % 2), 2), KD, KD).then_inc(xt_done, 1)

            def reduce_mod(n):
                pe.wait_ge(ada_summed, n + 1)
                kind, half = n // 2, n % 2
                if kind in (2, 5):
                    r = {4: 0, 5: 1, 10: 2, 11: 3}[n]
                    if r:
                        pe.wait_ge(row_ready, r)
                    M(bank(3), lhsT=ones[:], rhs=acc[n % 2], start=True, stop=False)
                    last = M(bank(3), lhsT=ones[0:1, :], rhs=adarow[0:1, r * 512:(r + 1) * 512], start=False, stop=True)
                else:
                    v = acc[n % 2].rearrange("p (m k) -> p k m", k=KD)
                    for k in range(KD):
                        last = M(bank(2)[half * 64:half * 64 + 64, kind * KD + k:kind * KD + k + 1],
                                 lhsT=v[:, k, :], rhs=ones[:, 0:1], start=True, stop=True)
                last.then_inc(mod_done, 1)

            pe.wait_ge(consts_in, 16 * 4)
            pe.wait_ge(set_up, 4)
            for t in range(4):
                transpose_x(t)
            for n in range(4):
                reduce_mod(n)
                transpose_x(n + 4)
            pe.wait_ge(rows_in, 16 * 6)
            pe.wait_ge(rel_rows, 1)
            for h in range(AH):
                if h >= 2:
                    pe.wait_ge(trep_read, h - 1)
                M(bank(h % 2)[:, 0:DIFFS], lhsT=relb[0:32, h * P:(h + 1) * P], rhs=onehot[0:32, :], start=True, stop=True).then_inc(trep_done, 1)
            pe.wait_ge(h_ready, 2)
            pe.wait_ge(trep_read, AH)

            def z_free(z):
                if z >= 2:
                    pe.wait_ge(z_act, z - 1)
                    turn = z - 2 - Z0
                    if turn >= 1:
                        pe.wait_ge(z_dve, 2 * (turn // 3) + turn % 3)

            def z_steps(z, stationary, half, ks):
                for k in ks:
                    last = M(bank(z % 2), lhsT=stationary[:, k], rhs=hT[:, k, half * HALF:(half + 1) * HALF],
                             start=(k == 0), stop=(k == KD - 1))
                if ks[-1] == KD - 1:
                    last.then_inc(z_done, 1)

            for z in range(Z0):
                z_free(z)
                if z == 0:
                    arrived(pe, "kv")
                if z == 2:
                    arrived(pe, "aq")
                st = view("kv", 256)[:, :, 0:P] if z < 2 else view("aq")[:, :, (z - 2) // 2 * P:((z - 2) // 2 + 1) * P]
                z_steps(z, st, z % 2, list(range(KD)))
                if z >= 2:
                    reduce_mod(z + 2)
            pe.wait_ge(bias_ready, 1)
            pe.wait_ge(mod_read, 2)
            pe.wait_ge(row_ready, 4)

            def attn_scores(n):
                i, g = n // 2, n % 2
                pe.wait_ge(z_act, Z0)
                if n:
                    pe.wait_ge(sa_read, n)
                base, lo = g * DH, (CHUNK if i == 0 else 0)
                for j in range(GRP):
                    last = M(bank(2, 2)[:, j * 256 + lo:j * 256 + BAND],
                             lhsT=mixT[base:base + DH, 4 + j, i * P:(i + 1) * P],
                             rhs=kT[base:base + DH, i * P - CHUNK + lo:(i + 1) * P], start=True, stop=True)
                last.then_inc(s_done, 1)

            def attn_transpose(n):
                i, g = n // 2, n % 2
                pe.wait_ge(p_ready, n + 1)
                if n:
                    pe.wait_ge(o_evac, n)
                p = sa_all[n % 2]
                for j in range(GRP):
                    last = nc.tensor.transpose(bank(4)[:, j * P:(j + 1) * P], p[:, 128 + j * BAND:256 + j * BAND], ident)
                if i:
                    for j in range(GRP):
                        last = nc.tensor.transpose(bank(5)[:, j * CHUNK:(j + 1) * CHUNK], p[0:CHUNK, j * BAND:j * BAND + P],
                                                   ident[0:CHUNK, 0:CHUNK])
                last.then_inc(pt_done, 1)

            def attn_values(n):
                i, g = n // 2, n % 2
                pe.wait_ge(pt_evac, n + 1)
                pe.wait_ge(v_evac, i + 1)
                base = g * DH
                o = bank(4)[base:base + DH, :]
                last = M(o, lhsT=vtok[:, i, 512 + base:512 + base + DH], rhs=pto, start=True, stop=(i == 0))
                if i:
                    last = M(o.rearrange("p (j t) -> p j t", j=GRP)[:, :, 0:CHUNK],
                             lhsT=vtok[CHUNK:P, i - 1, 512 + base:512 + base + DH],
                             rhs=ptp[CHUNK:P, :].rearrange("p (j t) -> p j t", j=GRP), start=False, stop=True)
                last.then_inc(o_done, 1)

            def gram(u, s):
                a, b = (kbuf, qbuf[u % 2]) if s == 0 else (xbuf[(s - 1) % 2],) * 2
                if s == 0:
                    pe.wait_ge(f_ready, u + 1)
                    pe.wait_ge(z_dve, 2 * u + 1)
                else:
                    pe.wait_ge(x_ready, 6 * u + s)
                if s >= 2:
                    pe.wait_ge(gram_read, 7 * u + s - 1)
                elif u:
                    pe.wait_ge(gram_read, 7 * u)
                for i in range(4):
                    last = M(bank(4 + s % 2)[:, i * P:(i + 1) * P], lhsT=a[:, i * P:(i + 1) * P], rhs=b[:, i * P:(i + 1) * P],
                             start=True, stop=True)
                last.then_inc(gram_done, 1)

            def decayed_keys(u):
                pe.wait_ge(kd_ready, u + 1)
                if u:
                    pe.wait_ge(st_ready, u)
                for i in range(4):
                    last = nc.tensor.transpose(bank(2)[:, i * P:(i + 1) * P], kdec[:, i * P:(i + 1) * P], ident)
                last.then_inc(kdt_done, 1)

            def state_updates(u):
                h, half = u // 2, u % 2
                pe.wait_ge(kdt_evac, u + 1)
                for cc in range(8):
                    i, r = cc // 2, (cc % 2) * CHUNK
                    last = M(bank(2 + cc % 2)[:, i * P:(i + 1) * P], lhsT=kdT[r:r + CHUNK, i * P:(i + 1) * P],
                             rhs=vtok[r:r + CHUNK, half * 4 + i, h * P:(h + 1) * P], start=True, stop=True)
                last.then_inc(u_done, 1)

            def head_product(u):
                h, half = u // 2, u % 2
                pe.wait_ge(st_ready, u + 1)
                pe.wait_ge(q_dec, u + 1)
                pe.wait_ge(gram_read, 7 * u + 7)
                if u:
                    pe.wait_ge(head_out, u)
                for i in range(4):
                    o = bank(6)[:, i * P:(i + 1) * P]
                    M(o, lhsT=vtok[:, half * 4 + i, h * P:(h + 1) * P], rhs=score[:, i * P:(i + 1) * P], start=True, stop=False,
                      skip_group_check=True)
                    for cc in (2 * i, 2 * i + 1):
                        last = M(bank(6)[:, cc * CHUNK:(cc + 1) * CHUNK], lhsT=state[:, cc, :], rhs=qdec[:, cc * CHUNK:(cc + 1) * CHUNK],
                                 start=False, stop=True, skip_group_check=True)
                last.then_inc(ho_done, 1)

            def mean_square(u):
                if u:
                    pe.wait_ge(rms_ready, u)
                pe.wait_ge(sq_ready, u + 1)
                M(bank(7), lhsT=mean[:], rhs=sq, start=True, stop=True).then_inc(ms_done, 1)

            arrived(pe, "hi")
            for i in range(NT):
                for step in range(2):
                    n = 2 * i + step
                    attn_scores(n)
                    if i:
                        attn_transpose(n - 2)
                    if step == 0 and i >= 2:
                        pe.wait_ge(v_evac, i - 1)
                    for k in range(4 * step, 4 * step + 4):
                        M(bank(i % 2), lhsT=hT[:, k, i * P:(i + 1) * P], rhs=view("hi")[:, k, :], start=(k == 0), stop=(k == KD - 1))
                    if step:
                        for k in range(KD):
                            last = M(bank(6 + i % 2)[:, 0:P], lhsT=hT[:, k, i * P:(i + 1) * P], rhs=view("kv", 256)[:, k, P:2 * P],
                                     start=(k == 0), stop=(k == KD - 1))
                        last.then_inc(v_done, 1)
                    if i:
                        attn_values(n - 2)
            for n in (14, 15):
                attn_transpose(n)
                attn_values(n)
            pe.wait_ge(v_evac, NT)
            pe.wait_ge(o_evac, 16)

            for name in ("hf", "hq", "hg"):
                arrived(pe, name)
            for period in range(UNITS + 1):
                u = period - 1
                for part3 in range(3):
                    z = Z0 + 3 * period + part3
                    if period < UNITS:
                        z_free(z)
                        st = view(("hf", "hq", "hg")[part3])[:, :, (period // 2) * P:(period // 2 + 1) * P]
                    for quarter in range(4):
                        if period < UNITS:
                            z_steps(z, st, period % 2, [2 * quarter, 2 * quarter + 1])
                        if u < 0:
                            continue
                        step = 4 * part3 + quarter
                        if step in (0, 1, 2):
                            gram(u, step)
                        elif step == 3:
                            decayed_keys(u)
                        elif step == 4:
                            gram(u, 3)
                        elif step == 5:
                            state_updates(u)
                        elif step in (6, 7, 8):
                            gram(u, step - 2)
                        elif step == 10:
                            head_product(u)
                        elif step == 11:
                            mean_square(u)

            pe.wait_ge(head_out, UNITS)
            pe.wait_ge(o_evac, 16)
            arrived(pe, "wo0")
            pe.wait_ge(piece_in[0], 16 * 5)
            wo = [slot(s).rearrange("p (m n) -> p m n", m=4) for s in (3, 0)]

            def route(t):
                pe.wait_ge(n2_ready, t + 1)
                if t:
                    pe.wait_ge(t2_evac, t)
                transposes(rbuf[t % 2], bank(4, 2), KD, KD).then_inc(t2_done, 1)
                pe.wait_ge(t2_evac, t + 1)
                pe.wait_ge(r_in, 16 * 7)
                if t >= 2:
                    pe.wait_ge(rt_read, t - 1)
                for k in range(KD):
                    last = M(bank(6 + t % 2)[:, 0:36], lhsT=h2T[t % 2][:, k * P:(k + 1) * P], rhs=wr[:, k, :],
                             start=(k == 0), stop=(k == KD - 1))
                last.then_inc(rt_done, 1)

            for t in range(NT):
                if t >= 2:
                    pe.wait_ge(mix_read, t - 1)
                for half in range(2):
                    for m in range(8):
                        last = M(bank(2 * (t % 2) + half), lhsT=mixT[:, m, t * P:(t + 1) * P],
                                 rhs=wo[m // 4][:, m % 4, half * HALF:(half + 1) * HALF], start=(m == 0), stop=(m == 7))
                last.then_inc(mix_done, 1)
                if t:
                    route(t - 1)
            route(NT - 1)
            pe.wait_ge(onehots, 1)
            M(bank(0)[:, 0:NT * NE], lhsT=tri, rhs=ohsum, start=True, stop=False)
            M(bank(0)[:, 0:NT * NE], lhsT=ones[:], rhs=before[:, 0:NT, :], start=False, stop=True)
            M(bank(1)[:, 0:NE], lhsT=ones[:], rhs=before[:, NT, :], start=True, stop=True).then_inc(ranked, 1)

            pe.wait_ge(plan_ready, 1)
            for done, n in ((g_done, 2), (u2_done, 2), (y_done, 3)):
                pe.sem_inc(done, n)
            pairs = pe.value_load(npi[0:1, 0:1], min_val=1, max_val=MAX_BLOCKS // 2)
            pe.wait_ge(xg_in[0], 16)
            transposes(xg[0], bank(0, 2), KD, KD).then_inc(xg_t, 1)
            with pe.Fori(0, pairs) as i:
                for b in range(2):
                    j = i * 2 + b
                    nb = 1 - b
                    w1v, w3v = (slot(3 * b + s).rearrange("p (k f) -> p k f", k=KD) for s in range(2))
                    w2v = slot(3 * b + 2).rearrange("p (k f) -> p k f", k=4)
                    pe.wait_ge(xT_evac, j + 1)
                    pe.wait_ge(silu_out, j + 1)
                    pe.wait_ge(w1_in[b], i * 16 + 16)
                    for k in range(KD):
                        last = M(bank(2), lhsT=xT[b][:, k * P:(k + 1) * P], rhs=w1v[:, k, :], start=(k == 0), stop=(k == KD - 1))
                    last.then_inc(g_done, 1)
                    pe.wait_ge(hid_ready, j + 1)
                    pe.wait_ge(w3_in[b], i * 16 + 16)
                    for k in range(KD):
                        last = M(bank(3), lhsT=xT[b][:, k * P:(k + 1) * P], rhs=w3v[:, k, :], start=(k == 0), stop=(k == KD - 1))
                    last.then_inc(u2_done, 1)
                    pe.wait_ge(xg_in[nb], i * 16 + (16 if b == 0 else 32))
                    transposes(xg[nb], bank(0, 2), KD, KD).then_inc(xg_t, 1)
                    pe.wait_ge(hid_ready, j + 2)
                    transposes(hid[b], bank(4), 4, 4).then_inc(ht_done, 1)
                    pe.wait_ge(ht_evac, j + 1)
                    pe.wait_ge(w2_in[b], i * 16 + 16)
                    pe.wait_ge(y_act, j + 1)
                    for k in range(4):
                        last = M(bank(6), lhsT=hidT[b][:, k * P:(k + 1) * P], rhs=w2v[:, k, 0:HALF], start=(k == 0), stop=(k == 3))
                    last.then_inc(y_done, 1)
                    pe.wait_ge(y_dve, j + 1)
                    for k in range(4):
                        last = M(bank(7), lhsT=hidT[b][:, k * P:(k + 1) * P], rhs=w2v[:, k, HALF:D], start=(k == 0), stop=(k == 3))
                    last.then_inc(y_done, 1)


def constants():
    i = np.arange(P)
    f = np.zeros((P, 2 * P + 56), np.float32)
    f[:, :P] = np.eye(P)
    f[:, P:2 * P] = i[:, None] < i[None, :]
    f[:, 2 * P:2 * P + 48] = np.arange(48)
    f[:, 2 * P + 48:] = np.arange(8) * P
    m = np.zeros((P, 7, P), np.int32)
    for n, w in enumerate(LEVELS):
        m[:, n + 1] = ((i[:, None] // (2 * w) == i[None, :] // (2 * w)) & (i[:, None] % (2 * w) < w)
                       & (i[None, :] % (2 * w) >= w))
    n = BAND - 1 - np.arange(DIFFS)
    side = (n < 0).astype(np.int32) * 16
    n = np.abs(n)
    far = np.minimum(8 + (np.log(np.maximum(n, 1) / 8) / np.log(128 / 8) * 8).astype(np.int32), 15)
    bucket = side + np.where(n < 8, n, far)
    onehot = (np.arange(32)[:, None] == bucket[None, :]).astype(np.float32)
    tok = (np.arange(NT)[None, :] * P + i[:, None]).astype(np.int32)
    return f, m.reshape(P, 7 * P), onehot, tok


def kernel(**inputs):
    import concourse.bacc as bacc
    from concourse.bass_utils import run_bass_kernel_spmd

    b_in = np.asarray(inputs["b_in"])
    tiles = b_in[0].reshape(22, P)
    heads = tiles[16:20].reshape(KVH, GRP, DH).transpose(1, 0, 2).reshape(GRP, P)
    low = np.asarray(inputs["hg_lower"])
    w_in = np.asarray(inputs["w_in"])
    order = np.arange(w_in.shape[2])
    order[2048:2560] = order[2048:2560].reshape(KVH, GRP, DH).transpose(1, 0, 2).reshape(-1)
    given = {k: np.ascontiguousarray(inputs[k]) for k in ("x", "c")}
    given["w_in"] = np.ascontiguousarray(w_in[:, :, order])
    given["b_in_row"] = np.ascontiguousarray(np.concatenate([b_in[:, 1024:1536], b_in[:, 2688:2816]], axis=1))
    given["b_in_cols"] = np.ascontiguousarray(np.concatenate([tiles[:16], heads, tiles[20:]]).T)
    given["w_out"] = np.ascontiguousarray(inputs["w_out"])
    given["hg_lower_cols"] = np.ascontiguousarray(low.reshape(2, HEADS, P).transpose(2, 0, 1).reshape(P, 2 * HEADS))
    for k in ("hg_norm", "attn_sinks", "rel_bias", "ada_w", "ada_b", "ln1_g", "ln1_b", "ln2_g", "ln2_b", "w_group",
              "b_group", "w_sub", "b_sub", "w1", "w3", "w2"):
        given[k] = np.ascontiguousarray(inputs[k])
    given["c_f32"], given["c_masks"], given["c_onehot"], given["c_tokens"] = constants()

    nc = bacc.Bacc("TRN2", target_bir_lowering=False, num_devices=1)
    arrays, args = {}, []
    for name, a in given.items():
        arrays[f"in_{name}"] = a
        args.append(nc.dram_tensor(f"in_{name}", a.shape, mybir.dt.from_np(a.dtype), kind="ExternalInput").ap())
    args.append(nc.dram_tensor("out_0", OUTS[0][0], mybir.dt.float32, kind="ExternalOutput").ap())
    block_kernel(nc, *args)
    r = run_bass_kernel_spmd(nc, [arrays], core_ids=[0])
    return r.results[0]["out_0"]
```

```python
from contextlib import ExitStack

import numpy as np

import concourse.bass as bass
from concourse import mybir

P = 128
D = 1024
T = 1024
KD = D // P
NT = T // P
CHUNK = 64
HEADS = 4
HALF = 512
UNITS = HEADS * 2
LEVELS = [32, 16, 8, 4, 2, 1]
AH = 8
KVH = 2
GRP = 4
DH = 64
BAND = 192
DIFFS = 320
NG = 4
EPG = 8
DE = 512
BLK = 64
NE = 32
MAX_BLOCKS = 2 * T // BLK + NE
MAX_EXPERT = T // BLK
ALPHA = 2.0 ** 0.25
EPS = 1e-5
NEG = -1.0e30
SLOT = 4096
OUTS = [((1, 1024, 1024), "float32")]


def block_kernel(nc, x, c, w_in, b_in_row, b_in_cols, w_out, hg_lower_cols, hg_norm, attn_sinks, rel_bias,
                 ada_w, ada_b, ln1_g, ln1_b, ln2_g, ln2_b, w_group, b_group, w_sub, b_sub, w1, w3, w2,
                 c_f32, c_masks, c_onehot, out):
    f32, i32, u32, u8 = mybir.dt.float32, mybir.dt.int32, mybir.dt.uint32, mybir.dt.uint8
    ALU, ACT, AX = mybir.AluOpType, mybir.ActivationFunctionType, mybir.AxisListType
    ctx = ExitStack()
    with ctx:
        def sb(name, shape, dt=f32):
            return ctx.enter_context(nc.sbuf_tensor(name, shape, dt))

        def sem(name):
            return ctx.enter_context(nc.semaphore(name))

        ring = sb("ring", [P, 6 * SLOT])
        hx = sb("hx", [P, NT * D])
        area = sb("area", [P, 17792])
        cf = sb("cf", [P, 2 * P + MAX_BLOCKS + MAX_EXPERT + NT])
        masks = sb("masks", [P, 7 * P], u8)
        ones = sb("ones", [P, P])
        mean = sb("mean", [P, P])
        keep = sb("keep", [P, HALF], mybir.dt.bfloat16)
        modc = sb("modc", [P, 6, KD])
        adac = sb("adac", [P, 6, KD])
        cond = sb("cond", [P, KD])
        small = sb("small", [P, 1024])

        def slot(s):
            return ring[:, s * SLOT:(s + 1) * SLOT]

        mixT = ring[:, 4 * SLOT:6 * SLOT].rearrange("p (m t) -> p m t", m=8)
        hT = hx[:, :].rearrange("p (k t) -> p k t", k=KD)
        x2 = hx[:, :].rearrange("p (t d) -> p t d", t=NT)
        ident, tri = cf[:, 0:128], cf[:, 128:256]
        iota = cf[:, 2 * P:2 * P + MAX_BLOCKS]
        thresholds = cf[:, 2 * P + MAX_BLOCKS:2 * P + MAX_BLOCKS + MAX_EXPERT]
        token_id = cf[:, 2 * P + MAX_BLOCKS + MAX_EXPERT:]

        cut = [0]

        def part(n):
            cut[0] += n
            assert cut[0] <= 17792, cut[0]
            return area[:, cut[0] - n:cut[0]]

        vtok = part(NT * 640).rearrange("p (t v) -> p t v", t=NT)
        kT = part(T)
        bias = part(AH * BAND).rearrange("p (h k) -> p h k", h=AH)
        sa_all = [part(64 + GRP * BAND) for _ in range(2)]
        ptp = part(GRP * CHUNK)
        pto = part(GRP * P)
        hg0 = cut[0]
        sg, fbuf, bcum, kbuf, score, qdec, kdec = (part(HALF) for _ in range(7))
        qbuf = [part(HALF) for _ in range(2)]
        ebuf = [part(HALF) for _ in range(2)]
        xbuf = [part(HALF) for _ in range(2)]
        state = part(8 * P).rearrange("p (c v) -> p c v", c=8)
        kdT, sq, rms = sa_all[0][:, 0:HALF], sa_all[1][:, 0:HALF], pto
        cut[0] = hg0
        xin = [part(D) for _ in range(2)]
        xn = [part(D) for _ in range(2)]
        acc = [part(HALF) for _ in range(2)]
        adarow = part(2048)
        trep = area[:, 0:AH * DIFFS].rearrange("p (h m) -> p h m", h=AH)
        wide_masks = area[:, 3072:3072 + 7 * P].bitcast(i32)
        relb = kT
        hirow = part(HALF)
        onehot = sa_all[1][:, 0:DIFFS]
        rowbuf = pto
        cut[0] = 0
        gt1 = part(D)
        g1, b1 = part(D), part(D)
        xr = [part(D) for _ in range(2)]
        rbuf = [part(D) for _ in range(2)]
        h2T = [part(D) for _ in range(2)]
        wr = part(KD * 36).rearrange("p (k n) -> p k n", k=KD)
        br = part(36)
        lg = part(NT * 36).rearrange("p (t n) -> p t n", t=NT)
        oh = part(2 * NT * NE).rearrange("p (c t e) -> p c t e", c=2, t=NT)
        ohsum = part(NT * NE).rearrange("p (t e) -> p t e", t=NT)
        before = part(9 * NE).rearrange("p (t e) -> p t e", t=9)
        pos = part(NT * NE).rearrange("p (t e) -> p t e", t=NT)
        prod = part(2 * NT * NE)
        counted = part(NE * MAX_EXPERT).rearrange("p (e m) -> p e m", e=NE)
        blkcmp = part(MAX_BLOCKS * NE).rearrange("p (b e) -> p b e", b=MAX_BLOCKS)
        row_oh = part(2 * NT * BLK).rearrange("p (n r) -> p n r", r=BLK)
        blk_oh = part(2 * NT * MAX_BLOCKS).rearrange("p (n j) -> p n j", j=MAX_BLOCKS)
        cnt, nblk, bend, bstart, cend, shift, padding = (part(NE) for _ in range(7))
        row0f = part(MAX_BLOCKS)
        cut[0] = 0
        xg, xT, sl, hid, hidT, yo, gt2 = part(D), part(HALF), part(DE), part(DE), part(2 * P), part(HALF), part(HALF)
        g2, b2 = part(D), part(D)
        ya = [ring[:, t * D:(t + 1) * D] for t in range(NT)]
        yb = [ring[:, (NT + t) * D:(NT + t + 1) * D] for t in range(NT)]

        at = [0]

        def bit(*shape):
            n = int(np.prod(shape))
            at[0] += n
            assert at[0] <= 1024
            v = small[:, at[0] - n:at[0]]
            if len(shape) == 2:
                v = v.rearrange("p (a b) -> p a b", a=shape[0])
            return v

        stats = bit(2, 12)
        mv = bit(2, 2)
        rstd = bit(2, 1)
        lowc = bit(2, HEADS)
        lowd = bit(HEADS)
        lb, oml = bit(HEADS), bit(HEADS)
        bcols = bit(22)
        nbcols = bit(22)
        norm, eps = bit(1), bit(1)
        rel_src = bit(AH)
        carry = bit(P)
        sink = bit(AH)
        mx = bit(2, GRP)
        sums, esink, rden = bit(2, GRP), bit(2, GRP), bit(2, GRP)
        eblast = bit(8)
        ecols = bit(2, KD)
        gmax, emax = bit(NT, 8), bit(NT, 8)
        gpad, e8 = bit(NT, 8), bit(NT, 8)
        gsel = bit(NT)
        oh4 = bit(NT, NG)
        gexp = bit(NT, NG)
        psel, ex, den, wa, wb = bit(NT), bit(NT), bit(NT), bit(NT), bit(NT)
        eid = bit(2, NT)
        eidx = bit(2, NT)
        slotf = bit(2, NT)
        rowf, blkf = bit(2, NT), bit(2, NT)
        nmr = bit(2, 1)
        gidx = sb("gidx", [P, NT, 8], u32)
        eix = sb("eix", [P, NT, 8], u32)
        sloti = sb("sloti", [P, 2, NT], i32)
        bitsi = sb("bitsi", [P, 2, NT], i32)
        yrowi = sb("yrowi", [P, 2, NT], i32)
        nblki = sb("nblki", [P, NE], i32)
        bendi = sb("bendi", [P, NE], i32)
        row0i = sb("row0i", [P, MAX_BLOCKS], i32)
        slot_tok = sb("slot_tok", [P, MAX_BLOCKS + 2], i32)
        pick = sb("pick", [P, 1], i32)

        ps = ctx.enter_context(nc.psum_tensor("ps", [P, 8 * 512], f32))

        def bank(b, n=1):
            return ps[:, b * 512:(b + n) * 512]

        diffs_d = nc.dram_tensor("diffs_d", [P, AH, DIFFS], f32).ap()
        gates_d = nc.dram_tensor("gates_d", [2, D], f32).ap()
        n2_d = nc.dram_tensor("n2_d", [T, D], f32).ap()
        y_d = nc.dram_tensor("y_d", [2 * T + BLK, D], f32).ap()

        piece_in = [sem(f"piece_in{s}") for s in range(5)]
        consts_in, cols_in, rows_in, x_in = sem("consts_in"), sem("cols_in"), sem("rows_in"), [sem("x_in0"), sem("x_in1")]
        set_up, filled = sem("set_up"), sem("filled")
        cond_e, cond_ready = sem("cond_e"), sem("cond_ready")
        xn_ready, xt_done, xt_evac = sem("xn_ready"), sem("xt_done"), sem("xt_evac")
        ada_summed, mod_done, mod_read, row_out = sem("ada_summed"), sem("mod_done"), sem("mod_read"), sem("row_out")
        lowexp = sem("lowexp")
        rel_rows, trep_done, trep_read, diffs_out, bias_in, bias_ready = (
            sem("rel_rows"), sem("trep_done"), sem("trep_read"), sem("diffs_out"), sem("bias_in"), sem("bias_ready"))
        v_done, v_evac = sem("v_done"), sem("v_evac")
        z_done, z_act, z_dve, z_sig, q_dec = (sem(n) for n in ("z_done", "z_act", "z_dve", "z_sig", "q_dec"))
        var_ready, rstd_ready, rms_ready = sem("var_ready"), sem("rstd_ready"), sem("rms_ready")
        o_scaled = sem("o_scaled")
        h_ready, xv_evac = sem("h_ready"), sem("xv_evac")
        row_ready, sa_clear = sem("row_ready"), sem("sa_clear")
        s_done, s_shift, p_exp, p_ready, pt_done, pt_evac, o_done, o_evac, sa_read = (sem(n) for n in (
            "s_done", "s_shift", "p_exp", "p_ready", "pt_done", "pt_evac", "o_done", "o_evac", "sa_read"))
        f_ready, lf_ready, scanned, e_in, e_out, x_ready, gram_done, gram_read = (sem(n) for n in (
            "f_ready", "lf_ready", "scanned", "e_in", "e_out", "x_ready", "gram_done", "gram_read"))
        dec_out, kd_in, kd_out, kd_ready, kdt_done, kdt_evac, u_done, st_ready, ho_done, sq_ready, ms_done, head_out = (
            sem(n) for n in ("dec_out", "kd_in", "kd_out", "kd_ready", "kdt_done", "kdt_evac", "u_done", "st_ready",
                             "ho_done", "sq_ready", "ms_done", "head_out"))
        mix_done, mix_read, xr_in, r_in, n2_ready, n2_out, t2_done, t2_evac, rt_done, rt_read = (
            sem("mix_done"), sem("mix_read"), [sem("xr_in0"), sem("xr_in1")], sem("r_in"), sem("n2_ready"),
            [sem("n2_out0"), sem("n2_out1")], sem("t2_done"), sem("t2_evac"), sem("rt_done"), sem("rt_read"))
        rexp_in, rexp_out, onehots, ranked, slots_ready, table_done, table_ready, plan_ready, rows_ready = (sem(n) for n in (
            "rexp_in", "rexp_out", "onehots", "ranked", "slots_ready", "table_done", "table_ready", "plan_ready", "rows_ready"))
        w1_in, w3_in, w2_in = ([sem(f"{n}_in{b}") for b in range(2)] for n in ("w1", "w3", "w2"))
        pick_ready = sem("pick_ready")
        xg_in, xg_t, xT_evac = sem("xg_in"), sem("xg_t"), sem("xT_evac")
        gu_done = [sem("gu_done0"), sem("gu_done1")]
        hid_ready, ht_evac = [sem("hid_ready0"), sem("hid_ready1")], [sem("ht_evac0"), sem("ht_evac1")]
        silu_out, ht_done, y_done, y_scaled, y_out = (sem(n) for n in ("silu_out", "ht_done", "y_done", "y_scaled", "y_out"))
        blocks_out, ys_in = sem("blocks_out"), [sem(f"ys_in{t}") for t in range(NT)]
        fin_rows, x2_scaled = sem("fin_rows"), sem("x2_scaled")
        nmr_ready, applied, gained, fin_ready, fin_out = (sem(n) for n in ("nmr_ready", "applied", "gained", "fin_ready", "fin_out"))
        v_chain, a_chain, p_chain = sem("v_chain"), sem("a_chain"), sem("p_chain")

        held = {0: ["ada0", "kv", "hf", "wo1"], 1: ["ada1", "aq", "hq"], 2: ["ada2", "hi", "hg"],
                3: ["ada3", "ada4", "ada6", "ada8", "ada10", "wo0"], 4: ["ada5", "ada7", "ada9", "ada11"]}
        place = {n: (s, i + 1) for s, names in held.items() for i, n in enumerate(names)}
        W_COL = {"hq": 0, "hf": 512, "hi": 1024, "hg": 1536, "aq": 2048, "kv": 2560}
        Z0 = 10
        Z_ALL = Z0 + 3 * UNITS

        W1, W3, W2 = (1, 3), (2, 4), (0, 5)

        def arrived(eng, name):
            s, n = place[name]
            eng.wait_ge(piece_in[s], 16 * n)

        def view(name, n=512):
            return slot(place[name][0])[:, 0:KD * n].rearrange("p (k f) -> p k f", k=KD)

        w_in_v = w_in[0].rearrange("(p k) n -> p k n", p=P)
        ada_v = ada_w[0].rearrange("(p k) n -> p k n", p=P)

        block = ctx.enter_context(nc.Block())

        @block.sync
        def _(sp):
            def load(name, src, dst):
                s, n = place[name]
                sp.dma_start(dst, src).then_inc(piece_in[s], 16)

            def load_ada(n):
                load(f"ada{n}", ada_v[:, :, n * 512:(n + 1) * 512], view(f"ada{n}"))

            def load_z(name, n=512):
                load(name, w_in_v[:, :, W_COL[name]:W_COL[name] + n], view(name, n))

            for n in range(4):
                load_ada(n)
            sp.wait_ge(ada_summed, 1)
            load_z("kv", 256)
            sp.wait_ge(ada_summed, 2)
            load_z("aq")
            sp.wait_ge(ada_summed, 3)
            load_z("hi")
            sp.wait_ge(ada_summed, 4)
            load_ada(4)
            load_ada(5)
            for n in range(6, 12):
                sp.wait_ge(ada_summed, n - 1)
                load_ada(n)
            sp.wait_ge(z_done, Z0)
            load_z("hq")
            sp.wait_ge(v_done, NT)
            load_z("hf")
            load_z("hg")
            sp.wait_ge(ada_summed, 11)
            load("wo0", w_out[0, 0:512, :].rearrange("(m p) n -> p m n", p=P), slot(3).rearrange("p (m n) -> p m n", m=4))
            sp.wait_ge(z_done, Z_ALL - 2)
            wo1 = slot(0).rearrange("p (m n) -> p m n", m=4)
            for g in range(KVH):
                rows = w_out[0, 512 + g * 256:768 + g * 256, :].rearrange("(j p) n -> p j n", p=DH)
                sp.dma_start(wo1[g * DH:(g + 1) * DH, :, :], rows).then_inc(piece_in[0], 16)

            def load_gate_up(b, e):
                sp.dma_start(slot(W1[b]), w1[0][e].rearrange("o (p k) f -> (o p) (k f)", p=P)).then_inc(w1_in[b], 16)
                sp.dma_start(slot(W3[b]), w3[0][e].rearrange("o (p k) f -> (o p) (k f)", p=P)).then_inc(w3_in[b], 16)

            def load_down(b, e):
                sp.dma_start(slot(W2[b]).rearrange("p (k f) -> p k f", k=4),
                             w2[0][e].rearrange("o (k p) f -> (o p) k f", p=P)).then_inc(w2_in[b], 16)

            sp.wait_ge(z_done, Z_ALL)
            load_gate_up(0, slice(0, 1))
            sp.wait_ge(mix_done, NT)
            load_down(0, slice(0, 1))
            load_gate_up(1, slice(1, 2))
            load_down(1, slice(1, 2))
            sp.wait_ge(plan_ready, 1)
            with sp.Fori(1, NE // 2) as i:
                for b in range(2):
                    e = i * 2 + b
                    last = sp.value_load(bendi[0:1, bass.ds(e - 2, 1)], min_val=1, max_val=MAX_BLOCKS)
                    sp.wait_ge(gu_done[1], last)
                    load_gate_up(b, bass.ds(e, 1))
                    sp.wait_ge(y_done, last)
                    load_down(b, bass.ds(e, 1))

        @block.gpsimd
        def _(pool):
            nc.gpsimd.memset(ones[:], 1.0).then_inc(set_up, 1)
            nc.gpsimd.memset(keep[:], 1.0).then_inc(filled, 1)
            nc.gpsimd.memset(slot_tok[:, MAX_BLOCKS:], 0).then_inc(set_up, 1)
            nc.gpsimd.memset(eps, EPS)
            nc.gpsimd.memset(mean[:], 1.0 / P).then_inc(set_up, 1)
            pool.wait_ge(filled, 1)
            nc.gpsimd.memset(keep[:].rearrange("p (c s) -> p c s", s=CHUNK)[:, :, 0:1], 0.0).then_inc(set_up, 1)
            pool.wait_ge(set_up, 4)
            pool.wait_ge(trep_read, AH)
            pool.dma_start(diffs_d, trep).then_inc(diffs_out, 16)
            pool.wait_ge(diffs_out, 16)
            skewed = bass.AP(tensor=diffs_d.tensor, offset=P - 1, ap=[[AH * DIFFS - 1, P], [DIFFS, AH], [1, BAND]])
            pool.dma_start(bias, skewed).then_inc(bias_in, 16)
            for r in range(4):
                pool.wait_ge(row_ready, r + 1)
                pool.dma_start(gates_d[r // 2:r // 2 + 1, (r % 2) * 512:(r % 2 + 1) * 512], rowbuf[0:1, :]).then_inc(row_out, 16)
            for b in range(2):
                pool.wait_ge(n2_out[b], 16 * NT // 2)

            def gather():
                nc.gpsimd.indirect_dma_start(
                    out=xg[0:BLK, :], out_offset=None, in_=n2_d,
                    in_offset=bass.IndirectOffsetOnAxis(ap=pick[0:BLK, 0:1], axis=0)).then_inc(xg_in, 16)

            pool.wait_ge(plan_ready, 1)
            total = pool.value_load(bendi[0:1, NE - 1:NE], min_val=1, max_val=MAX_BLOCKS)
            picks = pool.alloc_register("picks")
            pool.reg_mov(picks, 2)
            pool.wait_ge(table_ready, 1)
            nc.gpsimd.tensor_copy(pick[0:BLK], slot_tok[0:BLK, 0:1]).then_inc(pick_ready, 1)
            pool.wait_ge(pick_ready, 1)
            gather()
            with pool.Fori(0, total) as j:
                pool.wait_ge(xg_t, j + 1)
                nc.gpsimd.tensor_copy(pick[0:BLK], slot_tok[0:BLK, bass.ds(j + 1, 1)]).then_inc(pick_ready, 1)
                pool.wait_ge(pick_ready, picks)
                pool.reg_add(picks, picks, 1)
                gather()

            pool.wait_ge(blocks_out, 1)
            for t in range(NT):
                for ch, buf in enumerate((ya, yb)):
                    nc.gpsimd.indirect_dma_start(
                        out=buf[t], out_offset=None, in_=y_d,
                        in_offset=bass.IndirectOffsetOnAxis(ap=yrowi[:, ch, t:t + 1], axis=0)).then_inc(ys_in[t], 16)
            for t in range(NT):
                pool.wait_ge(gained, t + 1)
                nc.gpsimd.tensor_tensor(ya[t], ya[t], b2, ALU.add).then_inc(fin_ready, 1)

        @block.scalar
        def _(act):
            n_link = [0]

            def link(ins):
                n_link[0] += 1
                ins.then_inc(a_chain, 1)
                act.wait_ge(a_chain, n_link[0])

            n_norm = [0]

            def root(s):
                n_norm[0] += 1
                act.wait_ge(var_ready, n_norm[0])
                link(nc.scalar.activation(rstd[:, s, :], mv[:, s, 1:2], ACT.Ln, bias=eps))
                nc.scalar.activation(rstd[:, s, :], rstd[:, s, :], ACT.Exp, scale=-0.5).then_inc(rstd_ready, 1)

            def evac_x(t):
                act.wait_ge(xt_done, t + 1)
                nc.scalar.activation(hT[:, 0:4, t * P:(t + 1) * P],
                                     bank(4 + 2 * (t % 2)).rearrange("p (k t) -> p k t", k=4), ACT.Copy).then_inc(xt_evac, 1)

            def sigmoid(z, col, dst, sem_out):
                act.wait_ge(z_done, z + 1)
                nc.scalar.activation(dst, bank(z % 2), ACT.Exp, bias=nbcols[:, col:col + 1], scale=-1.0).then_inc(z_act, 1)
                act.wait_ge(z_act, z + 1)
                link(nc.scalar.activation(dst, dst, ACT.Ln, bias=ones[:, 0:1]))
                nc.scalar.activation(dst, dst, ACT.Exp, scale=-1.0).then_inc(sem_out, 1)

            nc.scalar.preload_act_table_set("natural_log_exp_and_others")
            act.dma_start(cond[:], c.rearrange("o (p k) -> (o p) k", p=P)).then_inc(cols_in, 16)
            for t in range(2):
                act.dma_start(xin[t], x[0, t * P:(t + 1) * P, :]).then_inc(x_in[t], 16)
            act.dma_start(cf[:], c_f32).then_inc(consts_in, 16)
            act.dma_start(wide_masks, c_masks).then_inc(consts_in, 16)
            act.dma_start(onehot[0:32, :], c_onehot).then_inc(consts_in, 16)
            for kind in (0, 1, 3, 4):
                act.dma_start(adac[:, kind, :], ada_b[0, kind * D:(kind + 1) * D].rearrange("(p k) -> p k", p=P)).then_inc(cols_in, 16)
            act.dma_start(bcols, b_in_cols).then_inc(cols_in, 16)
            act.dma_start(lowc, hg_lower_cols.rearrange("p (r h) -> p r h", r=2)).then_inc(cols_in, 16)
            act.dma_start(norm, hg_norm[0].rearrange("(p o) -> p o", o=1)).then_inc(cols_in, 16)
            act.dma_start(sink, attn_sinks.broadcast_to([P, AH])).then_inc(rows_in, 16)
            act.dma_start(hirow, b_in_row[:, 0:HALF].broadcast_to([P, HALF])).then_inc(rows_in, 16)
            act.dma_start(carry, b_in_row[:, HALF:640].broadcast_to([P, P])).then_inc(rows_in, 16)
            act.dma_start(rel_src[0:32], rel_bias).then_inc(rows_in, 16)
            for i, kind in enumerate((2, 5)):
                act.dma_start(adarow[0:1, i * D:(i + 1) * D], ada_b[0:1, kind * D:(kind + 1) * D]).then_inc(rows_in, 16)
            act.wait_ge(cols_in, 16 * 8)
            act.wait_ge(set_up, 4)
            root(0)
            root(1)
            link(nc.scalar.activation(ecols[:, 0, :], cond[:], ACT.Exp, scale=-1.0))
            link(nc.scalar.activation(ecols[:, 0, :], ecols[:, 0, :], ACT.Ln, bias=ones[:, 0:1]))
            nc.scalar.activation(ecols[:, 0, :], ecols[:, 0, :], ACT.Exp, scale=-1.0).then_inc(cond_e, 1)
            act.wait_ge(lowexp, 1)
            nc.scalar.activation(lowc, lowc, ACT.Exp).then_inc(lowexp, 1)
            for t in range(2, NT + 2):
                if t >= 4:
                    root(t % 2)
                evac_x(t - 2)
                if t < NT:
                    act.wait_ge(xn_ready, t - 1)
                    act.dma_start(xin[t % 2], x[0, t * P:(t + 1) * P, :]).then_inc(x_in[t % 2], 16)
            act.wait_ge(mod_read, 1)
            act.wait_ge(xt_evac, NT)
            for k in range(4):
                last = nc.scalar.activation(hT[:, k, :], hT[:, k, :], ACT.Identity, bias=modc[:, 0, k:k + 1], scale=modc[:, 1, k:k + 1])
            last.then_inc(h_ready, 1)
            for z in range(Z0):
                act.wait_ge(z_done, z + 1)
                half = z % 2
                dst = kT[:, half * HALF:(half + 1) * HALF] if z < 2 else mixT[:, 4 + (z - 2) // 2, half * HALF:(half + 1) * HALF]
                col = 20 if z < 2 else 16 + (z - 2) // 2
                nc.scalar.activation(dst, bank(z % 2), ACT.Identity, bias=bcols[:, col:col + 1]).then_inc(z_act, 1)

            def attn_exp(n):
                act.wait_ge(s_shift, n + 1)
                lo = CHUNK if n < 2 else 0
                v = sa_all[n % 2][:, 64:].rearrange("p (h k) -> p h k", h=GRP)[:, :, lo:]
                nc.scalar.activation(v, v, ACT.Exp)
                nc.scalar.activation(esink[:, n % 2, :], esink[:, n % 2, :], ACT.Exp).then_inc(p_exp, 1)

            def attn_evac(n):
                i, g = n // 2, n % 2
                act.wait_ge(pt_done, n + 1)
                last = nc.scalar.activation(pto, bank(4), ACT.Copy)
                if i:
                    last = nc.scalar.activation(ptp[CHUNK:P, :], bank(5)[CHUNK:P, 0:GRP * CHUNK], ACT.Copy)
                last.then_inc(pt_evac, 1)

            def attn_out(n):
                i, g = n // 2, n % 2
                act.wait_ge(o_done, n + 1)
                nc.scalar.activation(mixT[g * DH:(g + 1) * DH, 4:8, i * P:(i + 1) * P],
                                     bank(4)[g * DH:(g + 1) * DH, :].rearrange("p (j t) -> p j t", j=GRP),
                                     ACT.Copy).then_inc(o_evac, 1)

            def exp_level(u, lv):
                act.wait_ge(e_in, 6 * u + lv + 1)
                nc.scalar.activation(ebuf[lv % 2], ebuf[lv % 2], ACT.Exp).then_inc(e_out, 1)

            def gate_z(n):
                period, which = n // 3, n % 3
                h, half = period // 2, period % 2
                dst = (sg, qbuf[period % 2], mixT[:, h, half * HALF:(half + 1) * HALF])[which]
                if which == 0 and period:
                    act.wait_ge(f_ready, period)
                if which == 1 and period >= 2:
                    act.wait_ge(gram_read, 7 * (period - 1))
                sigmoid(Z0 + n, (4, 0, 12)[which] + h, dst, z_sig)

            act.wait_ge(row_out, 16 * 4)
            for n in range(16):
                attn_exp(n)
                if n >= 2:
                    attn_evac(n - 2)
                    attn_out(n - 2)
            for n in (14, 15):
                attn_evac(n)
                attn_out(n)

            def rms_root(u):
                act.wait_ge(ms_done, u + 1)
                link(nc.scalar.activation(rms, bank(7), ACT.Ln, bias=eps))
                nc.scalar.activation(rms, rms, ACT.Exp, scale=-0.5).then_inc(rms_ready, 1)

            for period in range(UNITS + 1):
                u = period - 1
                for part3 in range(3):
                    n = 3 * period + part3
                    if 1 <= n <= 3 * UNITS:
                        gate_z(n - 1)
                    if u < 0:
                        continue
                    if part3 == 0:
                        act.wait_ge(f_ready, u + 1)
                        nc.scalar.activation(ebuf[1], fbuf, ACT.Ln).then_inc(lf_ready, 1)
                        act.wait_ge(scanned, u + 1)
                        if u:
                            act.wait_ge(ho_done, u)
                            act.wait_ge(st_ready, u)
                        nc.scalar.activation(qdec, bcum, ACT.Exp)
                        nc.scalar.activation(eblast, bcum.rearrange("p (c s) -> p c s", s=CHUNK)[:, :, CHUNK - 1:CHUNK].rearrange("p c o -> p (c o)"),
                                             ACT.Exp).then_inc(dec_out, 1)
                        exp_level(u, 0)
                        act.wait_ge(kd_in, u + 1)
                        nc.scalar.activation(kdec, kdec, ACT.Exp).then_inc(kd_out, 1)
                        exp_level(u, 1)
                        if u:
                            rms_root(u - 1)
                        for lv in (2, 3):
                            exp_level(u, lv)
                        act.wait_ge(kdt_done, u + 1)
                        nc.scalar.activation(kdT, bank(2), ACT.Copy).then_inc(kdt_evac, 1)
                    elif part3 == 1:
                        for lv in (4, 5):
                            exp_level(u, lv)
                    else:
                        act.wait_ge(ho_done, u + 1)
                        nc.scalar.activation(sq, bank(6), ACT.Square).then_inc(sq_ready, 1)
            rms_root(UNITS - 1)

            act.wait_ge(head_out, UNITS)
            act.wait_ge(row_out, 16 * 4)
            for dst, src in ((gt1, gates_d[0:1, :]), (g1, ln1_g), (b1, ln1_b)):
                act.dma_start(dst, src.broadcast_to([P, D])).then_inc(r_in, 16)
            for t in range(2):
                act.dma_start(xr[t], x[0, t * P:(t + 1) * P, :]).then_inc(xr_in[t], 16)
            act.dma_start(wr[:, :, 0:NG], w_group[0].rearrange("(p k) n -> p k n", p=P)).then_inc(r_in, 16)
            act.dma_start(wr[:, :, NG:36], w_sub[0].rearrange("(p k) n -> p k n", p=P)).then_inc(r_in, 16)
            act.dma_start(br[:, 0:NG], b_group.broadcast_to([P, NG])).then_inc(r_in, 16)
            act.dma_start(br[:, NG:36], b_sub.broadcast_to([P, NE])).then_inc(r_in, 16)
            for t in range(NT):
                root(0)
                root(1)
                act.wait_ge(n2_ready, t + 1)
                nc.scalar.activation(x2[:, t, :], x2[:, t, :], ACT.Copy, scale=ALPHA).then_inc(x2_scaled, 1)
                act.dma_start(n2_d[t * P:(t + 1) * P, :], rbuf[t % 2]).then_inc(n2_out[t % 2], 16)
                if t + 2 < NT:
                    act.dma_start(xr[t % 2], x[0, (t + 2) * P:(t + 3) * P, :]).then_inc(xr_in[t % 2], 16)
                act.wait_ge(t2_done, t + 1)
                if t >= 2:
                    act.wait_ge(rt_done, t - 1)
                for k in range(KD):
                    last = nc.scalar.activation(h2T[t % 2][:, k * P:(k + 1) * P], bank(4, 2)[:, k * P:(k + 1) * P],
                                                ACT.Identity, bias=modc[:, 3, k:k + 1], scale=modc[:, 4, k:k + 1])
                last.then_inc(t2_evac, 1)
            act.wait_ge(rexp_in, 1)
            nc.scalar.activation(gexp, gexp, ACT.Exp).then_inc(rexp_out, 1)
            act.wait_ge(rexp_in, 2)
            nc.scalar.activation(ex, ex, ACT.Exp).then_inc(rexp_out, 1)

            for dst, src in ((g2, ln2_g), (b2, ln2_b)):
                act.dma_start(dst, src.broadcast_to([P, D])).then_inc(fin_rows, 16)
            for half in range(2):
                act.dma_start(gt2[half * BLK:(half + 1) * BLK, :],
                              gates_d[1:2, half * HALF:(half + 1) * HALF].broadcast_to([BLK, HALF])).then_inc(fin_rows, 16)
            act.wait_ge(fin_rows, 16 * 4)
            act.dma_start(y_d[2 * T:2 * T + BLK, :].rearrange("r (h c) -> (r h) c", h=2), gt2).then_inc(y_out, 16)

            def evac_block(count):
                act.wait_ge(xg_t, count)
                for k in range(KD):
                    last = nc.scalar.activation(xT[:, k * BLK:(k + 1) * BLK], bank(0)[:, k * BLK:(k + 1) * BLK],
                                                ACT.Identity, bias=modc[:, 3, k:k + 1], scale=modc[:, 4, k:k + 1])
                last.then_inc(xT_evac, 1)

            nc.scalar.preload_act_table(ACT.Silu)
            evac_block(1)
            act.wait_ge(rows_ready, 1)
            total = act.value_load(bendi[0:1, NE - 1:NE], min_val=1, max_val=MAX_BLOCKS)
            with act.Fori(0, total) as j:
                row = act.value_load(row0i[0:1, bass.ds(j, 1)], min_val=0, max_val=2 * T)
                for half in range(2):
                    f = slice(half * 2 * P, (half + 1) * 2 * P)
                    act.wait_ge(gu_done[half], j + 1)
                    nc.scalar.activation(sl[BLK:P, f], bank(2 + half)[0:BLK, 0:2 * P], ACT.Silu).then_inc(silu_out, 1)
                evac_block(j + 2)
                act.wait_ge(y_scaled, j + 2)
                for half in range(2):
                    act.dma_start(y_d[bass.ds(row, BLK), half * HALF:(half + 1) * HALF],
                                  yo[half * BLK:(half + 1) * BLK, :]).then_inc(y_out, 16)
            nc.scalar.preload_act_table_set("natural_log_exp_and_others")
            for t in range(NT + 1):
                if t < NT:
                    root(t % 2)
                if t:
                    act.wait_ge(nmr_ready, t)
                    nc.scalar.activation(ya[t - 1], ya[t - 1], ACT.Identity, bias=nmr[:, (t - 1) % 2, :],
                                         scale=rstd[:, (t - 1) % 2, :]).then_inc(applied, 1)
            for t in range(NT):
                act.wait_ge(fin_ready, t + 1)
                act.dma_start(out[0, t * P:(t + 1) * P, :], ya[t]).then_inc(fin_out, 16)
            act.wait_ge(fin_out, 16 * NT)

        @block.vector
        def _(dve):
            n_link = [0]

            def link(ins):
                n_link[0] += 1
                ins.then_inc(v_chain, 1)
                dve.wait_ge(v_chain, n_link[0])

            V = nc.vector
            n_norm = [0]

            def normalise(src, dst, s, done=None):
                V.bn_stats(stats[:, s, 0:6], src[:, 0:512])
                link(V.bn_stats(stats[:, s, 6:12], src[:, 512:1024]))
                V.bn_aggr(mv[:, s, :], stats[:, s, :]).then_inc(var_ready, 1)
                n_norm[0] += 1
                dve.wait_ge(var_ready, n_norm[0])
                dve.wait_ge(rstd_ready, n_norm[0])
                ins = V.tensor_scalar(dst, src, mv[:, s, 0:1], rstd[:, s, :], ALU.subtract, ALU.mult)
                if done is None:
                    link(ins)
                else:
                    ins.then_inc(done, 1)

            def layer_norm1(t):
                dve.wait_ge(x_in[t % 2], 16 * (t // 2 + 1))
                if t >= 2:
                    dve.wait_ge(xt_done, t - 1)
                normalise(xin[t % 2], xn[t % 2], t % 2, xn_ready)

            def ada_sum(n):
                arrived(dve, f"ada{n}")
                if n >= 2:
                    dve.wait_ge(mod_done, n - 1)
                a, w = acc[n % 2], view(f"ada{n}")
                link(V.tensor_scalar(a, w[:, 0, :], cond[:, 0:1], None, ALU.mult))
                for k in range(1, KD):
                    ins = V.scalar_tensor_tensor(a, w[:, k, :], cond[:, k:k + 1], a, ALU.mult, ALU.add)
                    if k < KD - 1:
                        link(ins)
                ins.then_inc(ada_summed, 1)

            def take_row(r):
                dve.wait_ge(mod_done, (5, 6, 11, 12)[r])
                if r:
                    dve.wait_ge(row_out, 16 * r)
                V.tensor_copy(rowbuf, bank(3)).then_inc(row_ready, 1)

            def evac_x(t):
                dve.wait_ge(xt_done, t + 1)
                V.tensor_copy(hT[:, 4:8, t * P:(t + 1) * P], bank(5 + 2 * (t % 2)).rearrange("p (k t) -> p k t", k=4)).then_inc(xv_evac, 1)

            layer_norm1(0)
            layer_norm1(1)
            dve.wait_ge(cols_in, 16 * 8)
            dve.wait_ge(cond_e, 1)
            link(V.tensor_tensor(cond[:], cond[:], ecols[:, 0, :], ALU.mult))
            link(V.tensor_tensor(lowd, lowc[:, 0, :], lowc[:, 1, :], ALU.max))
            V.tensor_tensor(lowc, lowc, lowd[:, None, :].broadcast_to([P, 2, HEADS]), ALU.subtract).then_inc(lowexp, 1)
            dve.wait_ge(lowexp, 2)
            link(V.tensor_tensor(lowd, lowc[:, 0, :], lowc[:, 1, :], ALU.add))
            link(V.reciprocal(lowd, lowd))
            link(V.tensor_tensor(lb, lowc[:, 0, :], lowd, ALU.mult))
            link(V.tensor_scalar(oml, lb, -1.0, 1.0, ALU.mult, ALU.add))
            link(V.tensor_scalar(nbcols, bcols, -1.0, None, ALU.mult))
            evac_x(0)
            layer_norm1(2)
            evac_x(1)
            layer_norm1(3)
            for n in range(4):
                ada_sum(n)
                evac_x(n + 2)
                if n + 4 < NT:
                    layer_norm1(n + 4)
            dve.wait_ge(mod_done, 4)
            V.scalar_tensor_tensor(modc[:, 0, :], bank(2)[:, 0:KD], 0.0, adac[:, 0, :], ALU.add, ALU.add)
            V.scalar_tensor_tensor(modc[:, 1, :], bank(2)[:, KD:2 * KD], 1.0, adac[:, 1, :], ALU.add, ALU.add).then_inc(mod_read, 1)
            dve.wait_ge(mod_read, 1)
            evac_x(NT - 2)
            evac_x(NT - 1)
            dve.wait_ge(xv_evac, NT)
            for k in range(4, KD):
                ins = V.tensor_scalar(hT[:, k, :], hT[:, k, :], modc[:, 1, k:k + 1], modc[:, 0, k:k + 1], ALU.mult, ALU.add)
            ins.then_inc(h_ready, 1)
            dve.wait_ge(rows_in, 16 * 6)
            dve.wait_ge(consts_in, 16 * 3)
            V.tensor_copy(masks[:], wide_masks)
            V.tensor_copy(relb[0:32, :].rearrange("b (h m) -> b h m", h=AH),
                          rel_src[0:32, :, None].broadcast_to([32, AH, P])).then_inc(rel_rows, 1)
            for h in range(AH):
                dve.wait_ge(trep_done, h + 1)
                V.tensor_copy(trep[:, h, :], bank(h % 2)[:, 0:DIFFS]).then_inc(trep_read, 1)
            dve.wait_ge(bias_in, 16)
            V.memset(bias[0:CHUNK, :, P:BAND], NEG)
            V.memset(bias[CHUNK:P, :, 0:CHUNK], NEG).then_inc(bias_ready, 1)
            row = 0
            for n in range(4, 12):
                ada_sum(n)
                if n in (4, 5, 10, 11):
                    take_row(row)
                    row += 1
            V.memset(sa_all[0][:, 0:64], 0.0)
            V.memset(sa_all[1][:, 0:64], 0.0).then_inc(sa_clear, 1)
            V.scalar_tensor_tensor(modc[:, 3, :], bank(2)[:, 3 * KD:4 * KD], 0.0, adac[:, 3, :], ALU.add, ALU.add)
            V.scalar_tensor_tensor(modc[:, 4, :], bank(2)[:, 4 * KD:5 * KD], 1.0, adac[:, 4, :], ALU.add, ALU.add).then_inc(mod_read, 1)
            dve.wait_ge(sa_clear, 1)
            dve.wait_ge(bias_ready, 1)

            def attn_shift(n):
                i, g = n // 2, n % 2
                lo = CHUNK if i == 0 else 0
                v = sa_all[n % 2][:, 64:].rearrange("p (h k) -> p h k", h=GRP)[:, :, lo:]
                src = bank(2, 2).rearrange("p (h k) -> p h k", h=GRP)[:, :, lo:BAND]
                dve.wait_ge(s_done, n + 1)
                if n >= 2:
                    dve.wait_ge(pt_done, n - 1)
                V.scalar_tensor_tensor(v, src, DH ** -0.5, bias[:, g * GRP:(g + 1) * GRP, lo:], ALU.mult, ALU.add).then_inc(sa_read, 1)
                dve.wait_ge(sa_read, n + 1)
                link(V.tensor_reduce(mx[:, n % 2, :], v, AX.X, ALU.max))
                link(V.tensor_tensor(mx[:, n % 2, :], mx[:, n % 2, :], sink[:, g * GRP:(g + 1) * GRP], ALU.max))
                V.tensor_tensor(v, v, mx[:, n % 2, :, None].broadcast_to([P, GRP, BAND - lo]), ALU.subtract)
                V.tensor_tensor(esink[:, n % 2, :], sink[:, g * GRP:(g + 1) * GRP], mx[:, n % 2, :], ALU.subtract).then_inc(s_shift, 1)

            def attn_divide(n):
                i = n // 2
                lo = CHUNK if i == 0 else 0
                v = sa_all[n % 2][:, 64:].rearrange("p (h k) -> p h k", h=GRP)[:, :, lo:]
                dve.wait_ge(p_exp, n + 1)
                link(V.tensor_reduce(sums[:, n % 2, :], v, AX.X, ALU.add))
                link(V.tensor_tensor(sums[:, n % 2, :], sums[:, n % 2, :], esink[:, n % 2, :], ALU.add))
                link(V.reciprocal(rden[:, n % 2, :], sums[:, n % 2, :]))
                V.tensor_tensor(v, v, rden[:, n % 2, :, None].broadcast_to([P, GRP, BAND - lo]), ALU.mult).then_inc(p_ready, 1)

            def halves(buf, w):
                v = buf.rearrange("p (n two w) -> p n two w", two=2, w=w)
                return v[:, :, 0, :], v[:, :, 1, :]

            def level_exponent(u, lv):
                w = LEVELS[lv]
                lo, hi = halves(bcum, w)
                elo, ehi = halves(ebuf[lv % 2], w)
                ref = lo[:, :, w - 1:w].broadcast_to([P, HALF // (2 * w), w])
                if lv == 1:
                    dve.wait_ge(scanned, u + 1)
                V.tensor_tensor(elo, ref, lo, ALU.subtract)
                V.tensor_tensor(ehi, hi, ref, ALU.subtract).then_inc(e_in, 1)

            def level_factors(u, lv):
                w = LEVELS[lv]
                klo, _ = halves(kbuf, w)
                _, qhi = halves(qbuf[u % 2], w)
                elo, ehi = halves(ebuf[lv % 2], w)
                xlo, xhi = halves(xbuf[lv % 2], w)
                dve.wait_ge(e_out, 6 * u + lv + 1)
                if lv >= 2:
                    dve.wait_ge(gram_done, 7 * u + lv)
                V.tensor_tensor(xlo, klo, elo, ALU.mult)
                V.tensor_tensor(xhi, qhi, ehi, ALU.mult).then_inc(x_ready, 1)

            def take_gram(u, s):
                dve.wait_ge(gram_done, 7 * u + s + 1)
                g = bank(4 + s % 2).rearrange("p (i t) -> p i t", i=4)
                sc = score.rearrange("p (i t) -> p i t", i=4)
                if s == 0:
                    if u:
                        dve.wait_ge(ho_done, u)
                    V.tensor_tensor(sc, g, ident[:, None, :].broadcast_to([P, 4, P]), ALU.mult).then_inc(gram_read, 1)
                else:
                    dve.wait_ge(gram_read, 7 * u + s)
                    V.copy_predicated(sc, masks[:, None, s * P:(s + 1) * P].broadcast_to([P, 4, P]), g).then_inc(gram_read, 1)

            def gate_z(n):
                z, ph, phalf = Z0 + n, n // 6, (n // 3) % 2
                dst = qbuf[phalf] if n % 3 == 1 else mixT[:, ph, phalf * HALF:(phalf + 1) * HALF]
                col = (0 if n % 3 == 1 else 12) + ph
                dve.wait_ge(z_sig, n + 1)
                V.scalar_tensor_tensor(dst, bank(z % 2), bcols[:, col:col + 1], dst, ALU.add, ALU.mult).then_inc(z_dve, 1)

            for i in range(NT):
                attn_shift(2 * i)
                if i:
                    attn_divide(2 * i - 1)
                attn_shift(2 * i + 1)
                attn_divide(2 * i)
                dve.wait_ge(v_done, i + 1)
                V.tensor_tensor(vtok[:, i, 0:512], bank(i % 2), hirow, ALU.add)
                V.tensor_tensor(vtok[:, i, 512:640], bank(6 + i % 2)[:, 0:128], carry, ALU.add).then_inc(v_evac, 1)
            attn_divide(15)

            def head_norm(u):
                dve.wait_ge(rms_ready, u + 1)
                dve.wait_ge(z_dve, 2 * u + 2)
                g = mixT[:, u // 2, (u % 2) * HALF:(u % 2 + 1) * HALF]
                V.tensor_tensor(rms, rms, bank(6), ALU.mult).then_inc(o_scaled, 1)
                dve.wait_ge(o_scaled, u + 1)
                V.scalar_tensor_tensor(g, g, norm[:, 0:1], rms, ALU.mult, ALU.mult).then_inc(head_out, 1)

            def carry_states(u):
                dve.wait_ge(u_done, u + 1)
                if u:
                    dve.wait_ge(ho_done, u)
                upd = bank(2, 2).rearrange("p (o c v) -> p c o v", o=2, c=4)
                if u % 2 == 0:
                    link(V.memset(state[:, 0, :], 0.0))
                else:
                    link(V.tensor_copy(state[:, 0, :], carry))
                for cc in range(7):
                    link(V.scalar_tensor_tensor(state[:, cc + 1, :], state[:, cc, :], eblast[:, cc:cc + 1], upd[:, cc // 2, cc % 2, :], ALU.mult, ALU.add))
                V.scalar_tensor_tensor(carry, state[:, 7, :], eblast[:, 7:8], upd[:, 3, 1, :], ALU.mult, ALU.add).then_inc(st_ready, 1)
                dve.wait_ge(st_ready, u + 1)

            for period in range(UNITS + 1):
                u = period - 1
                h = u // 2
                for part3 in range(3):
                    n = 3 * period + part3
                    if 1 <= n <= 3 * UNITS and (n - 1) % 3:
                        gate_z(n - 1)
                    if u < 0:
                        continue
                    if part3 == 0:
                        dve.wait_ge(z_sig, 3 * u + 1)
                        link(V.tensor_scalar(fbuf, sg, oml[:, h:h + 1], lb[:, h:h + 1], ALU.mult, ALU.add))
                        V.tensor_scalar(kbuf, fbuf, -1.0, 1.0, ALU.mult, ALU.add).then_inc(f_ready, 1)
                        dve.wait_ge(lf_ready, u + 1)
                        V.tensor_tensor_scan(bcum, keep[:], ebuf[1], 0.0, ALU.mult, ALU.add).then_inc(scanned, 1)
                        dve.wait_ge(scanned, u + 1)
                        level_exponent(u, 0)
                        b3 = bcum.rearrange("p (c s) -> p c s", s=CHUNK)
                        V.tensor_tensor(kdec.rearrange("p (c s) -> p c s", s=CHUNK),
                                        b3[:, :, CHUNK - 1:CHUNK].broadcast_to([P, 8, CHUNK]), b3, ALU.subtract).then_inc(kd_in, 1)
                        dve.wait_ge(f_ready, u + 1)
                        level_exponent(u, 1)
                        dve.wait_ge(dec_out, u + 1)
                        dve.wait_ge(z_dve, 2 * u + 1)
                        V.tensor_tensor(qdec, qdec, qbuf[u % 2], ALU.mult).then_inc(q_dec, 1)
                        level_factors(u, 0)
                        dve.wait_ge(kd_out, u + 1)
                        V.tensor_tensor(kdec, kdec, kbuf, ALU.mult).then_inc(kd_ready, 1)
                        take_gram(u, 0)
                        dve.wait_ge(x_ready, 6 * u + 1)
                        level_exponent(u, 2)
                        level_factors(u, 1)
                        if u:
                            head_norm(u - 1)
                        take_gram(u, 1)
                        dve.wait_ge(x_ready, 6 * u + 2)
                        level_exponent(u, 3)
                        level_factors(u, 2)
                        take_gram(u, 2)
                    elif part3 == 1:
                        dve.wait_ge(x_ready, 6 * u + 3)
                        level_exponent(u, 4)
                        level_factors(u, 3)
                        take_gram(u, 3)
                        dve.wait_ge(x_ready, 6 * u + 4)
                        level_exponent(u, 5)
                        carry_states(u)
                        level_factors(u, 4)
                        take_gram(u, 4)
                        level_factors(u, 5)
                        take_gram(u, 5)
                    else:
                        take_gram(u, 6)
            head_norm(UNITS - 1)

            def take_logits(t):
                dve.wait_ge(rt_done, t + 1)
                V.tensor_tensor(lg[:, t, :], bank(6 + t % 2)[:, 0:36], br, ALU.add).then_inc(rt_read, 1)

            V.memset(before[:, 0, :], 0.0)
            V.memset(gpad, -3.0e38)
            dve.wait_ge(r_in, 16 * 7)
            for t in range(NT):
                dve.wait_ge(mix_done, t + 1)
                dve.wait_ge(xr_in[t % 2], 16 * (t // 2 + 1))
                if t >= 2:
                    dve.wait_ge(n2_out[t % 2], 16 * (t // 2))
                    dve.wait_ge(t2_done, t - 1)
                r = rbuf[t % 2]
                V.tensor_tensor(r, bank(2 * (t % 2), 2), gt1, ALU.mult).then_inc(mix_read, 1)
                dve.wait_ge(mix_read, t + 1)
                link(V.scalar_tensor_tensor(r, xr[t % 2], ALPHA, r, ALU.mult, ALU.add))
                normalise(r, x2[:, t, :], 0)
                link(V.tensor_tensor(x2[:, t, :], x2[:, t, :], g1, ALU.mult))
                link(V.tensor_tensor(x2[:, t, :], x2[:, t, :], b1, ALU.add))
                normalise(x2[:, t, :], r, 1, n2_ready)
                if t >= 2:
                    take_logits(t - 2)
            take_logits(NT - 2)
            take_logits(NT - 1)
            dve.wait_ge(rt_read, NT)
            link(V.tensor_copy(gpad[:, :, 0:NG], lg[:, :, 0:NG]))
            for t in range(NT):
                link(V.max(gmax[:, t, :], gpad[:, t, :]))
                link(V.max_index(gidx[:, t, :], gmax[:, t, :], gpad[:, t, :]))
            V.tensor_tensor(gexp, lg[:, :, 0:NG], gmax[:, :, 0:1].broadcast_to([P, NT, NG]), ALU.subtract).then_inc(rexp_in, 1)
            link(V.tensor_copy(gsel, gidx[:, :, 0]))
            link(V.tensor_tensor(oh4, iota[:, None, 0:NG].broadcast_to([P, NT, NG]), gsel[:, :, None].broadcast_to([P, NT, NG]), ALU.is_equal))
            link(V.tensor_tensor(prod[:, 0:NT * NE].rearrange("p (t e g) -> p t e g", t=NT, g=NG),
                                 lg[:, :, NG:36].rearrange("p t (g e) -> p t e g", g=NG),
                                 oh4[:, :, None, :].broadcast_to([P, NT, EPG, NG]), ALU.mult))
            link(V.tensor_reduce(e8, prod[:, 0:NT * NE].rearrange("p (t e g) -> p t e g", t=NT, g=NG), AX.X, ALU.add))
            for t in range(NT):
                link(V.max(emax[:, t, :], e8[:, t, :]))
                link(V.max_index(eix[:, t, :], emax[:, t, :], e8[:, t, :]))
            V.tensor_tensor(ex, emax[:, :, 1], emax[:, :, 0], ALU.subtract).then_inc(rexp_in, 1)
            for ch in range(2):
                link(V.tensor_copy(eidx[:, ch, :], eix[:, :, ch]))
                link(V.scalar_tensor_tensor(eid[:, ch, :], gsel, float(EPG), eidx[:, ch, :], ALU.mult, ALU.add))
                link(V.tensor_tensor(oh[:, ch], iota[:, None, 0:NE].broadcast_to([P, NT, NE]),
                                     eid[:, ch, :, None].broadcast_to([P, NT, NE]), ALU.is_equal))
            link(V.tensor_tensor(ohsum, oh[:, 0], oh[:, 1], ALU.add))
            for t in range(NT):
                ins = V.tensor_tensor(before[:, t + 1, :], before[:, t, :], ohsum[:, t, :], ALU.add)
                if t < NT - 1:
                    link(ins)
            ins.then_inc(onehots, 1)
            dve.wait_ge(ranked, 1)
            link(V.tensor_copy(cnt, bank(1)[:, 0:NE]))
            link(V.tensor_tensor(counted, cnt[:, :, None].broadcast_to([P, NE, MAX_EXPERT]),
                                 thresholds[:, None, :].broadcast_to([P, NE, MAX_EXPERT]), ALU.is_gt))
            link(V.tensor_reduce(nblk, counted, AX.X, ALU.add))
            link(V.tensor_scalar(nblk, nblk, 1.0, None, ALU.max))
            link(V.tensor_tensor_scan(bend, ones[:, 0:NE], nblk, 0.0, ALU.mult, ALU.add))
            link(V.tensor_tensor_scan(cend, ones[:, 0:NE], cnt, 0.0, ALU.mult, ALU.add))
            link(V.tensor_tensor(bstart, bend, nblk, ALU.subtract))
            link(V.tensor_tensor(cend, cend, cnt, ALU.subtract))
            link(V.scalar_tensor_tensor(shift, bstart, float(BLK), cend, ALU.mult, ALU.subtract))
            link(V.tensor_tensor(pos, bank(0)[:, 0:NT * NE].rearrange("p (t e) -> p t e", t=NT),
                                 cend[:, None, :].broadcast_to([P, NT, NE]), ALU.add))
            pv = prod.rearrange("p (c t e) -> p c t e", c=2, t=NT)
            for ch in range(2):
                ins = V.tensor_tensor(pv[:, ch], oh[:, ch], pos, ALU.mult)
            link(ins)
            link(V.tensor_reduce(slotf, pv, AX.X, ALU.add))
            V.tensor_copy(yrowi[:], slotf)
            for ch in range(2):
                ins = V.tensor_tensor(pv[:, ch], oh[:, ch], shift[:, None, :].broadcast_to([P, NT, NE]), ALU.mult)
            link(ins)
            link(V.tensor_reduce(rowf, pv, AX.X, ALU.add))
            link(V.tensor_tensor(slotf, slotf, rowf, ALU.add))
            link(V.tensor_copy(sloti[:], slotf))
            link(V.tensor_scalar(bitsi[:], sloti[:], BLK - 1, None, ALU.bitwise_and))
            link(V.tensor_copy(rowf, bitsi[:]))
            link(V.tensor_tensor(slotf, slotf, rowf, ALU.subtract))
            link(V.tensor_scalar(blkf, slotf, 1.0 / BLK, None, ALU.mult))
            flat = (lambda v: v.rearrange("p c t -> p (c t)"))
            V.tensor_tensor(row_oh, iota[:, None, 0:BLK].broadcast_to([P, 2 * NT, BLK]),
                            flat(rowf)[:, :, None].broadcast_to([P, 2 * NT, BLK]), ALU.is_equal)
            link(V.tensor_tensor(blk_oh, iota[:, None, :].broadcast_to([P, 2 * NT, MAX_BLOCKS]),
                                 flat(blkf)[:, :, None].broadcast_to([P, 2 * NT, MAX_BLOCKS]), ALU.is_equal))
            for ch in range(2):
                half = blk_oh[:, ch * NT:(ch + 1) * NT, :]
                ins = V.tensor_tensor(half, half, token_id[:, :, None].broadcast_to([P, NT, MAX_BLOCKS]), ALU.mult)
            ins.then_inc(slots_ready, 1)
            V.tensor_copy(nblki[0:1], nblk[0:1])
            V.tensor_copy(bendi[0:1], bend[0:1]).then_inc(plan_ready, 1)
            dve.wait_ge(table_done, 1)
            V.tensor_copy(slot_tok[0:BLK, 0:MAX_BLOCKS], bank(2)[0:BLK, 0:MAX_BLOCKS]).then_inc(table_ready, 1)
            link(V.scalar_tensor_tensor(padding[0:1], nblk[0:1], float(BLK), cnt[0:1], ALU.mult, ALU.subtract))
            link(V.tensor_tensor(blkcmp[0:1], iota[0:1, :, None].broadcast_to([1, MAX_BLOCKS, NE]),
                                 bend[0:1, None, :].broadcast_to([1, MAX_BLOCKS, NE]), ALU.is_ge))
            link(V.tensor_tensor(blkcmp[0:1], blkcmp[0:1], padding[0:1, None, :].broadcast_to([1, MAX_BLOCKS, NE]), ALU.mult))
            link(V.tensor_reduce(row0f[0:1], blkcmp[0:1], AX.X, ALU.add))
            link(V.scalar_tensor_tensor(row0f[0:1], iota[0:1], float(BLK), row0f[0:1], ALU.mult, ALU.subtract))
            V.tensor_copy(row0i[0:1], row0f[0:1]).then_inc(rows_ready, 1)
            dve.wait_ge(rexp_out, 2)
            link(V.tensor_reduce(psel, gexp, AX.X, ALU.add))
            link(V.tensor_scalar(den, ex, 1.0, None, ALU.add))
            link(V.tensor_tensor(den, den, psel, ALU.mult))
            link(V.reciprocal(wa, den))
            link(V.tensor_tensor(wb, wa, ex, ALU.mult))

            dve.wait_ge(fin_rows, 16 * 4)
            dve.wait_ge(plan_ready, 1)
            total = dve.value_load(bendi[0:1, NE - 1:NE], min_val=1, max_val=MAX_BLOCKS)
            dve.sem_inc(y_scaled, 1)
            with dve.Fori(0, total) as j:
                for half in range(2):
                    f = slice(half * 2 * P, (half + 1) * 2 * P)
                    dve.wait_ge(silu_out, j * 2 + 1 + half)
                    V.tensor_tensor(hid[BLK:P, f], sl[BLK:P, f], bank(2 + half)[BLK:P, 0:2 * P], ALU.mult).then_inc(hid_ready[half], 1)
                for half in range(2):
                    dve.wait_ge(ht_done, j * 2 + 1 + half)
                    V.tensor_copy(hidT[:, half * P:(half + 1) * P], bank(4 + half)[:, 0:P]).then_inc(ht_evac[half], 1)
                dve.wait_ge(y_done, j + 1)
                dve.wait_ge(y_out, j * 32 + 16)
                V.tensor_tensor(yo, bank(6), gt2, ALU.mult).then_inc(y_scaled, 1)

            dve.wait_ge(y_out, total * 32 + 16)
            dve.wait_ge(xg_in, total * 16 + 16)
            V.memset(stats[:, 0, 0:1], 0.0).then_inc(blocks_out, 1)
            dve.wait_ge(x2_scaled, NT)
            dve.wait_ge(blocks_out, 1)

            def combine(t):
                f, s = ya[t], t % 2
                dve.wait_ge(ys_in[t], 32)
                link(V.scalar_tensor_tensor(f, f, wa[:, t:t + 1], x2[:, t, :], ALU.mult, ALU.add))
                link(V.scalar_tensor_tensor(f, yb[t], wb[:, t:t + 1], f, ALU.mult, ALU.add))
                V.bn_stats(stats[:, s, 0:6], f[:, 0:512])
                link(V.bn_stats(stats[:, s, 6:12], f[:, 512:1024]))
                if t >= 2:
                    dve.wait_ge(applied, t - 1)
                V.bn_aggr(mv[:, s, :], stats[:, s, :]).then_inc(var_ready, 1)
                n_norm[0] += 1

            def deviation(t):
                s = t % 2
                dve.wait_ge(rstd_ready, n_norm[0] - (t < NT - 1))
                V.scalar_tensor_tensor(nmr[:, s, :], mv[:, s, 0:1], -1.0, rstd[:, s, :], ALU.mult, ALU.mult).then_inc(nmr_ready, 1)

            def gain(t):
                dve.wait_ge(applied, t + 1)
                V.tensor_tensor(ya[t], ya[t], g2, ALU.mult).then_inc(gained, 1)

            for t in range(NT + 1):
                if t < NT:
                    combine(t)
                if t:
                    deviation(t - 1)
                if t >= 2:
                    gain(t - 2)
            gain(NT - 1)

        @block.tensor
        def _(pe):
            M = nc.tensor.matmul

            def transposes(src, dst, n, step):
                v = src.rearrange("p (d k) -> p k d", k=step)
                for k in range(n):
                    last = nc.tensor.transpose(dst[:, k * P:(k + 1) * P], v[:, k, :], ident)
                return last

            def transpose_x(t):
                pe.wait_ge(xn_ready, t + 1)
                if t >= 2:
                    pe.wait_ge(xt_evac, t - 1)
                    pe.wait_ge(xv_evac, t - 1)
                transposes(xn[t % 2], bank(4 + 2 * (t % 2), 2), KD, KD).then_inc(xt_done, 1)

            def reduce_mod(n):
                pe.wait_ge(ada_summed, n + 1)
                kind, half = n // 2, n % 2
                if kind in (2, 5):
                    r = {4: 0, 5: 1, 10: 2, 11: 3}[n]
                    if r:
                        pe.wait_ge(row_ready, r)
                    M(bank(3), lhsT=ones[:], rhs=acc[n % 2], start=True, stop=False)
                    last = M(bank(3), lhsT=ones[0:1, :], rhs=adarow[0:1, r * 512:(r + 1) * 512], start=False, stop=True)
                else:
                    v = acc[n % 2].rearrange("p (m k) -> p k m", k=KD)
                    for k in range(KD):
                        last = M(bank(2)[half * 64:half * 64 + 64, kind * KD + k:kind * KD + k + 1],
                                 lhsT=v[:, k, :], rhs=ones[:, 0:1], start=True, stop=True)
                last.then_inc(mod_done, 1)

            pe.wait_ge(consts_in, 16 * 3)
            pe.wait_ge(set_up, 4)
            for t in range(4):
                transpose_x(t)
            for n in range(4):
                reduce_mod(n)
                transpose_x(n + 4)
            pe.wait_ge(rows_in, 16 * 6)
            pe.wait_ge(rel_rows, 1)
            for h in range(AH):
                if h >= 2:
                    pe.wait_ge(trep_read, h - 1)
                M(bank(h % 2)[:, 0:DIFFS], lhsT=relb[0:32, h * P:(h + 1) * P], rhs=onehot[0:32, :], start=True, stop=True).then_inc(trep_done, 1)
            pe.wait_ge(h_ready, 2)
            pe.wait_ge(trep_read, AH)

            def z_free(z):
                if z >= 2:
                    pe.wait_ge(z_act, z - 1)
                    turn = z - 2 - Z0
                    if turn >= 1:
                        pe.wait_ge(z_dve, 2 * (turn // 3) + turn % 3)

            def z_steps(z, stationary, half, ks):
                for k in ks:
                    last = M(bank(z % 2), lhsT=stationary[:, k], rhs=hT[:, k, half * HALF:(half + 1) * HALF],
                             start=(k == 0), stop=(k == KD - 1))
                if ks[-1] == KD - 1:
                    last.then_inc(z_done, 1)

            for z in range(Z0):
                z_free(z)
                if z == 0:
                    arrived(pe, "kv")
                if z == 2:
                    arrived(pe, "aq")
                st = view("kv", 256)[:, :, 0:P] if z < 2 else view("aq")[:, :, (z - 2) // 2 * P:((z - 2) // 2 + 1) * P]
                z_steps(z, st, z % 2, list(range(KD)))
                if z >= 2:
                    reduce_mod(z + 2)
            pe.wait_ge(bias_ready, 1)
            pe.wait_ge(mod_read, 2)
            pe.wait_ge(row_ready, 4)

            def attn_scores(n):
                i, g = n // 2, n % 2
                pe.wait_ge(z_act, Z0)
                if n:
                    pe.wait_ge(sa_read, n)
                base, lo = g * DH, (CHUNK if i == 0 else 0)
                for j in range(GRP):
                    last = M(bank(2, 2)[:, j * 256 + lo:j * 256 + BAND],
                             lhsT=mixT[base:base + DH, 4 + j, i * P:(i + 1) * P],
                             rhs=kT[base:base + DH, i * P - CHUNK + lo:(i + 1) * P], start=True, stop=True)
                last.then_inc(s_done, 1)

            def attn_transpose(n):
                i, g = n // 2, n % 2
                pe.wait_ge(p_ready, n + 1)
                if n:
                    pe.wait_ge(o_evac, n)
                p = sa_all[n % 2]
                for j in range(GRP):
                    last = nc.tensor.transpose(bank(4)[:, j * P:(j + 1) * P], p[:, 128 + j * BAND:256 + j * BAND], ident)
                if i:
                    for j in range(GRP):
                        last = nc.tensor.transpose(bank(5)[:, j * CHUNK:(j + 1) * CHUNK], p[0:CHUNK, j * BAND:j * BAND + P],
                                                   ident[0:CHUNK, 0:CHUNK])
                last.then_inc(pt_done, 1)

            def attn_values(n):
                i, g = n // 2, n % 2
                pe.wait_ge(pt_evac, n + 1)
                pe.wait_ge(v_evac, i + 1)
                base = g * DH
                o = bank(4)[base:base + DH, :]
                last = M(o, lhsT=vtok[:, i, 512 + base:512 + base + DH], rhs=pto, start=True, stop=(i == 0))
                if i:
                    last = M(o.rearrange("p (j t) -> p j t", j=GRP)[:, :, 0:CHUNK],
                             lhsT=vtok[CHUNK:P, i - 1, 512 + base:512 + base + DH],
                             rhs=ptp[CHUNK:P, :].rearrange("p (j t) -> p j t", j=GRP), start=False, stop=True)
                last.then_inc(o_done, 1)

            def gram(u, s):
                a, b = (kbuf, qbuf[u % 2]) if s == 0 else (xbuf[(s - 1) % 2],) * 2
                if s == 0:
                    pe.wait_ge(f_ready, u + 1)
                    pe.wait_ge(z_dve, 2 * u + 1)
                else:
                    pe.wait_ge(x_ready, 6 * u + s)
                if s >= 2:
                    pe.wait_ge(gram_read, 7 * u + s - 1)
                elif u:
                    pe.wait_ge(gram_read, 7 * u)
                for i in range(4):
                    last = M(bank(4 + s % 2)[:, i * P:(i + 1) * P], lhsT=a[:, i * P:(i + 1) * P], rhs=b[:, i * P:(i + 1) * P],
                             start=True, stop=True)
                last.then_inc(gram_done, 1)

            def decayed_keys(u):
                pe.wait_ge(kd_ready, u + 1)
                if u:
                    pe.wait_ge(st_ready, u)
                for i in range(4):
                    last = nc.tensor.transpose(bank(2)[:, i * P:(i + 1) * P], kdec[:, i * P:(i + 1) * P], ident)
                last.then_inc(kdt_done, 1)

            def state_updates(u):
                h, half = u // 2, u % 2
                pe.wait_ge(kdt_evac, u + 1)
                for cc in range(8):
                    i, r = cc // 2, (cc % 2) * CHUNK
                    last = M(bank(2 + cc % 2)[:, i * P:(i + 1) * P], lhsT=kdT[r:r + CHUNK, i * P:(i + 1) * P],
                             rhs=vtok[r:r + CHUNK, half * 4 + i, h * P:(h + 1) * P], start=True, stop=True)
                last.then_inc(u_done, 1)

            def head_product(u):
                h, half = u // 2, u % 2
                pe.wait_ge(st_ready, u + 1)
                pe.wait_ge(q_dec, u + 1)
                pe.wait_ge(gram_read, 7 * u + 7)
                if u:
                    pe.wait_ge(head_out, u)
                for i in range(4):
                    o = bank(6)[:, i * P:(i + 1) * P]
                    M(o, lhsT=vtok[:, half * 4 + i, h * P:(h + 1) * P], rhs=score[:, i * P:(i + 1) * P], start=True, stop=False,
                      skip_group_check=True)
                    for cc in (2 * i, 2 * i + 1):
                        last = M(bank(6)[:, cc * CHUNK:(cc + 1) * CHUNK], lhsT=state[:, cc, :], rhs=qdec[:, cc * CHUNK:(cc + 1) * CHUNK],
                                 start=False, stop=True, skip_group_check=True)
                last.then_inc(ho_done, 1)

            def mean_square(u):
                if u:
                    pe.wait_ge(rms_ready, u)
                pe.wait_ge(sq_ready, u + 1)
                M(bank(7), lhsT=mean[:], rhs=sq, start=True, stop=True).then_inc(ms_done, 1)

            arrived(pe, "hi")
            for i in range(NT):
                for step in range(2):
                    n = 2 * i + step
                    attn_scores(n)
                    if i:
                        attn_transpose(n - 2)
                    if step == 0 and i >= 2:
                        pe.wait_ge(v_evac, i - 1)
                    for k in range(4 * step, 4 * step + 4):
                        M(bank(i % 2), lhsT=hT[:, k, i * P:(i + 1) * P], rhs=view("hi")[:, k, :], start=(k == 0), stop=(k == KD - 1))
                    if step:
                        for k in range(KD):
                            last = M(bank(6 + i % 2)[:, 0:P], lhsT=hT[:, k, i * P:(i + 1) * P], rhs=view("kv", 256)[:, k, P:2 * P],
                                     start=(k == 0), stop=(k == KD - 1))
                        last.then_inc(v_done, 1)
                    if i:
                        attn_values(n - 2)
            for n in (14, 15):
                attn_transpose(n)
                attn_values(n)
            pe.wait_ge(v_evac, NT)
            pe.wait_ge(o_evac, 16)

            for name in ("hf", "hq", "hg"):
                arrived(pe, name)
            for period in range(UNITS + 1):
                u = period - 1
                for part3 in range(3):
                    z = Z0 + 3 * period + part3
                    if period < UNITS:
                        z_free(z)
                        st = view(("hf", "hq", "hg")[part3])[:, :, (period // 2) * P:(period // 2 + 1) * P]
                    for quarter in range(4):
                        if period < UNITS:
                            z_steps(z, st, period % 2, [2 * quarter, 2 * quarter + 1])
                        if u < 0:
                            continue
                        step = 4 * part3 + quarter
                        if step in (0, 1, 2):
                            gram(u, step)
                        elif step == 3:
                            decayed_keys(u)
                        elif step == 4:
                            gram(u, 3)
                        elif step == 5:
                            state_updates(u)
                        elif step in (6, 7, 8):
                            gram(u, step - 2)
                        elif step == 10:
                            head_product(u)
                        elif step == 11:
                            mean_square(u)

            pe.wait_ge(head_out, UNITS)
            pe.wait_ge(o_evac, 16)
            arrived(pe, "wo0")
            pe.wait_ge(piece_in[0], 16 * 5)
            wo = [slot(s).rearrange("p (m n) -> p m n", m=4) for s in (3, 0)]

            def transpose_norm(t):
                pe.wait_ge(n2_ready, t + 1)
                if t:
                    pe.wait_ge(t2_evac, t)
                transposes(rbuf[t % 2], bank(4, 2), KD, KD).then_inc(t2_done, 1)

            def route(t):
                pe.wait_ge(t2_evac, t + 1)
                pe.wait_ge(r_in, 16 * 7)
                if t >= 2:
                    pe.wait_ge(rt_read, t - 1)
                for k in range(KD):
                    last = M(bank(6 + t % 2)[:, 0:36], lhsT=h2T[t % 2][:, k * P:(k + 1) * P], rhs=wr[:, k, :],
                             start=(k == 0), stop=(k == KD - 1))
                last.then_inc(rt_done, 1)

            for t in range(NT):
                if t >= 2:
                    pe.wait_ge(mix_read, t - 1)
                for half in range(2):
                    for m in range(8):
                        last = M(bank(2 * (t % 2) + half), lhsT=mixT[:, m, t * P:(t + 1) * P],
                                 rhs=wo[m // 4][:, m % 4, half * HALF:(half + 1) * HALF], start=(m == 0), stop=(m == 7))
                    if half == 0 and t >= 2:
                        route(t - 2)
                last.then_inc(mix_done, 1)
                if t:
                    transpose_norm(t - 1)
            route(NT - 2)
            transpose_norm(NT - 1)
            route(NT - 1)
            pe.wait_ge(onehots, 1)
            M(bank(0)[:, 0:NT * NE], lhsT=tri, rhs=ohsum, start=True, stop=False)
            M(bank(0)[:, 0:NT * NE], lhsT=ones[:], rhs=before[:, 0:NT, :], start=False, stop=True)
            M(bank(1)[:, 0:NE], lhsT=ones[:], rhs=before[:, NT, :], start=True, stop=True).then_inc(ranked, 1)
            pe.wait_ge(slots_ready, 1)
            for n in range(2 * NT):
                last = M(bank(2)[0:BLK, 0:MAX_BLOCKS], lhsT=row_oh[:, n, :], rhs=blk_oh[:, n, :], start=(n == 0), stop=(n == 2 * NT - 1))
            last.then_inc(table_done, 1)

            pe.wait_ge(plan_ready, 1)
            blocks = pe.alloc_register("blocks")
            arrivals = pe.alloc_register("arrivals")
            gated = [pe.alloc_register(f"gated{half}") for half in range(2)]
            for counter in (blocks, *gated):
                pe.reg_mov(counter, 1)
            pe.reg_mov(arrivals, 32)

            def transpose_tokens():
                v = xg[0:BLK, :].rearrange("p (d k) -> p k d", k=KD)
                for k in range(KD):
                    last = nc.tensor.transpose(bank(0)[:, k * BLK:(k + 1) * BLK], v[:, k, :], ident[0:BLK, 0:BLK])
                last.then_inc(xg_t, 1)

            pe.wait_ge(xg_in, 16)
            transpose_tokens()
            with pe.Fori(0, NE // 2) as i:
                for b in range(2):
                    w1v, w3v = (slot(s[b]).rearrange("p (k f) -> p k f", k=KD) for s in (W1, W3))
                    w2v = slot(W2[b]).rearrange("p (k f) -> p k f", k=4)
                    own = pe.value_load(nblki[0:1, bass.ds(i * 2 + b, 1)], min_val=1, max_val=MAX_EXPERT)
                    with pe.Fori(0, own):
                        pe.wait_ge(w1_in[b], i * 16 + 16)
                        pe.wait_ge(w3_in[b], i * 16 + 16)
                        pe.wait_ge(xT_evac, blocks)
                        for half in range(2):
                            if half:
                                pe.wait_ge(xg_in, arrivals)
                                pe.reg_add(arrivals, arrivals, 16)
                                transpose_tokens()
                            f = slice(half * 2 * P, (half + 1) * 2 * P)
                            for k in range(KD):
                                x_k = xT[:, k * BLK:(k + 1) * BLK]
                                M(bank(2 + half)[0:BLK, 0:2 * P], lhsT=x_k, rhs=w1v[:, k, f], start=(k == 0), stop=(k == KD - 1))
                                last = M(bank(2 + half)[BLK:P, 0:2 * P], lhsT=x_k, rhs=w3v[:, k, f], start=(k == 0), stop=(k == KD - 1))
                            last.then_inc(gu_done[half], 1)
                        for half in range(2):
                            pe.wait_ge(hid_ready[half], gated[half])
                            pe.reg_add(gated[half], gated[half], 1)
                            for k in (2 * half, 2 * half + 1):
                                last = nc.tensor.transpose(bank(4 + half)[:, (k % 2) * BLK:(k % 2 + 1) * BLK],
                                                           hid[BLK:P, k * P:(k + 1) * P], ident[BLK:P, BLK:P])
                            last.then_inc(ht_done, 1)
                        pe.wait_ge(w2_in[b], i * 16 + 16)
                        pe.wait_ge(y_scaled, blocks)
                        for k in range(4):
                            if k % 2 == 0:
                                pe.wait_ge(ht_evac[k // 2], blocks)
                            for half in range(2):
                                last = M(bank(6)[half * BLK:(half + 1) * BLK, :], lhsT=hidT[:, k * BLK:(k + 1) * BLK],
                                         rhs=w2v[:, k, half * HALF:(half + 1) * HALF], start=(k == 0), stop=(k == 3))
                        last.then_inc(y_done, 1)
                        pe.reg_add(blocks, blocks, 1)


def constants():
    i = np.arange(P)
    f = np.zeros((P, 2 * P + MAX_BLOCKS + MAX_EXPERT + NT), np.float32)
    f[:, :P] = np.eye(P)
    f[:, P:2 * P] = i[:, None] < i[None, :]
    f[:, 2 * P:2 * P + MAX_BLOCKS] = np.arange(MAX_BLOCKS)
    f[:, 2 * P + MAX_BLOCKS:2 * P + MAX_BLOCKS + MAX_EXPERT] = np.arange(MAX_EXPERT) * BLK
    f[:, 2 * P + MAX_BLOCKS + MAX_EXPERT:] = np.arange(NT)[None, :] * P + i[:, None]
    m = np.zeros((P, 7, P), np.int32)
    for n, w in enumerate(LEVELS):
        m[:, n + 1] = ((i[:, None] // (2 * w) == i[None, :] // (2 * w)) & (i[:, None] % (2 * w) < w)
                       & (i[None, :] % (2 * w) >= w))
    n = BAND - 1 - np.arange(DIFFS)
    side = (n < 0).astype(np.int32) * 16
    n = np.abs(n)
    far = np.minimum(8 + (np.log(np.maximum(n, 1) / 8) / np.log(128 / 8) * 8).astype(np.int32), 15)
    bucket = side + np.where(n < 8, n, far)
    onehot = (np.arange(32)[:, None] == bucket[None, :]).astype(np.float32)
    return f, m.reshape(P, 7 * P), onehot


def kernel(**inputs):
    import concourse.bacc as bacc
    from concourse.bass_utils import run_bass_kernel_spmd

    b_in = np.asarray(inputs["b_in"])
    tiles = b_in[0].reshape(22, P)
    heads = tiles[16:20].reshape(KVH, GRP, DH).transpose(1, 0, 2).reshape(GRP, P)
    low = np.asarray(inputs["hg_lower"])
    w_in = np.asarray(inputs["w_in"])
    order = np.arange(w_in.shape[2])
    order[2048:2560] = order[2048:2560].reshape(KVH, GRP, DH).transpose(1, 0, 2).reshape(-1)
    given = {k: np.ascontiguousarray(inputs[k]) for k in ("x", "c")}
    given["w_in"] = np.ascontiguousarray(w_in[:, :, order])
    given["b_in_row"] = np.ascontiguousarray(np.concatenate([b_in[:, 1024:1536], b_in[:, 2688:2816]], axis=1))
    given["b_in_cols"] = np.ascontiguousarray(np.concatenate([tiles[:16], heads, tiles[20:]]).T)
    given["w_out"] = np.ascontiguousarray(inputs["w_out"])
    given["hg_lower_cols"] = np.ascontiguousarray(low.reshape(2, HEADS, P).transpose(2, 0, 1).reshape(P, 2 * HEADS))
    for k in ("hg_norm", "attn_sinks", "rel_bias", "ada_w", "ada_b", "ln1_g", "ln1_b", "ln2_g", "ln2_b", "w_group",
              "b_group", "w_sub", "b_sub", "w1", "w3", "w2"):
        given[k] = np.ascontiguousarray(inputs[k])
    given["c_f32"], given["c_masks"], given["c_onehot"] = constants()

    nc = bacc.Bacc("TRN2", target_bir_lowering=False, num_devices=1)
    arrays, args = {}, []
    for name, a in given.items():
        arrays[f"in_{name}"] = a
        args.append(nc.dram_tensor(f"in_{name}", a.shape, mybir.dt.from_np(a.dtype), kind="ExternalInput").ap())
    args.append(nc.dram_tensor("out_0", OUTS[0][0], mybir.dt.float32, kind="ExternalOutput").ap())
    block_kernel(nc, *args)
    r = run_bass_kernel_spmd(nc, [arrays], core_ids=[0])
    return r.results[0]["out_0"]
```

```python
from contextlib import ExitStack

import numpy as np

import concourse.bass as bass
from concourse import mybir

P = 128
D = 1024
T = 1024
KD = D // P
NT = T // P
CHUNK = 64
HEADS = 4
HALF = 512
UNITS = HEADS * 2
LEVELS = [32, 16, 8, 4, 2, 1]
AH = 8
KVH = 2
GRP = 4
DH = 64
BAND = 192
DIFFS = 320
NG = 4
EPG = 8
DE = 512
BLK = 64
NE = 32
MAX_BLOCKS = 2 * T // BLK + NE
MAX_EXPERT = T // BLK
ALPHA = 2.0 ** 0.25
EPS = 1e-5
NEG = -1.0e30
SLOT = 4096
OUTS = [((1, 1024, 1024), "float32")]


def block_kernel(nc, x, c, w_in, b_in_row, b_in_cols, w_out, hg_lower_cols, hg_norm, attn_sinks, rel_bias,
                 ada_w, ada_b, ln1_g, ln1_b, ln2_g, ln2_b, w_group, b_group, w_sub, b_sub, w1, w3, w2,
                 c_f32, c_masks, c_onehot, out):
    f32, i32, u32, u8 = mybir.dt.float32, mybir.dt.int32, mybir.dt.uint32, mybir.dt.uint8
    ALU, ACT, AX = mybir.AluOpType, mybir.ActivationFunctionType, mybir.AxisListType
    ctx = ExitStack()
    with ctx:
        def sb(name, shape, dt=f32):
            return ctx.enter_context(nc.sbuf_tensor(name, shape, dt))

        def sem(name):
            return ctx.enter_context(nc.semaphore(name))

        ring = sb("ring", [P, 6 * SLOT])
        hx = sb("hx", [P, NT * D])
        area = sb("area", [P, 17792])
        cf = sb("cf", [P, 2 * P + MAX_BLOCKS + MAX_EXPERT + NT])
        masks = sb("masks", [P, 7 * P], u8)
        ones = sb("ones", [P, P])
        mean = sb("mean", [P, P])
        keep = sb("keep", [P, HALF], mybir.dt.bfloat16)
        modc = sb("modc", [P, 6, KD])
        adac = sb("adac", [P, 6, KD])
        cond = sb("cond", [P, KD])
        small = sb("small", [P, 1024])

        def slot(s):
            return ring[:, s * SLOT:(s + 1) * SLOT]

        mixT = ring[:, 4 * SLOT:6 * SLOT].rearrange("p (m t) -> p m t", m=8)
        hT = hx[:, :].rearrange("p (k t) -> p k t", k=KD)
        x2 = hx[:, :].rearrange("p (t d) -> p t d", t=NT)
        ident, tri = cf[:, 0:128], cf[:, 128:256]
        iota = cf[:, 2 * P:2 * P + MAX_BLOCKS]
        thresholds = cf[:, 2 * P + MAX_BLOCKS:2 * P + MAX_BLOCKS + MAX_EXPERT]
        token_id = cf[:, 2 * P + MAX_BLOCKS + MAX_EXPERT:]

        cut = [0]

        def part(n):
            cut[0] += n
            assert cut[0] <= 17792, cut[0]
            return area[:, cut[0] - n:cut[0]]

        vtok = part(NT * 640).rearrange("p (t v) -> p t v", t=NT)
        kT = part(T)
        bias = part(AH * BAND).rearrange("p (h k) -> p h k", h=AH)
        sa_all = [part(64 + GRP * BAND) for _ in range(2)]
        ptp = part(GRP * CHUNK)
        pto = part(GRP * P)
        hg0 = cut[0]
        sg, fbuf, bcum, kbuf, score, qdec, kdec = (part(HALF) for _ in range(7))
        qbuf = [part(HALF) for _ in range(2)]
        ebuf = [part(HALF) for _ in range(2)]
        xbuf = [part(HALF) for _ in range(2)]
        state = part(8 * P).rearrange("p (c v) -> p c v", c=8)
        kdT, sq, rms = sa_all[0][:, 0:HALF], sa_all[1][:, 0:HALF], pto
        cut[0] = hg0
        xin = [part(D) for _ in range(2)] + [ring[:, 4 * SLOT + t * D:4 * SLOT + (t + 1) * D] for t in range(NT - 2)]
        xn = [part(D) for _ in range(2)]
        acc = [part(HALF) for _ in range(2)]
        adarow = part(2048)
        trep = area[:, 0:AH * DIFFS].rearrange("p (h m) -> p h m", h=AH)
        wide_masks = area[:, 3072:3072 + 7 * P].bitcast(i32)
        relb = kT
        cond_wide = area[:, 4096:4096 + KD * P].rearrange("p (k m) -> p k m", k=KD)
        hirow = part(HALF)
        onehot = sa_all[1][:, 0:DIFFS]
        rowbuf = pto
        cut[0] = 0
        gt1 = part(D)
        g1, b1 = part(D), part(D)
        xr = [part(D) for _ in range(2)]
        rbuf = [part(D) for _ in range(2)]
        h2T = [part(D) for _ in range(2)]
        wr = part(KD * 36).rearrange("p (k n) -> p k n", k=KD)
        br = part(36)
        lg = part(NT * 36).rearrange("p (t n) -> p t n", t=NT)
        oh = part(2 * NT * NE).rearrange("p (c t e) -> p c t e", c=2, t=NT)
        ohsum = part(NT * NE).rearrange("p (t e) -> p t e", t=NT)
        before = part(9 * NE).rearrange("p (t e) -> p t e", t=9)
        pos = part(NT * NE).rearrange("p (t e) -> p t e", t=NT)
        prod = part(2 * NT * NE)
        counted = part(NE * MAX_EXPERT).rearrange("p (e m) -> p e m", e=NE)
        blkcmp = part(MAX_BLOCKS * NE).rearrange("p (b e) -> p b e", b=MAX_BLOCKS)
        row_oh = part(2 * NT * BLK).rearrange("p (n r) -> p n r", r=BLK)
        blk_oh = part(2 * NT * MAX_BLOCKS).rearrange("p (n j) -> p n j", j=MAX_BLOCKS)
        cnt, nblk, bend, bstart, cend, shift, padding = (part(NE) for _ in range(7))
        row0f = part(MAX_BLOCKS)
        cut[0] = 0
        xg, xT, sl, hid, hidT, yo, gt2 = part(D), part(HALF), part(DE), part(DE), part(2 * P), part(HALF), part(HALF)
        g2 = part(D)
        b2 = xg
        late = [part(SLOT) for _ in range(3)]
        diag = [late[0][:, t * 2 * P:(t + 1) * 2 * P] for t in range(NT)]
        ya = [ring[:, t * D:(t + 1) * D] for t in range(NT)]
        yb = [ring[:, (NT + t) * D:(NT + t + 1) * D] for t in range(NT)]

        at = [0]

        def bit(*shape):
            n = int(np.prod(shape))
            at[0] += n
            assert at[0] <= 1024
            v = small[:, at[0] - n:at[0]]
            if len(shape) == 2:
                v = v.rearrange("p (a b) -> p a b", a=shape[0])
            return v

        stats = bit(2, 12)
        mv = bit(2, 2)
        rstd = bit(2, 1)
        lowc = bit(2, HEADS)
        lowd = bit(HEADS)
        lb, oml = bit(HEADS), bit(HEADS)
        bcols = bit(22)
        nbcols = bit(22)
        norm, eps = bit(1), bit(1)
        rel_src = bit(AH)
        carry = bit(P)
        sink = bit(AH)
        mx = bit(2, GRP)
        sums, esink, rden = bit(2, GRP), bit(2, GRP), bit(2, GRP)
        eblast = bit(8)
        ecols, mods = bit(1, KD), bit(2, KD)
        gmax, emax = bit(NT, 8), bit(NT, 8)
        gpad, e8 = bit(NT, 8), bit(NT, 8)
        gsel = bit(NT)
        oh4 = bit(NT, NG)
        gexp = bit(NT, NG)
        psel, ex, den, wa, wb = bit(NT), bit(NT), bit(NT), bit(NT), bit(NT)
        eid = bit(2, NT)
        eidx = bit(2, NT)
        slotf = bit(2, NT)
        rowf, blkf = bit(2, NT), bit(2, NT)
        nmr = bit(2, 1)
        gidx = sb("gidx", [P, NT, 8], u32)
        eix = sb("eix", [P, NT, 8], u32)
        sloti = sb("sloti", [P, 2, NT], i32)
        bitsi = sb("bitsi", [P, 2, NT], i32)
        yrowi = sb("yrowi", [P, 2, NT], i32)
        nblki = sb("nblki", [P, NE], i32)
        bendi = sb("bendi", [P, NE], i32)
        row0i = sb("row0i", [P, MAX_BLOCKS], i32)
        slot_tok = sb("slot_tok", [P, MAX_BLOCKS + 2], i32)
        pick = sb("pick", [P, 1], i32)

        ps = ctx.enter_context(nc.psum_tensor("ps", [P, 8 * 512], f32))

        def bank(b, n=1):
            return ps[:, b * 512:(b + n) * 512]

        diffs_d = nc.dram_tensor("diffs_d", [P, AH, DIFFS], f32).ap()
        gates_d = nc.dram_tensor("gates_d", [2, D], f32).ap()
        n2_d = nc.dram_tensor("n2_d", [T, D], f32).ap()
        y_d = nc.dram_tensor("y_d", [2 * T + BLK, D], f32).ap()

        piece_in = [sem(f"piece_in{s}") for s in range(5)]
        consts_in, cols_in, rows_in, x_in = sem("consts_in"), sem("cols_in"), sem("rows_in"), [sem(f"x_in{t}") for t in range(NT)]
        set_up, filled = sem("set_up"), sem("filled")
        cond_in, cond_e, cond_ready = sem("cond_in"), sem("cond_e"), sem("cond_ready")
        xn_ready, xt_done, xt_evac = sem("xn_ready"), sem("xt_done"), sem("xt_evac")
        ada_summed, mod_done, mod_taken, mod_read, row_out = sem("ada_summed"), sem("mod_done"), sem("mod_taken"), sem("mod_read"), sem("row_out")
        lowexp = sem("lowexp")
        rel_rows, trep_done, trep_read, diffs_out, bias_in, bias_ready = (
            sem("rel_rows"), sem("trep_done"), sem("trep_read"), sem("diffs_out"), sem("bias_in"), sem("bias_ready"))
        v_done, v_evac = sem("v_done"), sem("v_evac")
        z_done, z_act, z_dve, z_sig, q_dec = (sem(n) for n in ("z_done", "z_act", "z_dve", "z_sig", "q_dec"))
        var_ready, rstd_ready, rms_ready = sem("var_ready"), sem("rstd_ready"), sem("rms_ready")
        o_scaled = sem("o_scaled")
        h_ready, xv_evac = sem("h_ready"), sem("xv_evac")
        row_ready, sa_clear = sem("row_ready"), sem("sa_clear")
        s_done, s_shift, p_exp, p_ready, pt_done, pt_evac, o_done, o_evac, sa_read = (sem(n) for n in (
            "s_done", "s_shift", "p_exp", "p_ready", "pt_done", "pt_evac", "o_done", "o_evac", "sa_read"))
        f_ready, lf_ready, scanned, e_in, e_out, x_ready, gram_done, gram_read = (sem(n) for n in (
            "f_ready", "lf_ready", "scanned", "e_in", "e_out", "x_ready", "gram_done", "gram_read"))
        dec_out, kd_in, kd_out, kd_ready, kdt_done, kdt_evac, u_done, st_ready, ho_done, sq_ready, ms_done, head_out = (
            sem(n) for n in ("dec_out", "kd_in", "kd_out", "kd_ready", "kdt_done", "kdt_evac", "u_done", "st_ready",
                             "ho_done", "sq_ready", "ms_done", "head_out"))
        mix_done, mix_read, xr_in, r_in, n2_ready, n2_out, t2_done, t2_evac, rt_done, rt_read = (
            sem("mix_done"), sem("mix_read"), [sem("xr_in0"), sem("xr_in1")], sem("r_in"), sem("n2_ready"),
            [sem("n2_out0"), sem("n2_out1")], sem("t2_done"), sem("t2_evac"), sem("rt_done"), sem("rt_read"))
        pads_ready = sem("pads_ready")
        rexp_in, rexp_out, onehots, ranked, slots_ready, table_done, table_ready, plan_ready, rows_ready = (sem(n) for n in (
            "rexp_in", "rexp_out", "onehots", "ranked", "slots_ready", "table_done", "table_ready", "plan_ready", "rows_ready"))
        w1_in, w3_in, w2_in = ([sem(f"{n}_in{b}") for b in range(3)] for n in ("w1", "w3", "w2"))
        pick_ready = sem("pick_ready")
        xg_in, xg_t, xT_evac = sem("xg_in"), sem("xg_t"), sem("xT_evac")
        gu_done = [sem("gu_done0"), sem("gu_done1")]
        hid_ready, ht_evac = [sem("hid_ready0"), sem("hid_ready1")], [sem("ht_evac0"), sem("ht_evac1")]
        silu_out, ht_done, y_done, y_scaled, y_out = (sem(n) for n in ("silu_out", "ht_done", "y_done", "y_scaled", "y_out"))
        blocks_out, ys_in = sem("blocks_out"), [sem(f"ys_in{t}") for t in range(NT)]
        fin_rows, x2_scaled = sem("fin_rows"), sem("x2_scaled")
        last_ready = sem("last_ready")
        diag_ready, combined, sum_read = sem("diag_ready"), sem("combined"), sem("sum_read")
        nmr_ready, applied, gained, fin_ready, fin_out = (sem(n) for n in ("nmr_ready", "applied", "gained", "fin_ready", "fin_out"))
        v_chain, a_chain = sem("v_chain"), sem("a_chain")

        held = {0: ["ada0", "kv", "wo0"], 1: ["ada1", "aq", "hq"], 2: ["ada2", "hi", "hg"],
                3: ["ada3", "ada4", "ada6", "ada8", "ada10", "hf", "wo1"], 4: ["ada5", "ada7", "ada9", "ada11"]}
        place = {n: (s, i + 1) for s, names in held.items() for i, n in enumerate(names)}
        W_COL = {"hq": 0, "hf": 512, "hi": 1024, "hg": 1536, "aq": 2048, "kv": 2560}
        Z0 = 10
        Z_ALL = Z0 + 3 * UNITS

        SETS = 3
        W1, W3, W2 = [slot(1), slot(3), late[0]], [slot(2), slot(4), late[1]], [slot(0), slot(5), late[2]]

        def arrived(eng, name):
            s, n = place[name]
            eng.wait_ge(piece_in[s], 16 * n)

        def view(name, n=512):
            return slot(place[name][0])[:, 0:KD * n].rearrange("p (k f) -> p k f", k=KD)

        def halves(buf, w):
            v = buf.rearrange("p (n two w) -> p n two w", two=2, w=w)
            return v[:, :, 0, :], v[:, :, 1, :]

        w_in_v = w_in[0].rearrange("(p k) n -> p k n", p=P)
        ada_v = ada_w[0].rearrange("(p k) n -> p k n", p=P)

        block = ctx.enter_context(nc.Block())

        @block.sync
        def _(sp):
            def load(name, src, dst):
                s, n = place[name]
                sp.dma_start(dst, src).then_inc(piece_in[s], 16)

            def load_ada(n):
                load(f"ada{n}", ada_v[:, :, n * 512:(n + 1) * 512], view(f"ada{n}"))

            def load_z(name, n=512):
                load(name, w_in_v[:, :, W_COL[name]:W_COL[name] + n], view(name, n))

            for n in range(4):
                for t in (2 * n, 2 * n + 1):
                    sp.dma_start(xin[t], x[0, t * P:(t + 1) * P, :]).then_inc(x_in[t], 16)
                if n == 1:
                    sp.wait_ge(rows_in, 16 * 6)
                load_ada(n)
            sp.wait_ge(ada_summed, 1)
            load_z("kv", 256)
            sp.wait_ge(ada_summed, 2)
            load_z("aq")
            sp.wait_ge(ada_summed, 3)
            load_z("hi")
            sp.wait_ge(ada_summed, 4)
            load_ada(4)
            sp.wait_ge(xn_ready, NT)
            load_ada(5)
            for n in range(6, 12):
                sp.wait_ge(ada_summed, n - 1)
                load_ada(n)
            sp.wait_ge(z_done, Z0)
            load_z("hq")
            sp.wait_ge(ada_summed, 11)
            load_z("hf")
            sp.wait_ge(v_done, NT)
            load_z("hg")
            load("wo0", w_out[0, 0:512, :].rearrange("(m p) n -> p m n", p=P), slot(0).rearrange("p (m n) -> p m n", m=4))
            sp.wait_ge(z_done, Z_ALL - 2)
            wo1 = slot(3).rearrange("p (m n) -> p m n", m=4)
            for g in range(KVH):
                rows = w_out[0, 512 + g * 256:768 + g * 256, :].rearrange("(j p) n -> p j n", p=DH)
                sp.dma_start(wo1[g * DH:(g + 1) * DH, :, :], rows).then_inc(piece_in[3], 16)

            def load_gate_up(b, e):
                sp.dma_start(W1[b], w1[0][e].rearrange("o (p k) f -> (o p) (k f)", p=P)).then_inc(w1_in[b], 16)
                sp.dma_start(W3[b], w3[0][e].rearrange("o (p k) f -> (o p) (k f)", p=P)).then_inc(w3_in[b], 16)

            def load_down(b, e):
                sp.dma_start(W2[b].rearrange("p (k f) -> p k f", k=4),
                             w2[0][e].rearrange("o (k p) f -> (o p) k f", p=P)).then_inc(w2_in[b], 16)

            sp.wait_ge(z_done, Z_ALL)
            load_gate_up(0, slice(0, 1))
            sp.wait_ge(mix_done, NT)
            load_down(0, slice(0, 1))
            load_gate_up(1, slice(1, 2))
            load_down(1, slice(1, 2))
            sp.wait_ge(rows_ready, 1)
            for b in range(2):
                sp.wait_ge(n2_out[b], 16 * NT // 2)
            load_gate_up(2, slice(2, 3))
            sp.wait_ge(w1_in[2], 16)
            load_down(2, slice(2, 3))

            def load_expert(b, e, turn):
                last = sp.value_load(bendi[0:1, bass.ds(e - SETS, 1)], min_val=1, max_val=MAX_BLOCKS)
                sp.wait_ge(w3_in[b - 1], turn * 16 + (16 if b else 0))
                sp.wait_ge(gu_done[1], last)
                load_gate_up(b, bass.ds(e, 1))
                sp.wait_ge(w1_in[b], turn * 16 + 16)
                sp.wait_ge(y_done, last)
                load_down(b, bass.ds(e, 1))

            with sp.Fori(1, NE // SETS) as i:
                for b in range(SETS):
                    load_expert(b, i * SETS + b, i)
            for e in range(NE // SETS * SETS, NE):
                load_expert(e % SETS, e, e // SETS)

            for t in range(NT):
                if t < NT - 1:
                    sp.wait_ge(fin_ready, t + 1)
                else:
                    sp.wait_ge(last_ready, 1)
                sp.dma_start(out[0, t * P:(t + 1) * P, :], ya[t]).then_inc(fin_out, 16)
            sp.wait_ge(fin_out, 16 * NT)

        @block.gpsimd
        def _(pool):
            nc.gpsimd.memset(ones[:], 1.0).then_inc(set_up, 1)
            nc.gpsimd.memset(keep[:], 1.0).then_inc(filled, 1)
            nc.gpsimd.memset(slot_tok[:, MAX_BLOCKS:], 0).then_inc(set_up, 1)
            nc.gpsimd.memset(eps, EPS)
            nc.gpsimd.memset(mean[:], 1.0 / P).then_inc(set_up, 1)
            pool.wait_ge(filled, 1)
            nc.gpsimd.memset(keep[:].rearrange("p (c s) -> p c s", s=CHUNK)[:, :, 0:1], 0.0).then_inc(set_up, 1)
            pool.wait_ge(set_up, 4)
            pool.wait_ge(trep_read, AH)
            pool.dma_start(diffs_d, trep).then_inc(diffs_out, 16)
            pool.wait_ge(diffs_out, 16)
            skewed = bass.AP(tensor=diffs_d.tensor, offset=P - 1, ap=[[AH * DIFFS - 1, P], [DIFFS, AH], [1, BAND]])
            pool.dma_start(bias, skewed).then_inc(bias_in, 16)
            for r in range(4):
                pool.wait_ge(row_ready, r + 1)
                pool.dma_start(gates_d[r // 2:r // 2 + 1, (r % 2) * 512:(r % 2 + 1) * 512], rowbuf[0:1, :]).then_inc(row_out, 16)
            for b in range(2):
                pool.wait_ge(n2_out[b], 16 * NT // 2)

            def gather():
                nc.gpsimd.indirect_dma_start(
                    out=xg[0:BLK, :], out_offset=None, in_=n2_d,
                    in_offset=bass.IndirectOffsetOnAxis(ap=pick[0:BLK, 0:1], axis=0)).then_inc(xg_in, 16)

            pool.wait_ge(plan_ready, 1)
            total = pool.value_load(bendi[0:1, NE - 1:NE], min_val=1, max_val=MAX_BLOCKS)
            picks = pool.alloc_register("picks")
            pool.reg_mov(picks, 2)
            pool.wait_ge(table_ready, 1)
            nc.gpsimd.tensor_copy(pick[0:BLK], slot_tok[0:BLK, 0:1]).then_inc(pick_ready, 1)
            pool.wait_ge(pick_ready, 1)
            gather()
            with pool.Fori(0, total) as j:
                pool.wait_ge(xg_t, j + 1)
                nc.gpsimd.tensor_copy(pick[0:BLK], slot_tok[0:BLK, bass.ds(j + 1, 1)]).then_inc(pick_ready, 1)
                pool.wait_ge(pick_ready, picks)
                pool.reg_add(picks, picks, 1)
                gather()

            pool.wait_ge(blocks_out, 1)
            for t in range(NT):
                for ch, buf in enumerate((ya, yb)):
                    nc.gpsimd.indirect_dma_start(
                        out=buf[t], out_offset=None, in_=y_d,
                        in_offset=bass.IndirectOffsetOnAxis(ap=yrowi[:, ch, t:t + 1], axis=0)).then_inc(ys_in[t], 16)
            pool.wait_ge(fin_rows, 16 * 4)
            for t in range(NT - 1):
                pool.wait_ge(gained, t + 1)
                nc.gpsimd.tensor_tensor(ya[t], ya[t], b2, ALU.add).then_inc(fin_ready, 1)

        @block.scalar
        def _(act):
            n_link = [0]

            def link(ins):
                n_link[0] += 1
                ins.then_inc(a_chain, 1)
                act.wait_ge(a_chain, n_link[0])

            n_norm = [0]

            def root(s):
                n_norm[0] += 1
                act.wait_ge(var_ready, n_norm[0])
                link(nc.scalar.activation(rstd[:, s, :], mv[:, s, 1:2], ACT.Ln, bias=eps))
                nc.scalar.activation(rstd[:, s, :], rstd[:, s, :], ACT.Exp, scale=-0.5).then_inc(rstd_ready, 1)

            def evac_x(t):
                act.wait_ge(xt_done, t + 1)
                nc.scalar.activation(hT[:, 0:4, t * P:(t + 1) * P],
                                     bank(4 + 2 * (t % 2)).rearrange("p (k t) -> p k t", k=4), ACT.Copy).then_inc(xt_evac, 1)

            def sigmoid(z, col, dst, sem_out):
                act.wait_ge(z_done, z + 1)
                nc.scalar.activation(dst, bank(z % 2), ACT.Exp, bias=nbcols[:, col:col + 1], scale=-1.0).then_inc(z_act, 1)
                act.wait_ge(z_act, z + 1)
                link(nc.scalar.activation(dst, dst, ACT.Ln, bias=ones[:, 0:1]))
                nc.scalar.activation(dst, dst, ACT.Exp, scale=-1.0).then_inc(sem_out, 1)

            nc.scalar.preload_act_table_set("natural_log_exp_and_others")
            act.dma_start(cond[:], c.rearrange("o (p k) -> (o p) k", p=P)).then_inc(cond_in, 16)
            act.dma_start(cf[:], c_f32).then_inc(consts_in, 16)
            act.dma_start(wide_masks, c_masks).then_inc(consts_in, 16)
            act.dma_start(onehot[0:32, :], c_onehot).then_inc(consts_in, 16)
            for kind in (0, 1, 3, 4):
                act.dma_start(adac[:, kind, :], ada_b[0, kind * D:(kind + 1) * D].rearrange("(p k) -> p k", p=P)).then_inc(cols_in, 16)
            act.dma_start(bcols, b_in_cols).then_inc(cols_in, 16)
            act.dma_start(lowc, hg_lower_cols.rearrange("p (r h) -> p r h", r=2)).then_inc(cols_in, 16)
            act.dma_start(norm, hg_norm[0].rearrange("(p o) -> p o", o=1)).then_inc(cols_in, 16)
            act.dma_start(sink, attn_sinks.broadcast_to([P, AH])).then_inc(rows_in, 16)
            act.dma_start(hirow, b_in_row[:, 0:HALF].broadcast_to([P, HALF])).then_inc(rows_in, 16)
            act.dma_start(carry, b_in_row[:, HALF:640].broadcast_to([P, P])).then_inc(rows_in, 16)
            act.dma_start(rel_src[0:32], rel_bias).then_inc(rows_in, 16)
            for i, kind in enumerate((2, 5)):
                act.dma_start(adarow[0:1, i * D:(i + 1) * D], ada_b[0:1, kind * D:(kind + 1) * D]).then_inc(rows_in, 16)
            act.wait_ge(set_up, 4)
            act.wait_ge(cond_in, 16)
            link(nc.scalar.activation(ecols[:, 0, :], cond[:], ACT.Exp, scale=-1.0))
            link(nc.scalar.activation(ecols[:, 0, :], ecols[:, 0, :], ACT.Ln, bias=ones[:, 0:1]))
            nc.scalar.activation(ecols[:, 0, :], ecols[:, 0, :], ACT.Exp, scale=-1.0).then_inc(cond_e, 1)
            for t in range(3):
                root(t % 2)
            act.wait_ge(cols_in, 16 * 7)
            for t in range(NT):
                evac_x(t)
                if t + 3 < NT:
                    root((t + 3) % 2)
            act.wait_ge(mod_taken, 2)
            act.wait_ge(xt_evac, NT)
            for k in range(4):
                last = nc.scalar.activation(hT[:, k, :], hT[:, k, :], ACT.Identity, bias=modc[:, 0, k:k + 1], scale=modc[:, 1, k:k + 1])
            last.then_inc(h_ready, 1)
            for z in range(Z0):
                act.wait_ge(z_done, z + 1)
                half = z % 2
                dst = kT[:, half * HALF:(half + 1) * HALF] if z < 2 else mixT[:, 4 + (z - 2) // 2, half * HALF:(half + 1) * HALF]
                col = 20 if z < 2 else 16 + (z - 2) // 2
                if z == 1:
                    act.wait_ge(lowexp, 1)
                    nc.scalar.activation(lowc, lowc, ACT.Exp).then_inc(lowexp, 1)
                nc.scalar.activation(dst, bank(z % 2), ACT.Identity, bias=bcols[:, col:col + 1]).then_inc(z_act, 1)

            def attn_exp(n):
                act.wait_ge(s_shift, n + 1)
                lo = CHUNK if n < 2 else 0
                v = sa_all[n % 2][:, 64:].rearrange("p (h k) -> p h k", h=GRP)[:, :, lo:]
                nc.scalar.activation(v, v, ACT.Exp)
                nc.scalar.activation(esink[:, n % 2, :], esink[:, n % 2, :], ACT.Exp).then_inc(p_exp, 1)

            def attn_evac(n):
                i, g = n // 2, n % 2
                act.wait_ge(pt_done, n + 1)
                last = nc.scalar.activation(pto, bank(4), ACT.Copy)
                if i:
                    last = nc.scalar.activation(ptp[CHUNK:P, :], bank(5)[CHUNK:P, 0:GRP * CHUNK], ACT.Copy)
                last.then_inc(pt_evac, 1)

            def attn_out(n):
                i, g = n // 2, n % 2
                act.wait_ge(o_done, n + 1)
                nc.scalar.activation(mixT[g * DH:(g + 1) * DH, 4:8, i * P:(i + 1) * P],
                                     bank(4)[g * DH:(g + 1) * DH, :].rearrange("p (j t) -> p j t", j=GRP),
                                     ACT.Copy).then_inc(o_evac, 1)

            def exp_level(u, lv):
                act.wait_ge(e_in, 6 * u + lv + 1)
                nc.scalar.activation(ebuf[lv % 2], ebuf[lv % 2], ACT.Exp).then_inc(e_out, 1)

            def gate_z(n):
                period, which = n // 3, n % 3
                h, half = period // 2, period % 2
                dst = (sg, qbuf[period % 2], mixT[:, h, half * HALF:(half + 1) * HALF])[which]
                if which == 0 and period:
                    act.wait_ge(f_ready, period)
                if which == 1 and period >= 2:
                    act.wait_ge(gram_read, 7 * (period - 1))
                sigmoid(Z0 + n, (4, 0, 12)[which] + h, dst, z_sig)

            act.wait_ge(row_out, 16 * 4)
            for n in range(16):
                if n >= 2:
                    attn_evac(n - 2)
                attn_exp(n)
                if n >= 2:
                    attn_out(n - 2)
            for n in (14, 15):
                attn_evac(n)
                attn_out(n)

            def rms_root(u):
                act.wait_ge(ms_done, u + 1)
                link(nc.scalar.activation(rms, bank(7), ACT.Ln, bias=eps))
                nc.scalar.activation(rms, rms, ACT.Exp, scale=-0.5).then_inc(rms_ready, 1)

            for period in range(UNITS + 1):
                u = period - 1
                for part3 in range(3):
                    n = 3 * period + part3
                    if 1 <= n <= 3 * UNITS:
                        gate_z(n - 1)
                    if u < 0:
                        continue
                    if part3 == 0:
                        act.wait_ge(f_ready, u + 1)
                        nc.scalar.activation(ebuf[1], fbuf, ACT.Ln).then_inc(lf_ready, 1)
                        act.wait_ge(scanned, u + 1)
                        if u:
                            act.wait_ge(ho_done, u)
                            act.wait_ge(st_ready, u)
                        nc.scalar.activation(qdec, bcum, ACT.Exp)
                        nc.scalar.activation(eblast, bcum.rearrange("p (c s) -> p c s", s=CHUNK)[:, :, CHUNK - 1:CHUNK].rearrange("p c o -> p (c o)"),
                                             ACT.Exp).then_inc(dec_out, 1)
                        exp_level(u, 0)
                        act.wait_ge(kd_in, u + 1)
                        nc.scalar.activation(kdec, kdec, ACT.Exp).then_inc(kd_out, 1)
                        exp_level(u, 1)
                        if u:
                            rms_root(u - 1)
                        for lv in (2, 3):
                            exp_level(u, lv)
                        act.wait_ge(kdt_done, u + 1)
                        nc.scalar.activation(kdT, bank(2), ACT.Copy).then_inc(kdt_evac, 1)
                    elif part3 == 1:
                        for lv in (4, 5):
                            exp_level(u, lv)
                    else:
                        act.wait_ge(ho_done, u + 1)
                        nc.scalar.activation(sq, bank(6), ACT.Square).then_inc(sq_ready, 1)
            rms_root(UNITS - 1)

            act.wait_ge(head_out, UNITS)
            act.wait_ge(row_out, 16 * 4)
            for dst, src in ((gt1, gates_d[0:1, :]), (g1, ln1_g), (b1, ln1_b)):
                act.dma_start(dst, src.broadcast_to([P, D])).then_inc(r_in, 16)
            for t in range(2):
                act.dma_start(xr[t], x[0, t * P:(t + 1) * P, :]).then_inc(xr_in[t], 16)
            act.dma_start(wr[:, :, 0:NG], w_group[0].rearrange("(p k) n -> p k n", p=P)).then_inc(r_in, 16)
            act.dma_start(wr[:, :, NG:36], w_sub[0].rearrange("(p k) n -> p k n", p=P)).then_inc(r_in, 16)
            act.dma_start(br[:, 0:NG], b_group.broadcast_to([P, NG])).then_inc(r_in, 16)
            act.dma_start(br[:, NG:36], b_sub.broadcast_to([P, NE])).then_inc(r_in, 16)
            for t in range(NT):
                root(0)
                root(1)
                act.wait_ge(n2_ready, t + 1)
                act.dma_start(n2_d[t * P:(t + 1) * P, :], rbuf[t % 2]).then_inc(n2_out[t % 2], 16)
                if t + 2 < NT:
                    act.dma_start(xr[t % 2], x[0, (t + 2) * P:(t + 3) * P, :]).then_inc(xr_in[t % 2], 16)
                act.wait_ge(t2_done, t + 1)
                if t >= 2:
                    act.wait_ge(rt_done, t - 1)
                for k in range(KD):
                    last = nc.scalar.activation(h2T[t % 2][:, k * P:(k + 1) * P], bank(4, 2)[:, k * P:(k + 1) * P],
                                                ACT.Identity, bias=modc[:, 3, k:k + 1], scale=modc[:, 4, k:k + 1])
                last.then_inc(t2_evac, 1)
                nc.scalar.activation(x2[:, t, :], x2[:, t, :], ACT.Copy, scale=ALPHA).then_inc(x2_scaled, 1)
            act.wait_ge(rexp_in, 1)
            nc.scalar.activation(gexp, gexp, ACT.Exp).then_inc(rexp_out, 1)
            act.wait_ge(rexp_in, 2)
            nc.scalar.activation(ex, ex, ACT.Exp).then_inc(rexp_out, 1)

            act.dma_start(g2, ln2_g.broadcast_to([P, D])).then_inc(fin_rows, 16)
            for half in range(2):
                act.dma_start(gt2[half * BLK:(half + 1) * BLK, :],
                              gates_d[1:2, half * HALF:(half + 1) * HALF].broadcast_to([BLK, HALF])).then_inc(fin_rows, 16)
            act.wait_ge(fin_rows, 16 * 3)
            act.dma_start(y_d[2 * T:2 * T + BLK, :].rearrange("r (h c) -> (r h) c", h=2), gt2).then_inc(y_out, 16)

            def evac_block(count):
                act.wait_ge(xg_t, count)
                for k in range(KD):
                    last = nc.scalar.activation(xT[:, k * BLK:(k + 1) * BLK], bank(0)[:, k * BLK:(k + 1) * BLK],
                                                ACT.Identity, bias=modc[:, 3, k:k + 1], scale=modc[:, 4, k:k + 1])
                last.then_inc(xT_evac, 1)

            nc.scalar.preload_act_table(ACT.Silu)
            evac_block(1)
            act.wait_ge(rows_ready, 1)
            total = act.value_load(bendi[0:1, NE - 1:NE], min_val=1, max_val=MAX_BLOCKS)
            with act.Fori(0, total) as j:
                row = act.value_load(row0i[0:1, bass.ds(j, 1)], min_val=0, max_val=2 * T)
                for half in range(2):
                    f = slice(half * 2 * P, (half + 1) * 2 * P)
                    act.wait_ge(gu_done[half], j + 1)
                    nc.scalar.activation(sl[BLK:P, f], bank(2 + half)[0:BLK, 0:2 * P], ACT.Silu).then_inc(silu_out, 1)
                evac_block(j + 2)
                act.wait_ge(y_scaled, j + 2)
                for half in range(2):
                    act.dma_start(y_d[bass.ds(row, BLK), half * HALF:(half + 1) * HALF],
                                  yo[half * BLK:(half + 1) * BLK, :]).then_inc(y_out, 16)
            act.wait_ge(blocks_out, 1)
            act.dma_start(b2, ln2_b.broadcast_to([P, D])).then_inc(fin_rows, 16)
            nc.scalar.preload_act_table_set("natural_log_exp_and_others")
            for t in range(NT + 1):
                if t < NT:
                    root(t % 2)
                if t:
                    act.wait_ge(nmr_ready, t)
                    nc.scalar.activation(ya[t - 1], ya[t - 1], ACT.Identity, bias=nmr[:, (t - 1) % 2, :],
                                         scale=rstd[:, (t - 1) % 2, :]).then_inc(applied, 1)

        @block.vector
        def _(dve):
            n_link = [0]

            def link(ins):
                n_link[0] += 1
                ins.then_inc(v_chain, 1)
                dve.wait_ge(v_chain, n_link[0])

            V = nc.vector
            n_norm = [0]

            def normalise(src, dst, s, done=None):
                V.bn_stats(stats[:, s, 0:6], src[:, 0:512])
                link(V.bn_stats(stats[:, s, 6:12], src[:, 512:1024]))
                V.bn_aggr(mv[:, s, :], stats[:, s, :]).then_inc(var_ready, 1)
                n_norm[0] += 1
                dve.wait_ge(var_ready, n_norm[0])
                dve.wait_ge(rstd_ready, n_norm[0])
                ins = V.tensor_scalar(dst, src, mv[:, s, 0:1], rstd[:, s, :], ALU.subtract, ALU.mult)
                if done is None:
                    link(ins)
                else:
                    ins.then_inc(done, 1)

            def norm_stats(t):
                dve.wait_ge(x_in[t], 16)
                V.bn_stats(stats[:, t % 2, 0:6], xin[t][:, 0:512])
                link(V.bn_stats(stats[:, t % 2, 6:12], xin[t][:, 512:1024]))
                V.bn_aggr(mv[:, t % 2, :], stats[:, t % 2, :]).then_inc(var_ready, 1)
                n_norm[0] += 1

            def norm_apply(t):
                dve.wait_ge(rstd_ready, t + 1)
                if t >= 2:
                    dve.wait_ge(xt_done, t - 1)
                V.tensor_scalar(xn[t % 2], xin[t], mv[:, t % 2, 0:1], rstd[:, t % 2, :], ALU.subtract, ALU.mult).then_inc(xn_ready, 1)
                dve.wait_ge(xn_ready, t + 1)

            def ada_sum(n):
                arrived(dve, f"ada{n}")
                if n >= 2:
                    dve.wait_ge(mod_done, n - 1)
                a, w = acc[n % 2], view(f"ada{n}")
                link(V.tensor_scalar(a, w[:, 0, :], cond[:, 0:1], None, ALU.mult))
                for k in range(1, KD):
                    ins = V.scalar_tensor_tensor(a, w[:, k, :], cond[:, k:k + 1], a, ALU.mult, ALU.add)
                    if k < KD - 1:
                        link(ins)
                ins.then_inc(ada_summed, 1)

            def take_row(r):
                dve.wait_ge(mod_done, (5, 6, 11, 12)[r])
                if r:
                    dve.wait_ge(row_out, 16 * r)
                V.tensor_copy(rowbuf, bank(3)).then_inc(row_ready, 1)

            def evac_x(t):
                dve.wait_ge(xt_done, t + 1)
                V.tensor_copy(hT[:, 4:8, t * P:(t + 1) * P], bank(5 + 2 * (t % 2)).rearrange("p (k t) -> p k t", k=4)).then_inc(xv_evac, 1)

            def lower_bounds():
                dve.wait_ge(cols_in, 16 * 7)
                link(V.tensor_tensor(lowd, lowc[:, 0, :], lowc[:, 1, :], ALU.max))
                V.tensor_tensor(lowc, lowc, lowd[:, None, :].broadcast_to([P, 2, HEADS]), ALU.subtract).then_inc(lowexp, 1)
                dve.wait_ge(lowexp, 2)
                link(V.tensor_tensor(lowd, lowc[:, 0, :], lowc[:, 1, :], ALU.add))
                link(V.reciprocal(lowd, lowd))
                link(V.tensor_tensor(lb, lowc[:, 0, :], lowd, ALU.mult))
                link(V.tensor_scalar(oml, lb, -1.0, 1.0, ALU.mult, ALU.add))
                link(V.tensor_scalar(nbcols, bcols, -1.0, None, ALU.mult))

            def take_mod(n):
                kind, half = n // 2, n % 2
                if n == 0:
                    dve.wait_ge(consts_in, 16 * 3)
                    dve.wait_ge(cols_in, 16 * 7)
                dve.wait_ge(mod_done, n + 1)
                link(V.tensor_tensor(acc[half].rearrange("p (g k) -> p g k", k=KD),
                                     bank(2 + half).rearrange("p (g k) -> p g k", k=KD),
                                     ident[:, half * 64:(half + 1) * 64, None].broadcast_to([P, 64, KD]), ALU.mult))
                V.tensor_reduce(mods[:, half, :], acc[half].rearrange("p (g k) -> p k g", k=KD), AX.X, ALU.add).then_inc(ada_summed, 1)
                if half:
                    dve.wait_ge(ada_summed, n + 1)
                    link(V.tensor_tensor(modc[:, kind, :], mods[:, 0, :], mods[:, 1, :], ALU.add))
                    V.scalar_tensor_tensor(modc[:, kind, :], modc[:, kind, :], float(kind), adac[:, kind, :], ALU.add, ALU.add).then_inc(mod_taken, 1)

            dve.wait_ge(cond_in, 16)
            dve.wait_ge(cond_e, 1)
            link(V.tensor_tensor(cond[:], cond[:], ecols[:, 0, :], ALU.mult))
            V.tensor_copy(cond_wide, cond[:, :, None].broadcast_to([P, KD, P])).then_inc(cond_ready, 1)
            norm_stats(0)
            norm_stats(1)
            for t in range(2):
                dve.wait_ge(var_ready, t + 1)
                norm_apply(t)
                if t == 0:
                    norm_stats(2)
            dve.wait_ge(rows_in, 16 * 6)
            V.tensor_copy(relb[0:32, :].rearrange("b (h m) -> b h m", h=AH),
                          rel_src[0:32, :, None].broadcast_to([32, AH, P])).then_inc(rel_rows, 1)
            for n in range(4):
                take_mod(n)
                for t in (2 * n, 2 * n + 1):
                    evac_x(t)
                    if t + 3 < NT:
                        norm_stats(t + 3)
                    if t + 2 < NT:
                        dve.wait_ge(var_ready, t + 3)
                        norm_apply(t + 2)
                for h in (2 * n, 2 * n + 1):
                    dve.wait_ge(trep_done, h + 1)
                    V.tensor_copy(trep[:, h, :], bank(h % 2)[:, 0:DIFFS]).then_inc(trep_read, 1)
            dve.wait_ge(mod_taken, 2)
            dve.wait_ge(xv_evac, NT)
            for k in range(4, KD):
                ins = V.tensor_scalar(hT[:, k, :], hT[:, k, :], modc[:, 1, k:k + 1], modc[:, 0, k:k + 1], ALU.mult, ALU.add)
            ins.then_inc(h_ready, 1)
            V.tensor_copy(masks[:], wide_masks)
            lower_bounds()
            dve.wait_ge(bias_in, 16)
            V.memset(bias[0:CHUNK, :, P:BAND], NEG)
            V.memset(bias[CHUNK:P, :, 0:CHUNK], NEG).then_inc(bias_ready, 1)
            row = 0
            for n in range(4, 12):
                ada_sum(n)
                if n in (4, 5, 10, 11):
                    take_row(row)
                    row += 1
            V.memset(sa_all[0][:, 0:64], 0.0)
            V.memset(sa_all[1][:, 0:64], 0.0).then_inc(sa_clear, 1)
            V.scalar_tensor_tensor(modc[:, 3, :], bank(2)[:, 3 * KD:4 * KD], 0.0, adac[:, 3, :], ALU.add, ALU.add)
            V.scalar_tensor_tensor(modc[:, 4, :], bank(2)[:, 4 * KD:5 * KD], 1.0, adac[:, 4, :], ALU.add, ALU.add).then_inc(mod_read, 1)
            dve.wait_ge(sa_clear, 1)
            dve.wait_ge(bias_ready, 1)

            def attn_shift(n):
                i, g = n // 2, n % 2
                lo = CHUNK if i == 0 else 0
                v = sa_all[n % 2][:, 64:].rearrange("p (h k) -> p h k", h=GRP)[:, :, lo:]
                src = bank(2, 2).rearrange("p (h k) -> p h k", h=GRP)[:, :, lo:BAND]
                dve.wait_ge(s_done, n + 1)
                if n >= 2:
                    dve.wait_ge(pt_done, n - 1)
                V.scalar_tensor_tensor(v, src, DH ** -0.5, bias[:, g * GRP:(g + 1) * GRP, lo:], ALU.mult, ALU.add).then_inc(sa_read, 1)
                dve.wait_ge(sa_read, n + 1)
                link(V.tensor_reduce(mx[:, n % 2, :], v, AX.X, ALU.max))
                link(V.tensor_tensor(mx[:, n % 2, :], mx[:, n % 2, :], sink[:, g * GRP:(g + 1) * GRP], ALU.max))
                V.tensor_tensor(v, v, mx[:, n % 2, :, None].broadcast_to([P, GRP, BAND - lo]), ALU.subtract)
                V.tensor_tensor(esink[:, n % 2, :], sink[:, g * GRP:(g + 1) * GRP], mx[:, n % 2, :], ALU.subtract).then_inc(s_shift, 1)

            def attn_divide(n):
                i = n // 2
                lo = CHUNK if i == 0 else 0
                v = sa_all[n % 2][:, 64:].rearrange("p (h k) -> p h k", h=GRP)[:, :, lo:]
                dve.wait_ge(p_exp, n + 1)
                link(V.tensor_reduce(sums[:, n % 2, :], v, AX.X, ALU.add))
                link(V.tensor_tensor(sums[:, n % 2, :], sums[:, n % 2, :], esink[:, n % 2, :], ALU.add))
                link(V.reciprocal(rden[:, n % 2, :], sums[:, n % 2, :]))
                V.tensor_tensor(v, v, rden[:, n % 2, :, None].broadcast_to([P, GRP, BAND - lo]), ALU.mult).then_inc(p_ready, 1)

            def level_exponent(u, lv):
                w = LEVELS[lv]
                lo, hi = halves(bcum, w)
                elo, ehi = halves(ebuf[lv % 2], w)
                ref = lo[:, :, w - 1:w].broadcast_to([P, HALF // (2 * w), w])
                if lv == 1:
                    dve.wait_ge(scanned, u + 1)
                V.tensor_tensor(elo, ref, lo, ALU.subtract)
                V.tensor_tensor(ehi, hi, ref, ALU.subtract).then_inc(e_in, 1)

            def level_factors(u, lv):
                w = LEVELS[lv]
                klo, _ = halves(kbuf, w)
                _, qhi = halves(qbuf[u % 2], w)
                elo, ehi = halves(ebuf[lv % 2], w)
                xlo, xhi = halves(xbuf[lv % 2], w)
                dve.wait_ge(e_out, 6 * u + lv + 1)
                if lv >= 2:
                    dve.wait_ge(gram_done, 7 * u + lv)
                V.tensor_tensor(xlo, klo, elo, ALU.mult)
                V.tensor_tensor(xhi, qhi, ehi, ALU.mult).then_inc(x_ready, 1)

            def take_gram(u, s):
                dve.wait_ge(gram_done, 7 * u + s + 1)
                g = bank(4 + s % 2)
                sc = score.rearrange("p (i t) -> p i t", i=4)
                if s == 0:
                    if u:
                        dve.wait_ge(ho_done, u)
                    V.tensor_tensor(sc, g.rearrange("p (i t) -> p i t", i=4), ident[:, None, :].broadcast_to([P, 4, P]), ALU.mult).then_inc(gram_read, 1)
                else:
                    dve.wait_ge(gram_read, 7 * u + s)
                    w = LEVELS[s - 1]
                    V.copy_predicated(sc.rearrange("p i (n two w) -> p i n two w", two=2, w=w)[:, :, :, 1, :],
                                      masks[:, s * P:(s + 1) * P].rearrange("p (n two w) -> p n two w", two=2, w=w)[:, None, :, 1, :]
                                      .broadcast_to([P, 4, P // 2 // w, w]),
                                      g[:, 0:2 * P].rearrange("p (i n w) -> p i n w", i=4, w=w)).then_inc(gram_read, 1)

            def gate_z(n):
                z, ph, phalf = Z0 + n, n // 6, (n // 3) % 2
                dst = qbuf[phalf] if n % 3 == 1 else mixT[:, ph, phalf * HALF:(phalf + 1) * HALF]
                col = (0 if n % 3 == 1 else 12) + ph
                dve.wait_ge(z_sig, n + 1)
                V.scalar_tensor_tensor(dst, bank(z % 2), bcols[:, col:col + 1], dst, ALU.add, ALU.mult).then_inc(z_dve, 1)

            for i in range(NT):
                attn_shift(2 * i)
                if i:
                    attn_divide(2 * i - 1)
                attn_shift(2 * i + 1)
                attn_divide(2 * i)
                dve.wait_ge(v_done, i + 1)
                V.tensor_tensor(vtok[:, i, 0:512], bank(i % 2), hirow, ALU.add)
                V.tensor_tensor(vtok[:, i, 512:640], bank(6 + i % 2)[:, 0:128], carry, ALU.add).then_inc(v_evac, 1)
            attn_divide(15)

            def head_norm(u):
                dve.wait_ge(rms_ready, u + 1)
                dve.wait_ge(z_dve, 2 * u + 2)
                g = mixT[:, u // 2, (u % 2) * HALF:(u % 2 + 1) * HALF]
                V.tensor_tensor(rms, rms, bank(6), ALU.mult).then_inc(o_scaled, 1)
                dve.wait_ge(o_scaled, u + 1)
                V.scalar_tensor_tensor(g, g, norm[:, 0:1], rms, ALU.mult, ALU.mult).then_inc(head_out, 1)

            def carry_states(u):
                dve.wait_ge(u_done, u + 1)
                if u:
                    dve.wait_ge(ho_done, u)
                upd = bank(2, 2).rearrange("p (o c v) -> p c o v", o=2, c=4)
                if u % 2 == 0:
                    link(V.memset(state[:, 0, :], 0.0))
                else:
                    link(V.tensor_copy(state[:, 0, :], carry))
                for cc in range(7):
                    link(V.scalar_tensor_tensor(state[:, cc + 1, :], state[:, cc, :], eblast[:, cc:cc + 1], upd[:, cc // 2, cc % 2, :], ALU.mult, ALU.add))
                V.scalar_tensor_tensor(carry, state[:, 7, :], eblast[:, 7:8], upd[:, 3, 1, :], ALU.mult, ALU.add).then_inc(st_ready, 1)
                dve.wait_ge(st_ready, u + 1)

            for period in range(UNITS + 1):
                u = period - 1
                h = u // 2
                for part3 in range(3):
                    n = 3 * period + part3
                    if 1 <= n <= 3 * UNITS and (n - 1) % 3:
                        gate_z(n - 1)
                    if u < 0:
                        continue
                    if part3 == 0:
                        dve.wait_ge(z_sig, 3 * u + 1)
                        link(V.tensor_scalar(fbuf, sg, oml[:, h:h + 1], lb[:, h:h + 1], ALU.mult, ALU.add))
                        V.tensor_scalar(kbuf, fbuf, -1.0, 1.0, ALU.mult, ALU.add).then_inc(f_ready, 1)
                        dve.wait_ge(lf_ready, u + 1)
                        V.tensor_tensor_scan(bcum, keep[:], ebuf[1], 0.0, ALU.mult, ALU.add).then_inc(scanned, 1)
                        dve.wait_ge(scanned, u + 1)
                        level_exponent(u, 0)
                        b3 = bcum.rearrange("p (c s) -> p c s", s=CHUNK)
                        V.tensor_tensor(kdec.rearrange("p (c s) -> p c s", s=CHUNK),
                                        b3[:, :, CHUNK - 1:CHUNK].broadcast_to([P, 8, CHUNK]), b3, ALU.subtract).then_inc(kd_in, 1)
                        dve.wait_ge(f_ready, u + 1)
                        level_exponent(u, 1)
                        dve.wait_ge(dec_out, u + 1)
                        dve.wait_ge(z_dve, 2 * u + 1)
                        V.tensor_tensor(qdec, qdec, qbuf[u % 2], ALU.mult).then_inc(q_dec, 1)
                        level_factors(u, 0)
                        dve.wait_ge(kd_out, u + 1)
                        V.tensor_tensor(kdec, kdec, kbuf, ALU.mult).then_inc(kd_ready, 1)
                        take_gram(u, 0)
                        dve.wait_ge(x_ready, 6 * u + 1)
                        level_exponent(u, 2)
                        level_factors(u, 1)
                        if u:
                            head_norm(u - 1)
                        take_gram(u, 1)
                        dve.wait_ge(x_ready, 6 * u + 2)
                        level_exponent(u, 3)
                        level_factors(u, 2)
                        take_gram(u, 2)
                    elif part3 == 1:
                        dve.wait_ge(x_ready, 6 * u + 3)
                        level_exponent(u, 4)
                        level_factors(u, 3)
                        take_gram(u, 3)
                        dve.wait_ge(x_ready, 6 * u + 4)
                        level_exponent(u, 5)
                        carry_states(u)
                        level_factors(u, 4)
                        take_gram(u, 4)
                        level_factors(u, 5)
                        take_gram(u, 5)
                    else:
                        take_gram(u, 6)
            head_norm(UNITS - 1)

            def take_logits(t):
                dve.wait_ge(rt_done, t + 1)
                V.tensor_tensor(lg[:, t, :], bank(6 + t % 2)[:, 0:36], br, ALU.add).then_inc(rt_read, 1)
                dve.wait_ge(rt_read, t + 1)
                link(V.tensor_copy(gpad[:, t, 0:NG], lg[:, t, 0:NG]))
                link(V.max(gmax[:, t, :], gpad[:, t, :]))
                link(V.max_index(gidx[:, t, :], gmax[:, t, :], gpad[:, t, :]))
                link(V.tensor_copy(gsel[:, t:t + 1], gidx[:, t, 0:1]))
                link(V.tensor_scalar(oh4[:, t, :], iota[:, 0:NG], gsel[:, t:t + 1], None, ALU.is_equal))
                pt = prod[:, 0:NE].rearrange("p (e g) -> p e g", g=NG)
                link(V.tensor_tensor(pt, lg[:, t, NG:36].rearrange("p (g e) -> p e g", g=NG),
                                     oh4[:, t, None, :].broadcast_to([P, EPG, NG]), ALU.mult))
                link(V.tensor_reduce(e8[:, t, :], pt, AX.X, ALU.add))
                link(V.max(emax[:, t, :], e8[:, t, :]))
                link(V.max_index(eix[:, t, :], emax[:, t, :], e8[:, t, :]))
                link(V.tensor_copy(eidx[:, :, t], eix[:, t, 0:2]))
                for ch in range(2):
                    ins = V.scalar_tensor_tensor(eid[:, ch, t:t + 1], gsel[:, t:t + 1], float(EPG), eidx[:, ch, t:t + 1], ALU.mult, ALU.add)
                link(ins)
                for ch in range(2):
                    ins = V.tensor_scalar(oh[:, ch, t, :], iota[:, 0:NE], eid[:, ch, t:t + 1], None, ALU.is_equal)
                link(ins)
                link(V.tensor_tensor(ohsum[:, t, :], oh[:, 0, t, :], oh[:, 1, t, :], ALU.add))
                ins = V.tensor_tensor(before[:, t + 1, :], before[:, t, :], ohsum[:, t, :], ALU.add)
                if t < NT - 1:
                    link(ins)
                else:
                    ins.then_inc(onehots, 1)

            V.memset(before[:, 0, :], 0.0)
            V.memset(gpad, -3.0e38).then_inc(pads_ready, 1)
            dve.wait_ge(pads_ready, 1)
            dve.wait_ge(r_in, 16 * 7)
            for t in range(NT):
                dve.wait_ge(mix_done, t + 1)
                dve.wait_ge(xr_in[t % 2], 16 * (t // 2 + 1))
                if t >= 2:
                    dve.wait_ge(n2_out[t % 2], 16 * (t // 2))
                    dve.wait_ge(t2_done, t - 1)
                r = rbuf[t % 2]
                V.tensor_tensor(r, bank(2 * (t % 2), 2), gt1, ALU.mult).then_inc(mix_read, 1)
                dve.wait_ge(mix_read, t + 1)
                link(V.scalar_tensor_tensor(r, xr[t % 2], ALPHA, r, ALU.mult, ALU.add))
                normalise(r, x2[:, t, :], 0)
                link(V.tensor_tensor(x2[:, t, :], x2[:, t, :], g1, ALU.mult))
                link(V.tensor_tensor(x2[:, t, :], x2[:, t, :], b1, ALU.add))
                normalise(x2[:, t, :], r, 1, n2_ready)
                if t >= 2:
                    take_logits(t - 2)
            take_logits(NT - 2)
            take_logits(NT - 1)
            V.tensor_tensor(gexp, lg[:, :, 0:NG], gmax[:, :, 0:1].broadcast_to([P, NT, NG]), ALU.subtract).then_inc(rexp_in, 1)
            V.tensor_tensor(ex, emax[:, :, 1], emax[:, :, 0], ALU.subtract).then_inc(rexp_in, 1)
            dve.wait_ge(ranked, 1)
            link(V.tensor_copy(cnt, bank(1)[:, 0:NE]))
            link(V.tensor_tensor(counted, cnt[:, :, None].broadcast_to([P, NE, MAX_EXPERT]),
                                 thresholds[:, None, :].broadcast_to([P, NE, MAX_EXPERT]), ALU.is_gt))
            link(V.tensor_reduce(nblk, counted, AX.X, ALU.add))
            link(V.tensor_scalar(nblk, nblk, 1.0, None, ALU.max))
            link(V.tensor_tensor_scan(bend, ones[:, 0:NE], nblk, 0.0, ALU.mult, ALU.add))
            link(V.tensor_tensor_scan(cend, ones[:, 0:NE], cnt, 0.0, ALU.mult, ALU.add))
            link(V.tensor_tensor(bstart, bend, nblk, ALU.subtract))
            link(V.tensor_tensor(cend, cend, cnt, ALU.subtract))
            rank = bank(0)[:, 0:NT * NE].rearrange("p (t e) -> p t e", t=NT)
            pv = prod.rearrange("p (c t e) -> p c t e", c=2, t=NT)
            link(V.scalar_tensor_tensor(pos, bstart[:, None, :].broadcast_to([P, NT, NE]), float(BLK), rank, ALU.mult, ALU.add))
            for ch in range(2):
                ins = V.tensor_tensor(pv[:, ch], oh[:, ch], pos, ALU.mult)
            link(ins)
            link(V.tensor_reduce(slotf, pv, AX.X, ALU.add))
            link(V.tensor_copy(sloti[:], slotf))
            link(V.tensor_scalar(bitsi[:], sloti[:], BLK - 1, None, ALU.bitwise_and))
            link(V.tensor_copy(rowf, bitsi[:]))
            link(V.tensor_tensor(slotf, slotf, rowf, ALU.subtract))
            link(V.tensor_scalar(blkf, slotf, 1.0 / BLK, None, ALU.mult))
            for n in range(2 * NT):
                ch, t = n // NT, n % NT
                V.tensor_scalar(row_oh[:, n, :], iota[:, 0:BLK], rowf[:, ch, t:t + 1], None, ALU.is_equal)
                V.tensor_scalar(blk_oh[:, n, :], iota, blkf[:, ch, t:t + 1], token_id[:, t:t + 1], ALU.is_equal, ALU.mult).then_inc(slots_ready, 1)
            V.tensor_copy(nblki[0:1], nblk[0:1])
            V.tensor_copy(bendi[0:1], bend[0:1]).then_inc(plan_ready, 1)
            dve.wait_ge(table_done, 1)
            V.tensor_copy(slot_tok[0:BLK, 0:MAX_BLOCKS], bank(2)[0:BLK, 0:MAX_BLOCKS]).then_inc(table_ready, 1)
            link(V.scalar_tensor_tensor(shift, bstart, float(BLK), cend, ALU.mult, ALU.subtract))
            for ch in range(2):
                ins = V.tensor_tensor(pv[:, ch], oh[:, ch], shift[:, None, :].broadcast_to([P, NT, NE]), ALU.mult)
            link(ins)
            link(V.tensor_reduce(slotf, pv, AX.X, ALU.add))
            V.tensor_tensor(yrowi[:], sloti[:], slotf, ALU.subtract)
            link(V.scalar_tensor_tensor(padding[0:1], nblk[0:1], float(BLK), cnt[0:1], ALU.mult, ALU.subtract))
            link(V.tensor_tensor(blkcmp[0:1], iota[0:1, :, None].broadcast_to([1, MAX_BLOCKS, NE]),
                                 bend[0:1, None, :].broadcast_to([1, MAX_BLOCKS, NE]), ALU.is_ge))
            link(V.tensor_tensor(blkcmp[0:1], blkcmp[0:1], padding[0:1, None, :].broadcast_to([1, MAX_BLOCKS, NE]), ALU.mult))
            link(V.tensor_reduce(row0f[0:1], blkcmp[0:1], AX.X, ALU.add))
            link(V.scalar_tensor_tensor(row0f[0:1], iota[0:1], float(BLK), row0f[0:1], ALU.mult, ALU.subtract))
            V.tensor_copy(row0i[0:1], row0f[0:1]).then_inc(rows_ready, 1)
            dve.wait_ge(rexp_out, 2)
            link(V.tensor_reduce(psel, gexp, AX.X, ALU.add))
            link(V.tensor_scalar(den, ex, 1.0, None, ALU.add))
            link(V.tensor_tensor(den, den, psel, ALU.mult))
            link(V.reciprocal(wa, den))
            link(V.tensor_tensor(wb, wa, ex, ALU.mult))

            dve.wait_ge(fin_rows, 16 * 3)
            dve.wait_ge(plan_ready, 1)
            total = dve.value_load(bendi[0:1, NE - 1:NE], min_val=1, max_val=MAX_BLOCKS)
            dve.sem_inc(y_scaled, 1)
            with dve.Fori(0, total) as j:
                for half in range(2):
                    f = slice(half * 2 * P, (half + 1) * 2 * P)
                    dve.wait_ge(silu_out, j * 2 + 1 + half)
                    V.tensor_tensor(hid[BLK:P, f], sl[BLK:P, f], bank(2 + half)[BLK:P, 0:2 * P], ALU.mult).then_inc(hid_ready[half], 1)
                    dve.wait_ge(ht_done, j * 2 + 1 + half)
                    V.tensor_copy(hidT[:, half * P:(half + 1) * P], bank(4 + half)[:, 0:P]).then_inc(ht_evac[half], 1)
                dve.wait_ge(y_done, j + 1)
                dve.wait_ge(y_out, j * 32 + 16)
                V.tensor_tensor(yo, bank(6), gt2, ALU.mult).then_inc(y_scaled, 1)

            dve.wait_ge(y_out, total * 32 + 16)
            dve.wait_ge(xg_in, total * 16 + 16)
            V.memset(stats[:, 0, 0:1], 0.0).then_inc(blocks_out, 1)
            for t in range(NT):
                V.tensor_scalar(diag[t][:, 0:P], ident, wa[:, t:t + 1], None, ALU.mult)
                V.tensor_scalar(diag[t][:, P:2 * P], ident, wb[:, t:t + 1], None, ALU.mult).then_inc(diag_ready, 1)
            dve.wait_ge(x2_scaled, NT)
            dve.wait_ge(blocks_out, 1)

            def combine(t):
                f, s = ya[t], t % 2
                dve.wait_ge(combined, t + 1)
                V.tensor_tensor(f, bank(2 + 2 * s, 2), x2[:, t, :], ALU.add).then_inc(sum_read, 1)
                dve.wait_ge(sum_read, t + 1)
                V.bn_stats(stats[:, s, 0:6], f[:, 0:512])
                link(V.bn_stats(stats[:, s, 6:12], f[:, 512:1024]))
                if t >= 2:
                    dve.wait_ge(applied, t - 1)
                V.bn_aggr(mv[:, s, :], stats[:, s, :]).then_inc(var_ready, 1)
                n_norm[0] += 1

            def deviation(t):
                s = t % 2
                dve.wait_ge(rstd_ready, n_norm[0] - (t < NT - 1))
                V.scalar_tensor_tensor(nmr[:, s, :], mv[:, s, 0:1], -1.0, rstd[:, s, :], ALU.mult, ALU.mult).then_inc(nmr_ready, 1)

            def gain(t):
                dve.wait_ge(applied, t + 1)
                V.tensor_tensor(ya[t], ya[t], g2, ALU.mult).then_inc(gained, 1)

            for t in range(NT + 1):
                if t < NT:
                    combine(t)
                if t:
                    deviation(t - 1)
                if t >= 2:
                    gain(t - 2)
            gain(NT - 1)
            dve.wait_ge(fin_rows, 16 * 4)
            dve.wait_ge(gained, NT)
            V.tensor_tensor(ya[NT - 1], ya[NT - 1], b2, ALU.add).then_inc(last_ready, 1)

        @block.tensor
        def _(pe):
            M = nc.tensor.matmul

            def transposes(src, dst, n, step):
                v = src.rearrange("p (d k) -> p k d", k=step)
                for k in range(n):
                    last = nc.tensor.transpose(dst[:, k * P:(k + 1) * P], v[:, k, :], ident)
                return last

            def transpose_x(t):
                pe.wait_ge(xn_ready, t + 1)
                if t >= 2:
                    pe.wait_ge(xt_evac, t - 1)
                    pe.wait_ge(xv_evac, t - 1)
                transposes(xn[t % 2], bank(4 + 2 * (t % 2), 2), KD, KD).then_inc(xt_done, 1)

            def reduce_mod(n):
                pe.wait_ge(ada_summed, n + 1)
                kind, half = n // 2, n % 2
                if kind in (2, 5):
                    r = {4: 0, 5: 1, 10: 2, 11: 3}[n]
                    if r:
                        pe.wait_ge(row_ready, r)
                    M(bank(3), lhsT=ones[:], rhs=acc[n % 2], start=True, stop=False)
                    last = M(bank(3), lhsT=ones[0:1, :], rhs=adarow[0:1, r * 512:(r + 1) * 512], start=False, stop=True)
                else:
                    v = acc[n % 2].rearrange("p (m k) -> p k m", k=KD)
                    for k in range(KD):
                        last = M(bank(2)[half * 64:half * 64 + 64, kind * KD + k:kind * KD + k + 1],
                                 lhsT=v[:, k, :], rhs=ones[:, 0:1], start=True, stop=True)
                last.then_inc(mod_done, 1)

            def product_mod(n):
                if n == 0:
                    pe.wait_ge(cond_ready, 1)
                arrived(pe, f"ada{n}")
                if n >= 2:
                    pe.wait_ge(ada_summed, n - 1)
                for k in range(KD):
                    last = M(bank(2 + n % 2), lhsT=cond_wide[:, k, :], rhs=view(f"ada{n}")[:, k, :], start=(k == 0), stop=(k == KD - 1))
                last.then_inc(mod_done, 1)

            def bias_row(h):
                if h >= 2:
                    pe.wait_ge(trep_read, h - 1)
                M(bank(h % 2)[:, 0:DIFFS], lhsT=relb[0:32, h * P:(h + 1) * P], rhs=onehot[0:32, :], start=True, stop=True).then_inc(trep_done, 1)

            for n in range(4):
                product_mod(n)
                if n == 0:
                    pe.wait_ge(consts_in, 16 * 3)
                    pe.wait_ge(set_up, 4)
                transpose_x(2 * n)
                transpose_x(2 * n + 1)
                if n == 0:
                    pe.wait_ge(rows_in, 16 * 6)
                    pe.wait_ge(rel_rows, 1)
                for h in (2 * n, 2 * n + 1):
                    bias_row(h)
            pe.wait_ge(trep_read, AH)
            pe.wait_ge(h_ready, 2)
            pe.wait_ge(trep_read, AH)

            def z_free(z):
                if z >= 2:
                    pe.wait_ge(z_act, z - 1)
                    turn = z - 2 - Z0
                    if turn >= 1:
                        pe.wait_ge(z_dve, 2 * (turn // 3) + turn % 3)

            def z_steps(z, stationary, half, ks):
                for k in ks:
                    last = M(bank(z % 2), lhsT=stationary[:, k], rhs=hT[:, k, half * HALF:(half + 1) * HALF],
                             start=(k == 0), stop=(k == KD - 1))
                if ks[-1] == KD - 1:
                    last.then_inc(z_done, 1)

            for z in range(Z0):
                z_free(z)
                if z == 0:
                    arrived(pe, "kv")
                if z == 2:
                    arrived(pe, "aq")
                st = view("kv", 256)[:, :, 0:P] if z < 2 else view("aq")[:, :, (z - 2) // 2 * P:((z - 2) // 2 + 1) * P]
                z_steps(z, st, z % 2, list(range(KD)))
                if z >= 2:
                    reduce_mod(z + 2)
            pe.wait_ge(bias_ready, 1)
            pe.wait_ge(mod_read, 1)
            pe.wait_ge(row_ready, 4)

            def attn_scores(n):
                i, g = n // 2, n % 2
                pe.wait_ge(z_act, Z0)
                if n:
                    pe.wait_ge(sa_read, n)
                base, lo = g * DH, (CHUNK if i == 0 else 0)
                for j in range(GRP):
                    last = M(bank(2, 2)[:, j * 256 + lo:j * 256 + BAND],
                             lhsT=mixT[base:base + DH, 4 + j, i * P:(i + 1) * P],
                             rhs=kT[base:base + DH, i * P - CHUNK + lo:(i + 1) * P], start=True, stop=True)
                last.then_inc(s_done, 1)

            def attn_transpose(n):
                i, g = n // 2, n % 2
                pe.wait_ge(p_ready, n + 1)
                if n:
                    pe.wait_ge(o_evac, n)
                p = sa_all[n % 2]
                for j in range(GRP):
                    last = nc.tensor.transpose(bank(4)[:, j * P:(j + 1) * P], p[:, 128 + j * BAND:256 + j * BAND], ident)
                if i:
                    for j in range(GRP):
                        last = nc.tensor.transpose(bank(5)[:, j * CHUNK:(j + 1) * CHUNK], p[0:CHUNK, j * BAND:j * BAND + P],
                                                   ident[0:CHUNK, 0:CHUNK])
                last.then_inc(pt_done, 1)

            def attn_values(n):
                i, g = n // 2, n % 2
                pe.wait_ge(pt_evac, n + 1)
                pe.wait_ge(v_evac, i + 1)
                base = g * DH
                o = bank(4)[base:base + DH, :]
                last = M(o, lhsT=vtok[:, i, 512 + base:512 + base + DH], rhs=pto, start=True, stop=(i == 0))
                if i:
                    last = M(o.rearrange("p (j t) -> p j t", j=GRP)[:, :, 0:CHUNK],
                             lhsT=vtok[CHUNK:P, i - 1, 512 + base:512 + base + DH],
                             rhs=ptp[CHUNK:P, :].rearrange("p (j t) -> p j t", j=GRP), start=False, stop=True)
                last.then_inc(o_done, 1)

            def gram(u, s):
                a, b = (kbuf, qbuf[u % 2]) if s == 0 else (xbuf[(s - 1) % 2],) * 2
                if s == 0:
                    pe.wait_ge(f_ready, u + 1)
                    pe.wait_ge(z_dve, 2 * u + 1)
                else:
                    pe.wait_ge(x_ready, 6 * u + s)
                if s >= 2:
                    pe.wait_ge(gram_read, 7 * u + s - 1)
                elif u:
                    pe.wait_ge(gram_read, 7 * u)
                n = P if s == 0 else P // 2
                for i in range(4):
                    rhs = b[:, i * P:(i + 1) * P]
                    if s:
                        _, rhs = halves(rhs, LEVELS[s - 1])
                    last = M(bank(4 + s % 2)[:, i * n:(i + 1) * n], lhsT=a[:, i * P:(i + 1) * P], rhs=rhs,
                             start=True, stop=True)
                last.then_inc(gram_done, 1)

            def decayed_keys(u):
                pe.wait_ge(kd_ready, u + 1)
                if u:
                    pe.wait_ge(st_ready, u)
                for i in range(4):
                    last = nc.tensor.transpose(bank(2)[:, i * P:(i + 1) * P], kdec[:, i * P:(i + 1) * P], ident)
                last.then_inc(kdt_done, 1)

            def state_updates(u):
                h, half = u // 2, u % 2
                pe.wait_ge(kdt_evac, u + 1)
                for cc in range(8):
                    i, r = cc // 2, (cc % 2) * CHUNK
                    last = M(bank(2 + cc % 2)[:, i * P:(i + 1) * P], lhsT=kdT[r:r + CHUNK, i * P:(i + 1) * P],
                             rhs=vtok[r:r + CHUNK, half * 4 + i, h * P:(h + 1) * P], start=True, stop=True)
                last.then_inc(u_done, 1)

            def head_product(u):
                h, half = u // 2, u % 2
                pe.wait_ge(st_ready, u + 1)
                pe.wait_ge(q_dec, u + 1)
                pe.wait_ge(gram_read, 7 * u + 7)
                if u:
                    pe.wait_ge(head_out, u)
                for i in range(4):
                    o = bank(6)[:, i * P:(i + 1) * P]
                    M(o, lhsT=vtok[:, half * 4 + i, h * P:(h + 1) * P], rhs=score[:, i * P:(i + 1) * P], start=True, stop=False,
                      skip_group_check=True)
                    for cc in (2 * i, 2 * i + 1):
                        last = M(bank(6)[:, cc * CHUNK:(cc + 1) * CHUNK], lhsT=state[:, cc, :], rhs=qdec[:, cc * CHUNK:(cc + 1) * CHUNK],
                                 start=False, stop=True, skip_group_check=True)
                last.then_inc(ho_done, 1)

            def mean_square(u):
                if u:
                    pe.wait_ge(rms_ready, u)
                pe.wait_ge(sq_ready, u + 1)
                M(bank(7), lhsT=mean[:], rhs=sq, start=True, stop=True).then_inc(ms_done, 1)

            arrived(pe, "hi")
            for i in range(NT):
                for step in range(2):
                    n = 2 * i + step
                    attn_scores(n)
                    if i:
                        attn_transpose(n - 2)
                    if step == 0 and i >= 2:
                        pe.wait_ge(v_evac, i - 1)
                    for k in range(4 * step, 4 * step + 4):
                        M(bank(i % 2), lhsT=hT[:, k, i * P:(i + 1) * P], rhs=view("hi")[:, k, :], start=(k == 0), stop=(k == KD - 1))
                    if step:
                        for k in range(KD):
                            last = M(bank(6 + i % 2)[:, 0:P], lhsT=hT[:, k, i * P:(i + 1) * P], rhs=view("kv", 256)[:, k, P:2 * P],
                                     start=(k == 0), stop=(k == KD - 1))
                        last.then_inc(v_done, 1)
                    if i:
                        attn_values(n - 2)
            for n in (14, 15):
                attn_transpose(n)
                attn_values(n)
            pe.wait_ge(v_evac, NT)
            pe.wait_ge(o_evac, 16)

            for name in ("hf", "hq", "hg"):
                arrived(pe, name)
            for period in range(UNITS + 1):
                u = period - 1
                for part3 in range(3):
                    z = Z0 + 3 * period + part3
                    if period < UNITS:
                        z_free(z)
                        st = view(("hf", "hq", "hg")[part3])[:, :, (period // 2) * P:(period // 2 + 1) * P]
                    for quarter in range(4):
                        if period < UNITS:
                            z_steps(z, st, period % 2, [2 * quarter, 2 * quarter + 1])
                        if u < 0:
                            continue
                        step = 4 * part3 + quarter
                        if step == 0 and u:
                            mean_square(u - 1)
                        elif step == 1:
                            gram(u, 0)
                        elif step in (3, 4):
                            gram(u, step - 2)
                        elif step == 5:
                            decayed_keys(u)
                        elif step == 6:
                            gram(u, 3)
                        elif step == 7:
                            state_updates(u)
                        elif step in (8, 9, 10):
                            gram(u, step - 4)
                        elif step == 11:
                            head_product(u)
            mean_square(UNITS - 1)

            pe.wait_ge(head_out, UNITS)
            pe.wait_ge(o_evac, 16)
            arrived(pe, "wo0")
            pe.wait_ge(piece_in[3], 16 * 8)
            wo = [slot(s).rearrange("p (m n) -> p m n", m=4) for s in (0, 3)]

            def transpose_norm(t):
                pe.wait_ge(n2_ready, t + 1)
                if t:
                    pe.wait_ge(t2_evac, t)
                transposes(rbuf[t % 2], bank(4, 2), KD, KD).then_inc(t2_done, 1)

            def route(t):
                pe.wait_ge(t2_evac, t + 1)
                pe.wait_ge(r_in, 16 * 7)
                if t >= 2:
                    pe.wait_ge(rt_read, t - 1)
                for k in range(KD):
                    last = M(bank(6 + t % 2)[:, 0:36], lhsT=h2T[t % 2][:, k * P:(k + 1) * P], rhs=wr[:, k, :],
                             start=(k == 0), stop=(k == KD - 1))
                last.then_inc(rt_done, 1)

            for t in range(NT):
                if t >= 2:
                    pe.wait_ge(mix_read, t - 1)
                for half in range(2):
                    for m in range(8):
                        last = M(bank(2 * (t % 2) + half), lhsT=mixT[:, m, t * P:(t + 1) * P],
                                 rhs=wo[m // 4][:, m % 4, half * HALF:(half + 1) * HALF], start=(m == 0), stop=(m == 7))
                    if half == 0 and t >= 2:
                        route(t - 2)
                last.then_inc(mix_done, 1)
                if t:
                    transpose_norm(t - 1)
            route(NT - 2)
            transpose_norm(NT - 1)
            route(NT - 1)
            pe.wait_ge(onehots, 1)
            M(bank(0)[:, 0:NT * NE], lhsT=tri, rhs=ohsum, start=True, stop=False)
            M(bank(0)[:, 0:NT * NE], lhsT=ones[:], rhs=before[:, 0:NT, :], start=False, stop=True)
            M(bank(1)[:, 0:NE], lhsT=ones[:], rhs=before[:, NT, :], start=True, stop=True).then_inc(ranked, 1)
            for n in range(2 * NT):
                pe.wait_ge(slots_ready, n + 1)
                last = M(bank(2)[0:BLK, 0:MAX_BLOCKS], lhsT=row_oh[:, n, :], rhs=blk_oh[:, n, :], start=(n == 0), stop=(n == 2 * NT - 1))
            last.then_inc(table_done, 1)

            pe.wait_ge(plan_ready, 1)
            blocks = pe.alloc_register("blocks")
            arrivals = pe.alloc_register("arrivals")
            gated = [pe.alloc_register(f"gated{half}") for half in range(2)]
            for counter in (blocks, *gated):
                pe.reg_mov(counter, 1)
            pe.reg_mov(arrivals, 32)

            def transpose_tokens():
                v = xg[0:BLK, :].rearrange("p (d k) -> p k d", k=KD)
                for k in range(KD):
                    last = nc.tensor.transpose(bank(0)[:, k * BLK:(k + 1) * BLK], v[:, k, :], ident[0:BLK, 0:BLK])
                last.then_inc(xg_t, 1)

            pe.wait_ge(xg_in, 16)
            transpose_tokens()
            def transpose_hidden(half):
                pe.wait_ge(hid_ready[half], gated[half])
                pe.reg_add(gated[half], gated[half], 1)
                for k in (2 * half, 2 * half + 1):
                    last = nc.tensor.transpose(bank(4 + half)[:, (k % 2) * BLK:(k % 2 + 1) * BLK],
                                               hid[BLK:P, k * P:(k + 1) * P], ident[BLK:P, BLK:P])
                last.then_inc(ht_done, 1)

            def expert(i, b):
                w1v, w3v = (s[b].rearrange("p (k f) -> p k f", k=KD) for s in (W1, W3))
                w2v = W2[b].rearrange("p (k f) -> p k f", k=4)
                own = pe.value_load(nblki[0:1, bass.ds(i * SETS + b, 1)], min_val=1, max_val=MAX_EXPERT)
                with pe.Fori(0, own):
                    pe.wait_ge(w1_in[b], i * 16 + 16)
                    pe.wait_ge(w3_in[b], i * 16 + 16)
                    pe.wait_ge(xT_evac, blocks)
                    for half in range(2):
                        if half:
                            pe.wait_ge(xg_in, arrivals)
                            pe.reg_add(arrivals, arrivals, 16)
                            transpose_tokens()
                        f = slice(half * 2 * P, (half + 1) * 2 * P)
                        for k in range(KD):
                            if half and k == KD // 2:
                                transpose_hidden(0)
                            x_k = xT[:, k * BLK:(k + 1) * BLK]
                            M(bank(2 + half)[0:BLK, 0:2 * P], lhsT=x_k, rhs=w1v[:, k, f], start=(k == 0), stop=(k == KD - 1))
                            last = M(bank(2 + half)[BLK:P, 0:2 * P], lhsT=x_k, rhs=w3v[:, k, f], start=(k == 0), stop=(k == KD - 1))
                        last.then_inc(gu_done[half], 1)
                    pe.wait_ge(w2_in[b], i * 16 + 16)
                    pe.wait_ge(y_scaled, blocks)
                    for k in range(4):
                        if k == 1:
                            transpose_hidden(1)
                        if k % 2 == 0:
                            pe.wait_ge(ht_evac[k // 2], blocks)
                        for half in range(2):
                            last = M(bank(6)[half * BLK:(half + 1) * BLK, :], lhsT=hidT[:, k * BLK:(k + 1) * BLK],
                                     rhs=w2v[:, k, half * HALF:(half + 1) * HALF], start=(k == 0), stop=(k == 3))
                    last.then_inc(y_done, 1)
                    pe.reg_add(blocks, blocks, 1)

            with pe.Fori(0, NE // SETS) as i:
                for b in range(SETS):
                    expert(i, b)
            for b in range(NE % SETS):
                expert(NE // SETS, b)

            for t in range(NT):
                pe.wait_ge(ys_in[t], 32)
                pe.wait_ge(diag_ready, t + 1)
                if t >= 2:
                    pe.wait_ge(sum_read, t - 1)
                for half in range(2):
                    f = slice(half * HALF, (half + 1) * HALF)
                    M(bank(2 + 2 * (t % 2) + half), lhsT=diag[t][:, 0:P], rhs=ya[t][:, f], start=True, stop=False)
                    last = M(bank(2 + 2 * (t % 2) + half), lhsT=diag[t][:, P:2 * P], rhs=yb[t][:, f], start=False, stop=True)
                last.then_inc(combined, 1)


def constants():
    i = np.arange(P)
    f = np.zeros((P, 2 * P + MAX_BLOCKS + MAX_EXPERT + NT), np.float32)
    f[:, :P] = np.eye(P)
    f[:, P:2 * P] = i[:, None] < i[None, :]
    f[:, 2 * P:2 * P + MAX_BLOCKS] = np.arange(MAX_BLOCKS)
    f[:, 2 * P + MAX_BLOCKS:2 * P + MAX_BLOCKS + MAX_EXPERT] = np.arange(MAX_EXPERT) * BLK
    f[:, 2 * P + MAX_BLOCKS + MAX_EXPERT:] = np.arange(NT)[None, :] * P + i[:, None]
    m = np.zeros((P, 7, P), np.int32)
    for n, w in enumerate(LEVELS):
        m[:, n + 1] = ((i[:, None] // (2 * w) == i[None, :] // (2 * w)) & (i[:, None] % (2 * w) < w)
                       & (i[None, :] % (2 * w) >= w))
    n = BAND - 1 - np.arange(DIFFS)
    side = (n < 0).astype(np.int32) * 16
    n = np.abs(n)
    far = np.minimum(8 + (np.log(np.maximum(n, 1) / 8) / np.log(128 / 8) * 8).astype(np.int32), 15)
    bucket = side + np.where(n < 8, n, far)
    onehot = (np.arange(32)[:, None] == bucket[None, :]).astype(np.float32)
    return f, m.reshape(P, 7 * P), onehot


def kernel(**inputs):
    import concourse.bacc as bacc
    from concourse.bass_utils import run_bass_kernel_spmd

    b_in = np.asarray(inputs["b_in"])
    tiles = b_in[0].reshape(22, P)
    heads = tiles[16:20].reshape(KVH, GRP, DH).transpose(1, 0, 2).reshape(GRP, P)
    low = np.asarray(inputs["hg_lower"])
    w_in = np.asarray(inputs["w_in"])
    order = np.arange(w_in.shape[2])
    order[2048:2560] = order[2048:2560].reshape(KVH, GRP, DH).transpose(1, 0, 2).reshape(-1)
    given = {k: np.ascontiguousarray(inputs[k]) for k in ("x", "c")}
    given["w_in"] = np.ascontiguousarray(w_in[:, :, order])
    given["b_in_row"] = np.ascontiguousarray(np.concatenate([b_in[:, 1024:1536], b_in[:, 2688:2816]], axis=1))
    given["b_in_cols"] = np.ascontiguousarray(np.concatenate([tiles[:16], heads, tiles[20:]]).T)
    given["w_out"] = np.ascontiguousarray(inputs["w_out"])
    given["hg_lower_cols"] = np.ascontiguousarray(low.reshape(2, HEADS, P).transpose(2, 0, 1).reshape(P, 2 * HEADS))
    for k in ("hg_norm", "attn_sinks", "rel_bias", "ada_w", "ada_b", "ln1_g", "ln1_b", "ln2_g", "ln2_b", "w_group",
              "b_group", "w_sub", "b_sub", "w1", "w3", "w2"):
        given[k] = np.ascontiguousarray(inputs[k])
    given["c_f32"], given["c_masks"], given["c_onehot"] = constants()

    nc = bacc.Bacc("TRN2", target_bir_lowering=False, num_devices=1)
    arrays, args = {}, []
    for name, a in given.items():
        arrays[f"in_{name}"] = a
        args.append(nc.dram_tensor(f"in_{name}", a.shape, mybir.dt.from_np(a.dtype), kind="ExternalInput").ap())
    args.append(nc.dram_tensor("out_0", OUTS[0][0], mybir.dt.float32, kind="ExternalOutput").ap())
    block_kernel(nc, *args)
    r = run_bass_kernel_spmd(nc, [arrays], core_ids=[0])
    return r.results[0]["out_0"]
```
